# Optimizing a Trainium2 kernel written in Bass

```python
import math
import jax
import jax.numpy as jnp
from jax import lax
import numpy as np

D_MODEL = 1024
BATCH = 1
SEQ = 2048
DEPTH = 1

SB_HEADS = 8
SB_HEAD_DIM = 64
SB_WIDTH = SB_HEADS * SB_HEAD_DIM
SB_BLOCK = 128
HG_HEADS = 4
HG_HEAD_DIM = 128
HG_WIDTH = HG_HEADS * HG_HEAD_DIM
HG_CHUNK = 64
CONV_WIDTH = 512
CONV_K = 3
N_BRANCH = 3
IN_COLS = 4 * SB_WIDTH + 4 * HG_WIDTH + 4 * CONV_WIDTH + N_BRANCH * D_MODEL
LN_EPS = 1e-5
RMS_EPS = 1e-6

kernel_name = "hybrid_sb_hgrn2_shortconv_deepnorm"

def _standardize(x):
    xf = x.astype(jnp.float32)
    mu = jnp.mean(xf, axis=-1, keepdims=True)
    xc = xf - mu
    var = jnp.mean(xc * xc, axis=-1, keepdims=True)
    return xc * lax.rsqrt(var + LN_EPS)

def _stick_breaking(q, k, v):
    B, S, H, dh = q.shape
    scale = dh ** -0.5
    qf = q.astype(jnp.float32)
    kf = k.astype(jnp.float32)
    vf = v.astype(jnp.float32)
    outs = []
    for blk in range(S // SB_BLOCK):
        t0 = blk * SB_BLOCK
        t1 = t0 + SB_BLOCK
        z = jnp.einsum('bthd,bshd->bhts', qf[:, t0:t1], kf[:, :t1]) * scale
        mask = jnp.arange(t1)[None, :] < (t0 + jnp.arange(SB_BLOCK))[:, None]
        log_1m_beta = jnp.where(mask, -jax.nn.softplus(z), 0.0)
        log_surv = lax.cumsum(log_1m_beta, axis=3, reverse=True) - log_1m_beta
        a = jnp.where(mask, jnp.exp(jax.nn.log_sigmoid(z) + log_surv), 0.0)
        outs.append(jnp.einsum('bhts,bshd->bthd', a, vf[:, :t1]))
    return jnp.concatenate(outs, axis=1)

def _hgrn2(q, f_pre, i_in, lb):
    B, S, H, dk = q.shape
    dv = i_in.shape[-1]
    n_chunks = S // HG_CHUNK
    f = lb + (1.0 - lb) * jax.nn.sigmoid(f_pre.astype(jnp.float32))
    k = 1.0 - f
    g = jnp.log(f)

    def to_chunks(a):
        return a.reshape(B, n_chunks, HG_CHUNK, H, a.shape[-1]).transpose(1, 0, 3, 2, 4)

    qc = to_chunks(q.astype(jnp.float32))
    kc = to_chunks(k)
    vc = to_chunks(i_in.astype(jnp.float32))
    bc = jnp.cumsum(to_chunks(g), axis=3)
    causal = jnp.tril(jnp.ones((HG_CHUNK, HG_CHUNK), dtype=bool))

    def step(state, inp):
        q_c, k_c, v_c, b_c = inp
        inter = jnp.einsum('bhtd,bhde->bhte', q_c * jnp.exp(b_c), state)
        diff = b_c[:, :, :, None, :] - b_c[:, :, None, :, :]
        decay = jnp.exp(jnp.where(causal[:, :, None], diff, -jnp.inf))
        scores = jnp.einsum('bhtsd,bhsd->bhts', q_c[:, :, :, None, :] * decay, k_c)
        intra = jnp.einsum('bhts,bhse->bhte', scores, v_c)
        b_end = b_c[:, :, -1, :]
        k_dec = k_c * jnp.exp(b_end[:, :, None, :] - b_c)
        new_state = jnp.exp(b_end)[..., None] * state + jnp.einsum('bhsd,bhse->bhde', k_dec, v_c)
        return new_state, inter + intra

    state0 = jnp.zeros((B, H, dk, dv), jnp.float32)
    _, o = lax.scan(step, state0, (qc, kc, vc, bc))
    return o.transpose(1, 0, 3, 2, 4).reshape(B, S, H, dv)

def _short_conv(u, w):
    ch = u.shape[-1]
    return lax.conv_general_dilated(
        u, w[:, None, :].astype(u.dtype), window_strides=(1,), padding=[(CONV_K - 1, 0)],
        dimension_numbers=('NWC', 'WIO', 'NWC'), feature_group_count=ch)

def setup_inputs(seed: int = 0) -> dict:
    key = jax.random.key(seed)
    ks = jax.random.split(key, 12)
    beta = (8.0 * DEPTH) ** -0.25

    def nrm(k, shape, scale):
        return jax.random.normal(k, shape, jnp.float32) * scale

    return {
        "x": nrm(ks[0], (BATCH, SEQ, D_MODEL), 1.0),
        "c": nrm(ks[1], (BATCH, D_MODEL), 1.0),
        "w_mod": nrm(ks[2], (DEPTH, D_MODEL, 3 * D_MODEL), 0.2 * D_MODEL ** -0.5),
        "b_mod": nrm(ks[3], (DEPTH, 3 * D_MODEL), 0.01),
        "w_in": nrm(ks[4], (DEPTH, D_MODEL, IN_COLS), D_MODEL ** -0.5),
        "conv_w": nrm(ks[5], (DEPTH, CONV_K, CONV_WIDTH), CONV_K ** -0.5),
        "hgrn_norm_w": 1.0 + nrm(ks[6], (DEPTH, HG_HEAD_DIM), 0.02),
        "lower_bounds": nrm(ks[7], (DEPTH, HG_WIDTH), 0.1),
        "w_branch": nrm(ks[8], (DEPTH, N_BRANCH, SB_WIDTH, D_MODEL), beta * SB_WIDTH ** -0.5),
        "w_out": nrm(ks[9], (DEPTH, D_MODEL, D_MODEL), beta * D_MODEL ** -0.5),
        "ln_g": 1.0 + nrm(ks[10], (DEPTH, D_MODEL), 0.02),
        "ln_b": nrm(ks[11], (DEPTH, D_MODEL), 0.02),
    }

def reference(x, c, w_mod, b_mod, w_in, conv_w, hgrn_norm_w, lower_bounds, w_branch, w_out, ln_g, ln_b):
    B, S, D = x.shape
    dt = x.dtype
    alpha = (2.0 * DEPTH) ** 0.25
    p = jax.nn.softmax(lower_bounds.astype(jnp.float32), axis=0)
    lbs = jnp.cumsum(p, axis=0) - p[0:1]
    sizes = [SB_WIDTH] * 4 + [HG_WIDTH] * 4 + [CONV_WIDTH] * 4 + [D_MODEL] * N_BRANCH
    splits = np.cumsum(sizes[:-1]).tolist()

    for l in range(DEPTH):
        mod = (c @ w_mod[l] + b_mod[l])[:, None, :]
        shift, scale, gate = jnp.split(mod.astype(jnp.float32), 3, axis=-1)
        h = (_standardize(x) * (1.0 + scale) + shift).astype(dt)

        proj = h @ w_in[l]
        (q_a, k_a, v_a, z_a, q_b, f_b, i_b, z_b,
         pre_c, post_c, u_c, z_c, g_a, g_b, g_c) = jnp.split(proj, splits, axis=-1)

        o_a = _stick_breaking(q_a.reshape(B, S, SB_HEADS, SB_HEAD_DIM),
                              k_a.reshape(B, S, SB_HEADS, SB_HEAD_DIM),
                              v_a.reshape(B, S, SB_HEADS, SB_HEAD_DIM)).reshape(B, S, SB_WIDTH)
        y_a = (o_a * jax.nn.silu(z_a.astype(jnp.float32))).astype(dt)

        o_b = _hgrn2(jax.nn.silu(q_b).reshape(B, S, HG_HEADS, HG_HEAD_DIM),
                     f_b.reshape(B, S, HG_HEADS, HG_HEAD_DIM),
                     i_b.reshape(B, S, HG_HEADS, HG_HEAD_DIM),
                     lbs[l].reshape(HG_HEADS, HG_HEAD_DIM))
        o_b = o_b * lax.rsqrt(jnp.mean(o_b * o_b, axis=-1, keepdims=True) + RMS_EPS)
        o_b = (o_b * hgrn_norm_w[l].astype(jnp.float32)).reshape(B, S, HG_WIDTH)
        y_b = (o_b * jax.nn.silu(z_b.astype(jnp.float32))).astype(dt)

        y_c = post_c * _short_conv(pre_c * u_c, conv_w[l]) * jax.nn.silu(z_c)

        merged = (jax.nn.sigmoid(g_a) * (y_a @ w_branch[l, 0])
                  + jax.nn.sigmoid(g_b) * (y_b @ w_branch[l, 1])
                  + jax.nn.sigmoid(g_c) * (y_c.astype(dt) @ w_branch[l, 2]))
        y = (merged @ w_out[l]).astype(jnp.float32)

        r = alpha * x.astype(jnp.float32) + (1.0 + gate) * y
        x = (_standardize(r) * ln_g[l] + ln_b[l]).astype(dt)
    return x


_drawn_inputs = setup_inputs


def setup_inputs(seed=0):
    import zlib

    import numpy as np

    out = dict(_drawn_inputs(seed))
    spreads = {}
    factors = {'b_mod': 8.0, 'hgrn_norm_w': 8.0, 'ln_g': 2.922, 'ln_b': 2.83}
    for name, (base, spread) in spreads.items():
        noise = np.random.default_rng([zlib.crc32(name.encode()), seed]).standard_normal(out[name].shape)
        drawn = base * np.exp(spread * noise) if base else spread * noise
        out[name] = jnp.asarray(drawn.astype(out[name].dtype))
    for name, factor in factors.items():
        out[name] = (out[name] * factor).astype(out[name].dtype)
    return out
```

```python
from contextlib import ExitStack

import concourse.bass as bass
from concourse import mybir

F32 = mybir.dt.float32
F32R = mybir.dt.float32r
ACT = mybir.ActivationFunctionType
ALU = mybir.AluOpType
AX = mybir.AxisListType

P = 128
T = 2048
D = 1024
KD = D // P
TC = 512
NTC = T // TC
W = 512
WB = W // P
IN_COLS = 12 * W + 3 * D
NCB = IN_COLS // P
HEADS, DH = 8, 64
ALPHA = 2.0 ** 0.25
LN_EPS = 1e-5
RMS_EPS = 1e-6
SCALE = DH ** -0.5

QA, KA, VA, ZA, QB, FB, IB, ZB, PRE, POST, UC, ZC, GA = (WB * n for n in range(13))

RUNS_1 = [(QA, 8, "Copy", "split"), (ZA, 8, "Sigmoid", "gate"), (FB, 4, "Sigmoid", None),
          (ZB, 4, "Sigmoid", "gate")]
FUNCS = {"Copy": ACT.Copy, "Sigmoid": ACT.Sigmoid}
RUNS_2 = [(PRE, 12, "Copy", None), (ZC, 4, "Sigmoid", "gate"), (GA, 24, "Sigmoid", None)]


def after(eng, sem, value):
    if isinstance(value, int) and value <= 0:
        return
    eng.wait_ge(sem, value)


def modulated_input(nc, sem, g, x, c, w_mod, b_mod, scr):
    with ExitStack() as ctx:
        sb = lambda n, s, d=F32: ctx.enter_context(nc.sbuf_tensor(n, s, d))
        MC = 256
        NM = 3 * D // MC
        c_col = sb("c_col", [P, KD])
        c_rep = sb("c_rep", [P, KD, P])
        mod = sb("mod", [P, 3 * D])
        wm = [sb(f"wm{i}", [P, KD, MC]) for i in range(2)]
        xt = [sb(f"xt{i}", [P, D]) for i in range(4)]
        hm = [sb(f"hm{i}", [P, D]) for i in range(2)]
        stats = sb("stats", [P, 4, 12])
        count = sb("count", [P, 1])
        mv = sb("mv", [P, 4, 2])
        ve = sb("ve", [P, 4])
        std = sb("std", [P, 4])
        rstd = sb("rstd", [P, 4])
        ps_mod = [ctx.enter_context(nc.psum_tensor(f"ps_mod{i}", [P, MC], F32)) for i in range(2)]
        ps_t = [ctx.enter_context(nc.psum_tensor(f"ps_t{i}", [P, 4, P], F32)) for i in range(4)]
        c_loaded, b_loaded, c_spread = sem("c_loaded"), sem("b_loaded"), sem("c_spread")
        wm_loaded = [sem(f"wm_loaded{i}") for i in range(2)]
        mod_summed, mod_ready, gate_stored = sem("mod_summed"), sem("mod_ready"), sem("gate_stored")
        x_loaded = [sem(f"x_loaded{i}") for i in range(4)]
        stats_done, mv_done, ve_done, std_done = sem("stats_done"), sem("mv_done"), sem("ve_done"), sem("std_done")
        rstd_done, xhat_done, scaled_done, hm_done = sem("rstd_done"), sem("xhat_done"), sem("scaled_done"), sem("hm_done")
        turned, hi_done, lo_done = sem("turned"), sem("hi_done"), sem("lo_done")
        ident_zero = sem("ident_zero")
        ident_ready = sem("ident_ready")
        ident, hT_hi, hT_lo = g["ident"], g["hT_hi"], g["hT_lo"]
        block = ctx.enter_context(nc.Block())

        def load_x(eng, i, u):
            after(eng, xhat_done, 4 * i + u - 3)
            eng.dma_start(xt[u][:], x[bass.ts(4 * i + u, P), :]).then_inc(x_loaded[u], 16)

        @block.sync
        def _(sp):
            with nc.allow_non_contiguous_dma(reason="1024 values of c"):
                sp.dma_start(c_col[:], c.rearrange("a (k p) -> p (a k)", p=P)).then_inc(c_loaded, 16)
            sp.dma_start(mod[:], b_mod[0].partition_broadcast(P)).then_inc(b_loaded, 16)
            for m in range(NM):
                if m >= 2:
                    sp.wait_ge(mod_summed, m - 1)
                sp.dma_start(wm[m % 2][:], w_mod[0, :, m * MC:(m + 1) * MC].rearrange("(k p) n -> p k n", p=P)
                             ).then_inc(wm_loaded[m % 2], 16)
                if m == 1:
                    for u in range(4):
                        load_x(sp, 0, u)
            with sp.Fori(1, 4) as i:
                for u in range(4):
                    load_x(sp, i, u)
            sp.wait_ge(mod_ready, NM)
            sp.dma_start(scr["gate"], mod[0:1, 2 * D:3 * D]).then_inc(gate_stored, 16)
            sp.wait_ge(gate_stored, 16)

        @block.gpsimd
        def _(pool):
            nc.gpsimd.memset(ident[:], 0.0).then_inc(ident_zero, 1)
            pool.wait_ge(ident_zero, 1)
            nc.gpsimd.affine_select(out=ident[:], in_=ident[:], compare_op=ALU.not_equal, fill=1.0, base=0,
                                    pattern=[[-1, P]], channel_multiplier=1).then_inc(ident_ready, 1)
            pool.wait_ge(mod_ready, NM)
            with pool.Fori(0, 8) as i:
                for u in range(2):
                    pool.wait_ge(scaled_done, 2 * i + u + 1)
                    nc.gpsimd.tensor_tensor(hm[u][:], hm[u][:], mod[:, 0:D], ALU.add).then_inc(hm_done, 1)

        @block.tensor
        def _(pe):
            pe.wait_ge(c_spread, 1)
            for m in range(NM):
                pe.wait_ge(wm_loaded[m % 2], 16 * (m // 2 + 1))
                if m >= 2:
                    pe.wait_ge(mod_ready, m - 1)
                for k in range(KD):
                    mm = nc.tensor.matmul(ps_mod[m % 2][:], c_rep[:, k, :], wm[m % 2][:, k, :],
                                          start=k == 0, stop=k == KD - 1)
                mm.then_inc(mod_summed, 1)
            pe.wait_ge(ident_ready, 1)
            with pe.Fori(0, 8) as i:
                for u in range(2):
                    pe.wait_ge(hm_done, 2 * i + u + 1)
                    pe.wait_ge(lo_done, 4 * i + 2 * u + 2)
                    for half in range(2):
                        for k in range(4):
                            mm = nc.tensor.transpose(ps_t[2 * u + half][:, k, :],
                                                     hm[u][:, (4 * half + k) * P:(4 * half + k + 1) * P], ident[:])
                        mm.then_inc(turned, 1)

        @block.scalar
        def _(act):
            def root(i, u):
                act.wait_ge(ve_done, 4 * i + u + 1)
                nc.scalar.activation(std[:, u:u + 1], ve[:, u:u + 1], ACT.Sqrt).then_inc(std_done, 1)

            def high(t4, u):
                for half in range(2):
                    act.wait_ge(turned, 8 * t4 + 2 * u + half + 1)
                    nc.scalar.activation(hT_hi[:, 4 * half:4 * half + 4, bass.ds((4 * t4 + u) * P, P)],
                                         ps_t[2 * (u % 2) + half][:], ACT.Copy).then_inc(hi_done, 1)

            root(0, 0)
            with act.Fori(0, 3) as i:
                for u in range(4):
                    if u < 3:
                        root(i, u + 1)
                    else:
                        root(i + 1, 0)
                    high(i, u)
            for u in range(4):
                if u < 3:
                    root(3, u + 1)
                high(3, u)

        @block.vector
        def _(dve):
            nc.vector.sem_inc(lo_done, 4)

            def statistics(i, u):
                dve.wait_ge(x_loaded[u], 16 * (i + 1))
                for half in range(2):
                    nc.vector.bn_stats(stats[:, u, 6 * half:6 * half + 6], xt[u][:, 512 * half:512 * half + 512]
                                       ).then_inc(stats_done, 1)
                dve.wait_ge(stats_done, 8 * i + 2 * u + 2)
                nc.vector.tensor_copy(count[:], stats[:, u, 0:1])
                nc.vector.bn_aggr(mv[:, u, :], stats[:, u, :]).then_inc(mv_done, 1)
                dve.wait_ge(mv_done, 4 * i + u + 1)
                nc.vector.tensor_scalar(ve[:, u:u + 1], mv[:, u, 1:2], LN_EPS, None, ALU.add).then_inc(ve_done, 1)

            def normalise(i, u):
                n = 4 * i + u
                dve.wait_ge(std_done, n + 1)
                nc.vector.reciprocal(rstd[:, u:u + 1], std[:, u:u + 1]).then_inc(rstd_done, 1)
                dve.wait_ge(rstd_done, n + 1)
                after(dve, turned, 8 * i + 2 * u - 2)
                nc.vector.tensor_scalar(hm[u % 2][:], xt[u][:], mv[:, u, 0:1], rstd[:, u:u + 1],
                                        ALU.subtract, ALU.mult).then_inc(xhat_done, 1)
                dve.wait_ge(xhat_done, n + 1)
                nc.vector.tensor_tensor(hm[u % 2][:], hm[u % 2][:], mod[:, D:2 * D], ALU.mult).then_inc(scaled_done, 1)

            def low(i, u):
                for half in range(2):
                    dve.wait_ge(hi_done, 8 * i + 2 * u + half + 1)
                    at = bass.ds((4 * i + u) * P, P)
                    nc.vector.tensor_tensor(hT_lo[:, 4 * half:4 * half + 4, at], ps_t[2 * (u % 2) + half][:],
                                            hT_hi[:, 4 * half:4 * half + 4, at].bitcast(F32),
                                            ALU.subtract).then_inc(lo_done, 1)

            dve.wait_ge(c_loaded, 16)
            nc.vector.tensor_copy(c_rep[:], c_col[:].unsqueeze(2).to_broadcast([P, KD, P])).then_inc(c_spread, 1)
            dve.wait_ge(b_loaded, 16)
            for m in range(NM):
                dve.wait_ge(mod_summed, m + 1)
                cols = mod[:, m * MC:(m + 1) * MC]
                nc.vector.scalar_tensor_tensor(cols, ps_mod[m % 2][:], 0.0 if m * MC < D else 1.0, cols,
                                               ALU.add, ALU.add).then_inc(mod_ready, 1)
                if m == 5:
                    statistics(0, 0)
            dve.wait_ge(mod_ready, NM)

            def steps(i, first=False, last=False):
                for u in range(4):
                    if u < 3:
                        statistics(i, u + 1)
                    elif not last:
                        statistics(i + 1, 0)
                    normalise(i, u)
                    if u > 0:
                        low(i, u - 1)
                    elif not first:
                        low(i - 1, 3)

            steps(0, first=True)
            with dve.Fori(1, 3) as i:
                steps(i)
            steps(3, last=True)
            low(3, 3)


def token_major_values(nc, sem, g, w_in, scr):
    with ExitStack() as ctx:
        sb = lambda n, s, d=F32: ctx.enter_context(nc.sbuf_tensor(n, s, d))
        NC_ = 256
        UNITS = [(VA * P, 0, True), (VA * P + NC_, NC_, True), (IB * P, 0, False), (IB * P + NC_, NC_, False)]
        NT = T // P
        w_raw = [sb(f"vw_raw{i}", [P, KD, NC_]) for i in range(2)]
        w_hi = [sb(f"vw_hi{i}", [P, KD, NC_], F32R) for i in range(2)]
        w_lo = [sb(f"vw_lo{i}", [P, KD, NC_], F32R) for i in range(2)]
        v_hi = [sb(f"v_hi{i}", [P, NC_], F32R) for i in range(2)]
        v_lo = [sb(f"v_lo{i}", [P, NC_], F32R) for i in range(2)]
        i_out = [sb(f"i_out{i}", [P, NC_]) for i in range(2)]
        acc = [ctx.enter_context(nc.psum_tensor(f"v_acc{i}", [P, NC_], F32)) for i in range(2)]
        w_loaded = [sem(f"vw_loaded{i}") for i in range(2)]
        w_hi_done, w_lo_done, unit_done = sem("vw_hi_done"), sem("vw_lo_done"), sem("v_unit_done")
        acc_done, hi_done, lo_done, i_done = sem("v_acc_done"), sem("v_hi_done"), sem("v_lo_done"), sem("i_done")
        hi_stored = [sem(f"v_hi_stored{i}") for i in range(2)]
        lo_stored = [sem(f"v_lo_stored{i}") for i in range(2)]
        i_stored = [sem(f"i_stored{i}") for i in range(2)]
        hT_hi, hT_lo = g["hT_hi"], g["hT_lo"]
        block = ctx.enter_context(nc.Block())

        @block.sync
        def _(sp):
            def load(n):
                after(sp, w_lo_done, 8 * (n - 1))
                c0 = UNITS[n][0]
                sp.dma_start(w_raw[n % 2][:], w_in[0, :, c0:c0 + NC_].rearrange("(k p) n -> p k n", p=P)
                             ).then_inc(w_loaded[n % 2], 16)

            load(0)
            load(1)
            for n, (_, col, split) in enumerate(UNITS):
                for t in range(NT):
                    m = NT * n + t
                    rows = slice(t * P, (t + 1) * P)
                    if split:
                        sp.wait_ge(lo_done, m + 1)
                        sp.dma_start(scr["v_hi"][rows, col:col + NC_], v_hi[m % 2][:].bitcast(F32)
                                     ).then_inc(hi_stored[m % 2], 16)
                        sp.dma_start(scr["v_lo"][rows, col:col + NC_], v_lo[m % 2][:].bitcast(F32)
                                     ).then_inc(lo_stored[m % 2], 16)
                    else:
                        sp.wait_ge(i_done, m - 2 * NT + 1)
                        sp.dma_start(scr["i"][rows, col:col + NC_], i_out[m % 2][:]).then_inc(i_stored[m % 2], 16)
                if n + 2 < len(UNITS):
                    load(n + 2)
            for u in range(2):
                sp.wait_ge(hi_stored[u], 16 * NT)
                sp.wait_ge(lo_stored[u], 16 * NT)
                sp.wait_ge(i_stored[u], 16 * NT)

        @block.tensor
        def _(pe):
            for n, (_, _, split) in enumerate(UNITS):
                for t in range(NT):
                    m = NT * n + t
                    if m - 2 < 2 * NT:
                        after(pe, lo_done, m - 1)
                    else:
                        pe.wait_ge(i_done, m - 1 - 2 * NT)
                    tok = slice(t * P, (t + 1) * P)
                    for k in range(KD):
                        if t == 0:
                            pe.wait_ge(w_lo_done, KD * n + k + 1)
                        nc.tensor.matmul(acc[m % 2][:], hT_hi[:, k, tok], w_hi[n % 2][:, k, :], start=k == 0, stop=False)
                        nc.tensor.matmul(acc[m % 2][:], hT_hi[:, k, tok], w_lo[n % 2][:, k, :], start=False, stop=False)
                        mm = nc.tensor.matmul(acc[m % 2][:], hT_lo[:, k, tok], w_hi[n % 2][:, k, :],
                                              start=False, stop=k == KD - 1)
                    mm.then_inc(acc_done, 1)

        @block.scalar
        def _(act):
            def split_weights(n):
                act.wait_ge(w_loaded[n % 2], 16 * (n // 2 + 1))
                after(act, acc_done, NT * (n - 1))
                for k in range(KD):
                    nc.scalar.activation(w_hi[n % 2][:, k, :], w_raw[n % 2][:, k, :], ACT.Copy).then_inc(w_hi_done, 1)

            split_weights(0)
            for n, (_, _, split) in enumerate(UNITS):
                for t in range(NT):
                    m = NT * n + t
                    if t == 2 and n + 1 < len(UNITS):
                        split_weights(n + 1)
                    act.wait_ge(acc_done, m + 1)
                    if split:
                        after(act, hi_stored[m % 2], 16 * (m // 2))
                        nc.scalar.activation(v_hi[m % 2][:], acc[m % 2][:], ACT.Copy).then_inc(hi_done, 1)
                    else:
                        after(act, i_stored[m % 2], 16 * ((m - 2 * NT) // 2))
                        nc.scalar.activation(i_out[m % 2][:], acc[m % 2][:], ACT.Copy).then_inc(i_done, 1)

        @block.vector
        def _(dve):
            def split_weights(n):
                for k in range(KD):
                    dve.wait_ge(w_hi_done, KD * n + k + 1)
                    nc.vector.tensor_tensor(w_lo[n % 2][:, k, :], w_raw[n % 2][:, k, :],
                                            w_hi[n % 2][:, k, :].bitcast(F32), ALU.subtract).then_inc(w_lo_done, 1)

            split_weights(0)
            for n, (_, _, split) in enumerate(UNITS):
                for t in range(NT):
                    m = NT * n + t
                    if t == 2 and n + 1 < len(UNITS):
                        split_weights(n + 1)
                    if split:
                        dve.wait_ge(hi_done, m + 1)
                        after(dve, lo_stored[m % 2], 16 * (m // 2))
                        nc.vector.tensor_tensor(v_lo[m % 2][:], acc[m % 2][:], v_hi[m % 2][:].bitcast(F32),
                                                ALU.subtract).then_inc(lo_done, 1)


def project(nc, sem, g, w_in, scr, runs, tag):
    with ExitStack() as ctx:
        sb = lambda n, s, d=F32: ctx.enter_context(nc.sbuf_tensor(tag + n, s, d))
        s_ = lambda n: sem(tag + n)
        w_raw = sb("w_raw", [P, KD, P])
        w_hi = [sb(f"w_hi{i}", [P, KD, P], F32R) for i in range(2)]
        w_lo = [sb(f"w_lo{i}", [P, KD, P], F32R) for i in range(2)]
        out = [sb(f"out{i}", [P, TC]) for i in range(2)]
        split_hi = [sb(f"split_hi{i}", [P, TC], F32R) for i in range(2)]
        split_lo = [sb(f"split_lo{i}", [P, TC], F32R) for i in range(2)]
        acc = [ctx.enter_context(nc.psum_tensor(f"{tag}acc{i}", [P, TC], F32)) for i in range(2)]
        w_loaded, w_hi_done, w_lo_done, acc_done = s_("w_loaded"), s_("w_hi_done"), s_("w_lo_done"), s_("acc_done")
        act_out, dve_in, dve_out = s_("act_out"), s_("dve_in"), s_("dve_out")
        stored = [s_(f"stored{i}") for i in range(2)]
        stored_lo = [s_(f"stored_lo{i}") for i in range(2)]
        hT_hi, hT_lo = g["hT_hi"], g["hT_lo"]
        block = ctx.enter_context(nc.Block())

        plan, n0, a0, v0 = [], 0, 0, 0
        for cb, blocks, func, then in runs:
            plan.append((cb, blocks, func, then, n0, a0, v0))
            n0 += blocks
            if then is None:
                a0 += NTC * blocks
            else:
                v0 += NTC * blocks
        TOTAL = n0

        def each_run(eng, body):
            for r, run in enumerate(plan):
                with eng.Fori(0, run[1] // 2) as i:
                    body(run, i)

        @block.sync
        def _(sp):
            def load(cb, n):
                sp.wait_ge(w_lo_done, n)
                sp.dma_start(w_raw[:], w_in[0, :, bass.ds(cb * P, P)].rearrange("(k p) n -> p k n", p=P)
                             ).then_inc(w_loaded, 16)

            load(plan[0][0], 0)
            for r, (cb, blocks, func, then, n0, a0, v0) in enumerate(plan):
                def stores(i, u):
                    for tc in range(NTC):
                        q = 2 * NTC * i + NTC * u + tc
                        s = tc % 2
                        if then is None:
                            sp.wait_ge(act_out, a0 + q + 1)
                        else:
                            sp.wait_ge(dve_out, v0 + q + 1)
                        rows = scr["proj"][bass.ds((cb + 2 * i + u) * P, P), tc * TC:(tc + 1) * TC]
                        if then == "split":
                            sp.dma_start(rows, split_hi[s][:].bitcast(F32)).then_inc(stored[s], 16)
                            sp.dma_start(scr["proj_lo"][bass.ds((cb + 2 * i + u) * P, P), tc * TC:(tc + 1) * TC],
                                         split_lo[s][:].bitcast(F32)).then_inc(stored_lo[s], 16)
                        else:
                            sp.dma_start(rows, out[s][:]).then_inc(stored[s], 16)

                def pair(i, more):
                    load(cb + 2 * i + 1, n0 + 2 * i + 1)
                    stores(i, 0)
                    if more == "same":
                        load(cb + 2 * i + 2, n0 + 2 * i + 2)
                    elif more is not None:
                        load(more, n0 + 2 * i + 2)
                    stores(i, 1)

                if blocks > 2:
                    with sp.Fori(0, blocks // 2 - 1) as i:
                        pair(i, "same")
                pair(blocks // 2 - 1, plan[r + 1][0] if r + 1 < len(plan) else None)
            n_lo = sum(b for _, b, _, then in runs if then == "split")
            for s in range(2):
                sp.wait_ge(stored[s], 16 * TOTAL * NTC // 2)
                if n_lo:
                    sp.wait_ge(stored_lo[s], 16 * n_lo * NTC // 2)

        @block.tensor
        def _(pe):
            free = {None: act_out, "gate": dve_out, "split": dve_out}
            for r, (cb, blocks, func, then, n0, a0, v0) in enumerate(plan):
                if r:
                    pe.wait_ge(free[plan[r - 1][3]], a0 if plan[r - 1][3] is None else v0)
                base = a0 if then is None else v0

                def blocks2(i, peeled=False):
                    for u in range(2):
                        pe.wait_ge(w_lo_done, n0 + 2 * i + u + 1)
                        for tc in range(NTC):
                            q = 2 * NTC * i + NTC * u + tc
                            if not (peeled and u == 0 and tc < 2):
                                pe.wait_ge(free[then], base + q - 1)
                            tok = slice(tc * TC, (tc + 1) * TC)
                            for k in range(KD):
                                nc.tensor.matmul(acc[tc % 2][:], w_hi[u][:, k, :], hT_hi[:, k, tok], start=k == 0, stop=False)
                                nc.tensor.matmul(acc[tc % 2][:], w_hi[u][:, k, :], hT_lo[:, k, tok], start=False, stop=False)
                                mm = nc.tensor.matmul(acc[tc % 2][:], w_lo[u][:, k, :], hT_hi[:, k, tok],
                                                      start=False, stop=k == KD - 1)
                            mm.then_inc(acc_done, 1)

                blocks2(0, peeled=True)
                if blocks > 2:
                    with pe.Fori(1, blocks // 2) as i:
                        blocks2(i)

        @block.gpsimd
        def _(pool):
            with pool.Fori(0, TOTAL // 2) as i:
                for u in range(2):
                    pool.wait_ge(w_hi_done, 2 * i + u + 1)
                    nc.gpsimd.tensor_tensor(w_lo[u][:], w_raw[:], w_hi[u][:].bitcast(F32), ALU.subtract
                                            ).then_inc(w_lo_done, 1)

        @block.scalar
        def _(act):
            def split_weights(n, u):
                act.wait_ge(w_loaded, 16 * (n + 1))
                after(act, acc_done, NTC * (n - 1))
                nc.scalar.activation(w_hi[u][:], w_raw[:], ACT.Copy).then_inc(w_hi_done, 1)

            split_weights(0, 0)
            split_weights(1, 1)
            for r, (cb, blocks, func, then, n0, a0, v0) in enumerate(plan):
                def pair(i, more):
                    for u in range(2):
                        for tc in range(NTC):
                            m = NTC * (n0 + 2 * i + u) + tc
                            q = 2 * NTC * i + NTC * u + tc
                            s = tc % 2
                            act.wait_ge(acc_done, m + 1)
                            after(act, stored[s], 16 * ((NTC // 2) * (n0 + 2 * i + u) + tc // 2))
                            to = split_hi if then == "split" else out
                            ins = nc.scalar.activation(to[s][:], acc[s][:], FUNCS[func])
                            ins.then_inc(act_out if then is None else dve_in, 1)
                        if more:
                            split_weights(n0 + 2 * i + u + 2, u)

                first = 0
                if n0 == 0:
                    pair(0, TOTAL > 2)
                    first = 1
                last = blocks // 2 - 1
                if last > first:
                    with act.Fori(first, last) as i:
                        pair(i, True)
                if last >= first:
                    pair(last, r + 1 < len(plan))

        @block.vector
        def _(dve):
            lo_base = 0
            for r, (cb, blocks, func, then, n0, a0, v0) in enumerate(plan):
                if then is None:
                    continue

                def pair(i):
                    for u in range(2):
                        for tc in range(NTC):
                            q = 2 * NTC * i + NTC * u + tc
                            s = tc % 2
                            dve.wait_ge(dve_in, v0 + q + 1)
                            if then == "split":
                                after(dve, stored_lo[s], 16 * ((NTC // 2) * (lo_base + 2 * i + u) + tc // 2))
                                nc.vector.tensor_tensor(split_lo[s][:], acc[s][:], split_hi[s][:].bitcast(F32),
                                                        ALU.subtract).then_inc(dve_out, 1)
                            else:
                                nc.vector.tensor_tensor(out[s][:], acc[s][:], out[s][:], ALU.mult).then_inc(dve_out, 1)

                if v0 == 0:
                    pair(0)
                    if blocks > 2:
                        with dve.Fori(1, blocks // 2) as i:
                            pair(i)
                else:
                    with dve.Fori(0, blocks // 2) as i:
                        pair(i)
                if then == "split":
                    lo_base += blocks



LEAD = 8


def reached(eng, sem, count):
    if isinstance(count, int) and count <= 0:
        return
    eng.wait_ge(sem, count + LEAD)


def arrived(eng, sem, count, each=16):
    eng.wait_ge(sem, (count + 1) * each)


UNITS = [(g, j, b, TC if j < g else (b + 1) * P) for g in range(NTC) for j in range(g, -1, -1) for b in range(4)]
NU = len(UNITS)
STEPS = [(g, j) for g in range(NTC) for j in range(g, -1, -1)]
NS = len(STEPS)
LAG = 3


def attention(nc, sem, g_, scr):
    with ExitStack() as ctx:
        sb = lambda n, s, d=F32: ctx.enter_context(nc.sbuf_tensor("a_" + n, s, d))
        ps = lambda n, s: ctx.enter_context(nc.psum_tensor("a_" + n, s, F32))
        s_ = lambda n: sem("a_" + n)
        k_hh = sb("k_hh", [P, T], F32R)
        k_ll = sb("k_ll", [P, T], F32R)
        v_hl = sb("v_hl", [P, T // P, P], F32R)
        q_hl = [sb(f"q_hl{i}", [P, TC], F32R) for i in range(2)]
        miss = [sb(f"miss{i}", [P, TC]) for i in range(2)]
        hit = [sb(f"hit{i}", [P, TC]) for i in range(4)]
        left = [sb(f"left{i}", [P, TC + 1]) for i in range(4)]
        aT_hi = sb("aT_hi", [P, 4, TC], F32R)
        aT_lo = sb("aT_lo", [P, 4, TC], F32R)
        o_hl = sb("o_hl", [P, TC])
        gate = [sb(f"gate{i}", [DH, TC]) for i in range(2)]
        keep, skip = sb("keep", [P, P]), sb("skip", [P, P])
        fold = sb("fold", [P, DH])
        z_ps = [ps(f"z{i}", [P, TC]) for i in range(2)]
        t_ps = [ps(f"t{i}", [P, 4, P]) for i in range(2)]
        o_ps = [ps(f"o{i}", [P, TC]) for i in range(2)]
        f_ps = ps("f", [DH, TC])
        kv_loaded = [s_(f"kv_loaded{c}") for c in range(4)]
        q_loaded = [s_(f"q_loaded{i}") for i in range(2)]
        gate_loaded = [s_(f"gate_loaded{i}") for i in range(2)]
        y_stored = [s_(f"y_stored{i}") for i in range(2)]
        z_done, sig_done, masked, carried, scanned = s_("z_done"), s_("sig_done"), s_("masked"), s_("carried"), s_("scanned")
        a_done, turned, hi_done, lo_done = s_("a_done"), s_("turned"), s_("hi_done"), s_("lo_done")
        masks_made = s_("masks_made")
        av_done, o_copied, folded, y_done, set_up = s_("av_done"), s_("o_copied"), s_("folded"), s_("y_done"), s_("set_up")
        ident = g_["ident"]
        KV_TRANSFERS = 6 * 16
        block = ctx.enter_context(nc.Block())

        def units_until(g):
            return 4 * sum(range(1, g + 1))

        def load_kv(eng, h, c):
            step = STEPS.index((NTC - 1, c))
            reached(eng, av_done, NS * (h - 1) + step + 1)
            cols, rows = slice(c * TC, (c + 1) * TC), bass.ds(h * DH, DH)
            krow = bass.ds(W + h * DH, DH)
            for half, v in ((slice(0, DH), "v_hi"), (slice(DH, P), "v_lo")):
                eng.dma_start(v_hl[:, 4 * c:4 * c + 4, half].bitcast(F32),
                              scr[v][cols, rows].rearrange("(b p) d -> p b d", p=P)).then_inc(kv_loaded[c], 16)
            for half in (slice(0, DH), slice(DH, P)):
                eng.dma_start(k_hh[half, cols].bitcast(F32), scr["proj"][krow, cols]).then_inc(kv_loaded[c], 16)
                eng.dma_start(k_ll[half, cols].bitcast(F32), scr["proj_lo"][krow, cols]).then_inc(kv_loaded[c], 16)

        def load_q(eng, h, g):
            cols, rows = slice(g * TC, (g + 1) * TC), bass.ds(h * DH, DH)
            reached(eng, z_done, NU * h + units_until(g - 1) if g >= 1 else NU * (h - 1) + units_until(3))
            for half, q in ((slice(0, DH), "proj"), (slice(DH, P), "proj_lo")):
                eng.dma_start(q_hl[g % 2][half, :].bitcast(F32), scr[q][rows, cols]).then_inc(q_loaded[g % 2], 16)
            arrived(eng, y_stored[g % 2], 2 * h + g // 2)
            eng.dma_start(gate[g % 2][:], scr["proj"][bass.ds(ZA * P + h * DH, DH), cols]).then_inc(gate_loaded[g % 2], 16)

        def store_y(eng, h, g):
            reached(eng, y_done, NTC * h + g + 1)
            eng.dma_start(scr["y"][0, bass.ds(h * DH, DH), g * TC:(g + 1) * TC], gate[g % 2][:]).then_inc(y_stored[g % 2], 16)

        @block.sync
        def _(sp):
            for s in y_stored:
                sp.sem_inc(s, 16)
            for c in range(4):
                load_kv(sp, 0, c)
                if c == 0:
                    load_q(sp, 0, 0)

            def head(h, more):
                for g in range(NTC):
                    if g + 1 < NTC:
                        load_q(sp, h, g + 1)
                    elif more:
                        load_q(sp, h + 1, 0)
                        for c in (3, 2, 1, 0):
                            load_kv(sp, h + 1, c)
                    store_y(sp, h, g)

            with sp.Fori(0, HEADS - 1) as h:
                head(h, True)
            head(HEADS - 1, False)
            for s in y_stored:
                arrived(sp, s, 2 * HEADS)

        @block.tensor
        def _(pe):
            for s in (z_done, turned, av_done, folded):
                pe.sem_inc(s, LEAD)

            def scores(h, u):
                g, j, b, width = UNITS[u]
                if b == 0 and j == g:
                    pe.wait_ge(q_loaded[g % 2], (4 * h + 2 * (g // 2) + 2) * 16)
                    pe.wait_ge(kv_loaded[g], (h + 1) * KV_TRANSFERS)
                reached(pe, sig_done, NU * h + u - 1)
                q = q_hl[g % 2][:, b * P:(b + 1) * P]
                nc.tensor.matmul(z_ps[u % 2][:, 0:width], q, k_hh[:, j * TC:j * TC + width], start=True, stop=False)
                nc.tensor.matmul(z_ps[u % 2][:, 0:width], q, k_ll[:, j * TC:j * TC + width],
                                 start=False, stop=True).then_inc(z_done, 1)

            def turn(h, u):
                width = UNITS[u][3]
                reached(pe, a_done, NU * h + u + 1)
                reached(pe, lo_done, NU * h + u - 1)
                for k in range(width // P):
                    mm = nc.tensor.transpose(t_ps[u % 2][:, k, :], hit[u % 4][:, k * P:(k + 1) * P], ident[:])
                mm.then_inc(turned, 1)

            def weighted_values(h, s):
                g, j = STEPS[s]
                reached(pe, lo_done, NU * h + 4 * (s + 1))
                if j == g:
                    reached(pe, o_copied, NTC * h + g - 1)
                for k in range(4):
                    c0 = k * P if j == g else 0
                    for part in (aT_hi, aT_lo):
                        mm = nc.tensor.matmul(o_ps[g % 2][:, c0:TC], v_hl[:, 4 * j + k, :], part[:, k, c0:TC],
                                              start=j == g and k == 0 and part is aT_hi,
                                              stop=j == 0 and k == 3 and part is aT_lo)
                mm.then_inc(av_done, 1)

            def fold_parts(h, g):
                reached(pe, o_copied, NTC * h + g + 1)
                reached(pe, y_done, NTC * h + g)
                nc.tensor.matmul(f_ps[:], fold[:], o_hl[:], start=True, stop=True).then_inc(folded, 1)

            pe.wait_ge(set_up, 5)
            with pe.Fori(0, HEADS) as h:
                for n in range(NU + LAG + 3):
                    if n < NU:
                        scores(h, n)
                    if 0 <= n - LAG < NU:
                        turn(h, n - LAG)
                    v = n - LAG - 1
                    if v >= 0 and v < NU and v % 4 == 3:
                        weighted_values(h, v // 4)
                    v = n - LAG - 3
                    if 0 <= v < NU and v % 4 == 3 and STEPS[v // 4][1] == 0:
                        fold_parts(h, STEPS[v // 4][0])

        @block.scalar
        def _(act):
            for s in (sig_done, hi_done, o_copied):
                act.sem_inc(s, LEAD)

            def sigmoids(h, u):
                width = UNITS[u][3]
                reached(act, z_done, NU * h + u + 1)
                reached(act, scanned, NU * h + u - 1)
                nc.scalar.activation(miss[u % 2][:, 0:width], z_ps[u % 2][:, 0:width], ACT.Sigmoid, scale=-SCALE)
                reached(act, turned, NU * h + u - 3)
                nc.scalar.activation(hit[u % 4][:, 0:width], z_ps[u % 2][:, 0:width], ACT.Sigmoid, scale=SCALE
                                     ).then_inc(sig_done, 1)

            def high(h, u):
                b, width = UNITS[u][2:]
                n = width // P
                reached(act, turned, NU * h + u + 1)
                reached(act, av_done, NS * h + u // 4)
                nc.scalar.activation(aT_hi[:, 0:n, b * P:(b + 1) * P], t_ps[u % 2][:, 0:n, :], ACT.Copy).then_inc(hi_done, 1)

            def copy_o(h, g):
                s = STEPS.index((g, 0))
                reached(act, av_done, NS * h + s + 1)
                reached(act, folded, NTC * h + g)
                nc.scalar.activation(o_hl[:], o_ps[g % 2][:], ACT.Copy).then_inc(o_copied, 1)

            with act.Fori(0, HEADS) as h:
                for n in range(NU + LAG + 3):
                    if n < NU:
                        sigmoids(h, n)
                    if 0 <= n - LAG < NU:
                        high(h, n - LAG)
                    v = n - LAG - 2
                    if 0 <= v < NU and v % 4 == 3 and STEPS[v // 4][1] == 0:
                        copy_o(h, STEPS[v // 4][0])

        @block.vector
        def _(dve):
            for s in (masked, carried, scanned, lo_done, y_done):
                dve.sem_inc(s, LEAD)
            nc.vector.tensor_tensor(fold[:], ident[:, 0:DH], ident[:, DH:P], ALU.add).then_inc(set_up, 1)
            for b in range(4):
                nc.vector.memset(left[b][:], 1.0).then_inc(set_up, 1)
            dve.wait_ge(set_up, 5)
            dve.wait_ge(masks_made, 4)

            diagonals = [u for u in range(NU) if UNITS[u][0] == UNITS[u][1]]
            inner = [u for u in range(NU) if u not in diagonals]

            def scan(h, u):
                g, j, b, width = UNITS[u]
                if j == g:
                    start = 1.0
                    reached(dve, sig_done, NU * h + u + 1)
                    last = slice(width - P, width)
                    nc.vector.tensor_tensor(miss[u % 2][:, last], miss[u % 2][:, last], skip[:], ALU.max).then_inc(masked, 1)
                    nc.vector.tensor_tensor(hit[u % 4][:, last], hit[u % 4][:, last], keep[:], ALU.mult).then_inc(masked, 1)
                    reached(dve, masked, 2 * (len(diagonals) * h + diagonals.index(u) + 1))
                    reached(dve, a_done, NU * h + u - 3)
                else:
                    start = left[b][:, TC:TC + 1]
                    reached(dve, a_done, NU * h + u - 3)
                    nc.vector.tensor_copy(left[b][:, TC:TC + 1], left[b][:, 0:1]).then_inc(carried, 1)
                    reached(dve, sig_done, NU * h + u + 1)
                    reached(dve, carried, len(inner) * h + inner.index(u) + 1)
                nc.vector.tensor_tensor_scan(left[b][:, 0:width][:, ::-1], miss[u % 2][:, 0:width][:, ::-1],
                                             miss[u % 2][:, 0:width][:, ::-1], start, ALU.mult, ALU.bypass
                                             ).then_inc(scanned, 1)

            def low(h, u):
                b, width = UNITS[u][2:]
                n = width // P
                reached(dve, hi_done, NU * h + u + 1)
                cols = slice(b * P, (b + 1) * P)
                nc.vector.tensor_tensor(aT_lo[:, 0:n, cols], t_ps[u % 2][:, 0:n, :], aT_hi[:, 0:n, cols].bitcast(F32),
                                        ALU.subtract).then_inc(lo_done, 1)

            def gated(h, g):
                reached(dve, folded, NTC * h + g + 1)
                dve.wait_ge(gate_loaded[g % 2], (2 * h + g // 2 + 1) * 16)
                nc.vector.tensor_tensor(gate[g % 2][:], f_ps[:], gate[g % 2][:], ALU.mult).then_inc(y_done, 1)

            with dve.Fori(0, HEADS) as h:
                for n in range(NU + LAG + 4):
                    if n < NU:
                        scan(h, n)
                    if 0 <= n - LAG < NU:
                        low(h, n - LAG)
                    v = n - LAG - 3
                    if 0 <= v < NU and v % 4 == 3 and STEPS[v // 4][1] == 0:
                        gated(h, STEPS[v // 4][0])

        @block.gpsimd
        def _(pool):
            pool.sem_inc(a_done, LEAD)
            nc.gpsimd.memset(keep[:], 1.0).then_inc(masks_made, 1)
            nc.gpsimd.memset(skip[:], 0.0).then_inc(masks_made, 1)
            pool.wait_ge(masks_made, 2)
            for tile, fill in ((keep, 0.0), (skip, 1.0)):
                nc.gpsimd.affine_select(out=tile[:], in_=tile[:], compare_op=ALU.is_gt, fill=fill, base=0,
                                        pattern=[[-1, P]], channel_multiplier=1).then_inc(masks_made, 1)

            def weights(h, u):
                b, width = UNITS[u][2:]
                reached(pool, scanned, NU * h + u + 1)
                nc.gpsimd.tensor_tensor(hit[u % 4][:, 0:width], hit[u % 4][:, 0:width], left[b][:, 1:width + 1],
                                        ALU.mult).then_inc(a_done, 1)

            with pool.Fori(0, HEADS) as h:
                for n in range(NU):
                    weights(h, n)


HH = 4
C = P
NCH = T // C
LEVELS = [1 << n for n in range(7)]


def hgrn2(nc, sem, g_, scr, lower_bounds, hgrn_norm_w):
    with ExitStack() as ctx:
        sb = lambda n, s, d=F32: ctx.enter_context(nc.sbuf_tensor("h_" + n, s, d))
        ps = lambda n, s: ctx.enter_context(nc.psum_tensor("h_" + n, s, F32))
        s_ = lambda n: sem("h_" + n)
        NL = len(LEVELS)
        NIN = 2 * NL + 3
        q = [sb(f"q{i}", [P, HH, C]) for i in range(2)]
        pre = [sb(f"pre{i}", [P, HH, C]) for i in range(2)]
        suf = [sb(f"suf{i}", [P, HH, C]) for i in range(2)]
        k = [sb(f"k{i}", [P, HH, C]) for i in range(2)]
        gate = [sb(f"gate{i}", [P, HH, C]) for i in range(2)]
        v = [sb(f"v{i}", [P, HH, C]) for i in range(2)]
        k_left = [sb(f"k_left{n}", [P, HH, C]) for n in range(NL)]
        q_right = [sb(f"q_right{n}", [P, HH * C // 2]) for n in range(NL)]
        part = [sb(f"part{i}", [P, HH, C // 2]) for i in range(2)]
        scores = [sb(f"scores{i}", [P, HH, C]) for i in range(2)]
        q_pre = [sb(f"q_pre{i}", [P, HH, C]) for i in range(2)]
        k_end = sb("k_end", [P, HH, C])
        kT = [sb(f"kT{i}", [P, HH, C]) for i in range(2)]
        state = [sb(f"state{i}", [P, HH, C]) for i in range(2)]
        tot = [sb(f"tot{i}", [P, HH]) for i in range(2)]
        sq = sb("sq", [P, HH, C])
        root = sb("root", [P, HH, C])
        inv = sb("inv", [P, HH, C])
        y = [sb(f"y{i}", [P, HH, C]) for i in range(2)]
        mask = [sb(f"mask{n}", [P, C // 2]) for n in range(NL)]
        ones = sb("ones", [P, P])
        eps = sb("eps", [P, 1])
        norm_w = sb("norm_w", [P, 1])
        lb = sb("lb", [P, 6, HH])
        s_ps = [ps(f"s{i}", [P, HH, C]) for i in range(2)]
        kT_ps = ps("kT", [P, HH, C])
        st_ps = ps("st", [P, HH, C])
        o_ps = ps("o", [P, HH, C])
        ms_ps = ps("ms", [P, HH, C])
        par_loaded, set_up, masks_done, lb_done = s_("par_loaded"), s_("set_up"), s_("masks_done"), s_("lb_done")
        front_loaded = [s_(f"front_loaded{i}") for i in range(2)]
        tail_loaded = [s_(f"tail_loaded{i}") for i in range(2)]
        stored = [s_(f"stored{i}") for i in range(2)]
        prep, prepared, level_in, joined = s_("prep"), s_("prepared"), s_("level_in"), s_("joined")
        s_done, parted, added, kT_turned, kT_done = s_("s_done"), s_("parted"), s_("added"), s_("kT_turned"), s_("kT_done")
        st_done, o_done, state_done, sq_done = s_("st_done"), s_("o_done"), s_("state_done"), s_("sq_done")
        ms_done, root_done, inv_done, gated, y_done = s_("ms_done"), s_("root_done"), s_("inv_done"), s_("gated"), s_("y_done")
        ident = g_["ident"]
        block = ctx.enter_context(nc.Block())

        def halves(tile, H):
            return tile[:].rearrange("p h (n two x) -> p (h n) two x", two=2, x=H)

        def chunks(eng, front, tail):
            front(0, 0)
            with eng.Fori(0, NCH // 2 - 1) as i:
                front(2 * i + 1, 1)
                tail(2 * i, 0)
                front(2 * i + 2, 0)
                tail(2 * i + 1, 1)
            front(NCH - 1, 1)
            tail(NCH - 2, 0)
            tail(NCH - 1, 1)

        @block.sync
        def _(sp):
            for s in stored:
                sp.sem_inc(s, 16)
            with nc.allow_non_contiguous_dma(reason="640 parameters, one to a partition"):
                sp.dma_start(norm_w[:], hgrn_norm_w.rearrange("a p -> p a")).then_inc(par_loaded, 16)
                sp.dma_start(lb[:, 0, :], lower_bounds.rearrange("a (h p) -> p (a h)", p=P)).then_inc(par_loaded, 16)

            def load_front(c, u):
                at = bass.ds(c * C, C)
                reached(sp, level_in, NIN * (c - 1))
                for tile, cb in ((q, QB), (pre, FB)):
                    sp.dma_start(tile[u][:], scr["proj"][cb * P:cb * P + HH * P, at].rearrange("(h p) t -> p h t", p=P)
                                 ).then_inc(front_loaded[u], 16)

            def load_tail(c, u):
                at = bass.ds(c * C, C)
                reached(sp, y_done, c - 1)
                sp.dma_start(gate[u][:], scr["proj"][ZB * P:ZB * P + HH * P, at].rearrange("(h p) t -> p h t", p=P)
                             ).then_inc(tail_loaded[u], 16)
                sp.dma_start(v[u][:], scr["i"][at, :].rearrange("t (h d) -> t h d", h=HH)).then_inc(tail_loaded[u], 16)

            def store(c, u):
                reached(sp, y_done, c + 1)
                sp.dma_start(scr["y"][1, :, bass.ds(c * C, C)].rearrange("(h p) t -> p h t", p=P), y[u][:]
                             ).then_inc(stored[u], 16)

            load_front(0, 0)
            load_front(1, 1)
            load_tail(0, 0)
            load_front(2, 0)
            load_tail(1, 1)

            def step(c, u):
                load_front(c + 2, u)
                store(c - 1, 1 - u)
                load_tail(c + 1, 1 - u)

            with sp.Fori(0, NCH // 2 - 2) as i:
                step(2 * i + 1, 1)
                step(2 * i + 2, 0)
            step(NCH - 3, 1)
            store(NCH - 3, 1)
            load_tail(NCH - 1, 1)
            store(NCH - 2, 0)
            store(NCH - 1, 1)
            for s in stored:
                arrived(sp, s, NCH // 2)

        @block.gpsimd
        def _(pool):
            for s in (prep, prepared, added):
                pool.sem_inc(s, LEAD)
            nc.gpsimd.memset(ones[:], 1.0).then_inc(set_up, 1)
            nc.gpsimd.memset(eps[:], RMS_EPS).then_inc(set_up, 1)
            nc.gpsimd.memset(state[1][:], 0.0).then_inc(set_up, 1)
            for n, H in enumerate(LEVELS):
                nc.gpsimd.memset(k_left[n][:], 0.0).then_inc(set_up, 1)
                nc.gpsimd.memset(mask[n][:], 1.0).then_inc(masks_done, 1)
            pool.wait_ge(masks_done, NL)
            for n, H in enumerate(LEVELS):
                m = mask[n][:].rearrange("p (b x) -> p b x", x=H)
                nc.gpsimd.affine_select(out=m, in_=m, compare_op=ALU.is_ge, fill=0.0, base=0,
                                        pattern=[[-2 * H, C // (2 * H)], [0, H]], channel_multiplier=1).then_inc(masks_done, 1)
                pool.wait_ge(masks_done, NL + 2 * n + 1)
                nc.gpsimd.affine_select(out=m, in_=m, compare_op=ALU.is_ge, fill=0.0, base=H - 1,
                                        pattern=[[2 * H, C // (2 * H)], [0, H]], channel_multiplier=-1).then_inc(masks_done, 1)
            pool.wait_ge(lb_done, 6)

            def prepare_at(i, u):
                c = 2 * i + u
                pool.wait_ge(front_loaded[u], (i + 1) * 32)
                reached(pool, level_in, NIN * (c - 1))
                reached(pool, s_done, (NL + 1) * (c - 2) + 1)
                nc.gpsimd.tensor_tensor(pre[u][:], pre[u][:], lb[:, 5, :].unsqueeze(2).to_broadcast([P, HH, C]), ALU.mult
                                        ).then_inc(prep, 1)
                reached(pool, prep, 2 * c + 1)
                nc.gpsimd.tensor_tensor(pre[u][:], pre[u][:], lb[:, 4, :].unsqueeze(2).to_broadcast([P, HH, C]), ALU.add
                                        ).then_inc(prep, 1)
                reached(pool, prep, 2 * c + 2)
                nc.gpsimd.tensor_tensor(k[u][:], ones[:].unsqueeze(1).to_broadcast([P, HH, C]), pre[u][:], ALU.subtract
                                        ).then_inc(prepared, 1)
                nc.gpsimd.memset(suf[u][:], 1.0).then_inc(prepared, 1)

            def add_parts(c, u):
                for n, H in enumerate(LEVELS):
                    reached(pool, parted, (NL + 1) * c + n + 2)
                    if n:
                        reached(pool, added, NL * c + n)
                    right = halves(scores[u], H)[:, :, 1, :]
                    nc.gpsimd.tensor_tensor(right, right, part[(n + u) % 2][:].rearrange("p h (b x) -> p (h b) x", x=H),
                                            ALU.add).then_inc(added, 1)

            prepare_at(0, 0)
            with pool.Fori(0, NCH // 2 - 1) as i:
                prepare_at(i, 1)
                add_parts(2 * i, 0)
                prepare_at(i + 1, 0)
                add_parts(2 * i + 1, 1)
            prepare_at(NCH // 2 - 1, 1)
            add_parts(NCH - 2, 0)
            add_parts(NCH - 1, 1)

        @block.tensor
        def _(pe):
            for s in (s_done, kT_turned, st_done, o_done, ms_done):
                pe.sem_inc(s, LEAD)
            pe.wait_ge(set_up, 3 + NL)

            def front(c, u):
                for n in range(NL + 1):
                    if n == 0:
                        reached(pe, prepared, 2 * (c + 1))
                    else:
                        reached(pe, level_in, NIN * c + 2 * n)
                    reached(pe, parted, (NL + 1) * c + n - 1)
                    for h in range(HH):
                        if n == 0:
                            mm = nc.tensor.matmul(s_ps[(n + u * (NL + 1)) % 2][:, h, :], k[u][:, h, :], q[u][:, h, :],
                                                  start=True, stop=True)
                        else:
                            mm = nc.tensor.matmul(s_ps[(n + u * (NL + 1)) % 2][:, h, 0:C // 2], k_left[n - 1][:, h, :],
                                                  q_right[n - 1][:, h * C // 2:(h + 1) * C // 2], start=True, stop=True)
                    mm.then_inc(s_done, 1)
                reached(pe, level_in, NIN * (c + 1))
                reached(pe, kT_done, c)
                for h in range(HH):
                    mm = nc.tensor.transpose(kT_ps[:, h, :], k_end[:, h, :], ident[:])
                mm.then_inc(kT_turned, 1)

            def tail(c, u):
                pe.wait_ge(tail_loaded[u], (c - u + 2) * 16)
                reached(pe, kT_done, c + 1)
                reached(pe, state_done, HH * c)
                for h in range(HH):
                    mm = nc.tensor.matmul(st_ps[:, h, :], kT[u][:, h, :], v[u][:, h, :], start=True, stop=True)
                mm.then_inc(st_done, 1)
                reached(pe, added, NL * (c + 1))
                reached(pe, gated, c)
                for h in range(HH):
                    nc.tensor.matmul(o_ps[:, h, :], v[u][:, h, :], scores[u][:, h, :], start=True, stop=False)
                    mm = nc.tensor.matmul(o_ps[:, h, :], state[1 - u][:, h, :], q_pre[u][:, h, :], start=False, stop=True)
                mm.then_inc(o_done, 1)
                reached(pe, sq_done, c + 1)
                reached(pe, root_done, c)
                nc.tensor.matmul(ms_ps[:], ones[:], sq[:], start=True, stop=True).then_inc(ms_done, 1)

            chunks(pe, front, tail)

        @block.scalar
        def _(act):
            for s in (kT_done, sq_done, root_done):
                act.sem_inc(s, LEAD)
            act.wait_ge(par_loaded, 32)
            act.wait_ge(lb_done, 1)
            nc.scalar.activation(lb[:, 1, :], lb[:, 2, :], ACT.Exp).then_inc(lb_done, 1)
            act.wait_ge(set_up, 3 + NL)

            def front(c, u):
                reached(act, kT_turned, c + 1)
                reached(act, st_done, c - 1)
                nc.scalar.activation(kT[u][:], kT_ps[:], ACT.Copy).then_inc(kT_done, 1)

            def tail(c, u):
                reached(act, o_done, c + 1)
                reached(act, ms_done, c)
                nc.scalar.activation(sq[:], o_ps[:], ACT.Square).then_inc(sq_done, 1)
                reached(act, ms_done, c + 1)
                reached(act, inv_done, c)
                nc.scalar.activation(root[:], ms_ps[:], ACT.Sqrt, scale=1.0 / C, bias=eps[:]).then_inc(root_done, 1)

            chunks(act, front, tail)

        @block.vector
        def _(dve):
            for s in (level_in, joined, parted, state_done, inv_done, gated, y_done):
                dve.sem_inc(s, LEAD)
            dve.wait_ge(par_loaded, 32)
            nc.vector.tensor_tensor(lb[:, 2, :], lb[:, 0, :], lb[:, 0, :], ALU.subtract).then_inc(lb_done, 1)
            dve.wait_ge(lb_done, 2)
            nc.vector.reciprocal(lb[:, 3, :], lb[:, 1, :]).then_inc(lb_done, 1)
            dve.wait_ge(lb_done, 3)
            nc.vector.tensor_tensor(lb[:, 1, :], lb[:, 1, :], lb[:, 3, :], ALU.mult).then_inc(lb_done, 1)
            dve.wait_ge(lb_done, 4)
            nc.vector.tensor_tensor(lb[:, 4, :], lb[:, 1, :], lb[:, 1, :], ALU.subtract).then_inc(lb_done, 1)
            dve.wait_ge(lb_done, 5)
            nc.vector.tensor_scalar(lb[:, 5, :], lb[:, 4, :], -1.0, 1.0, ALU.mult, ALU.add).then_inc(lb_done, 1)
            dve.wait_ge(set_up, 3 + NL)
            dve.wait_ge(masks_done, 3 * NL)

            def take_part(c, u, n):
                reached(dve, s_done, (NL + 1) * c + n + 1)
                bank = s_ps[(n + u * (NL + 1)) % 2]
                if n == 0:
                    reached(dve, o_done, c - 1)
                    nc.vector.tensor_tensor(scores[u][:], bank[:], ident[:].unsqueeze(1).to_broadcast([P, HH, C]),
                                            ALU.mult).then_inc(parted, 1)
                else:
                    reached(dve, added, NL * c + n - 2)
                    nc.vector.tensor_tensor(part[(n - 1 + u) % 2][:], bank[:, :, 0:C // 2],
                                            mask[n - 1][:].unsqueeze(1).to_broadcast([P, HH, C // 2]),
                                            ALU.mult).then_inc(parted, 1)

            def front(c, u):
                reached(dve, prepared, 2 * (c + 1))
                reached(dve, s_done, (NL + 1) * c)
                for n, H in enumerate(LEVELS):
                    if n:
                        reached(dve, joined, 2 * NL * c + 2 * n)
                    left, right = slice(0, 1), slice(1, 2)
                    kl, kk, ss, pp, qq = (halves(x, H) for x in (k_left[n], k[u], suf[u], pre[u], q[u]))
                    nc.vector.tensor_tensor(kl[:, :, 0, :], kk[:, :, 0, :], ss[:, :, 0, :], ALU.mult).then_inc(level_in, 1)
                    nc.vector.tensor_tensor(q_right[n][:].rearrange("p (b x) -> p b x", x=H), qq[:, :, 1, :], pp[:, :, 1, :],
                                            ALU.mult).then_inc(level_in, 1)
                    nb = HH * C // (2 * H)
                    nc.vector.tensor_tensor(ss[:, :, 0, :], ss[:, :, 0, :], pp[:, :, 1, H - 1:H].to_broadcast([P, nb, H]),
                                            ALU.mult).then_inc(joined, 1)
                    take_part(c, u, n)
                    reached(dve, joined, 2 * NL * c + 2 * n + 1)
                    nc.vector.tensor_tensor(pp[:, :, 1, :], pp[:, :, 1, :], pp[:, :, 0, H - 1:H].to_broadcast([P, nb, H]),
                                            ALU.mult).then_inc(joined, 1)
                reached(dve, joined, 2 * NL * (c + 1))
                reached(dve, kT_turned, c)
                nc.vector.tensor_tensor(k_end[:], k[u][:], suf[u][:], ALU.mult).then_inc(level_in, 1)
                reached(dve, o_done, c - 1)
                nc.vector.tensor_tensor(q_pre[u][:], q[u][:], pre[u][:], ALU.mult).then_inc(level_in, 1)
                nc.vector.tensor_copy(tot[u][:], pre[u][:, :, C - 1]).then_inc(level_in, 1)
                take_part(c, u, NL)

            def tail(c, u):
                reached(dve, level_in, NIN * (c + 1))
                reached(dve, st_done, c + 1)
                reached(dve, o_done, c)
                for h in range(HH):
                    nc.vector.scalar_tensor_tensor(state[u][:, h, :], state[1 - u][:, h, :], tot[u][:, h:h + 1],
                                                   st_ps[:, h, :], ALU.mult, ALU.add).then_inc(state_done, 1)
                dve.wait_ge(tail_loaded[u], (c - u + 2) * 16)
                reached(dve, sq_done, c + 1)
                nc.vector.scalar_tensor_tensor(gate[u][:], o_ps[:], norm_w[:, 0:1], gate[u][:], ALU.mult, ALU.mult
                                               ).then_inc(gated, 1)
                reached(dve, root_done, c + 1)
                reached(dve, y_done, c)
                nc.vector.reciprocal(inv[:], root[:]).then_inc(inv_done, 1)
                reached(dve, inv_done, c + 1)
                reached(dve, gated, c + 1)
                dve.wait_ge(stored[u], (c - u + 2) * 8)
                nc.vector.tensor_tensor(y[u][:], gate[u][:], inv[:], ALU.mult).then_inc(y_done, 1)

            chunks(dve, front, tail)


def short_conv(nc, sem, scr, conv_w):
    with ExitStack() as ctx:
        sb = lambda n, s, d=F32: ctx.enter_context(nc.sbuf_tensor("c_" + n, s, d))
        s_ = lambda n: sem("c_" + n)
        TAPS = 3
        pre = [sb(f"pre{i}", [P, T]) for i in range(2)]
        post = [sb(f"post{i}", [P, T]) for i in range(2)]
        u_ = [sb(f"u{i}", [P, T]) for i in range(2)]
        z = [sb(f"z{i}", [P, T]) for i in range(2)]
        prod = [sb(f"prod{i}", [P, TAPS - 1 + T]) for i in range(2)]
        acc = [sb(f"acc{i}", [P, T]) for i in range(2)]
        w = sb("w", [P, TAPS, WB])
        w_loaded = s_("w_loaded")
        loaded = [s_(f"loaded{i}") for i in range(2)]
        stored = [s_(f"stored{i}") for i in range(2)]
        prod_done, gate_done, acc_done, pads = s_("prod_done"), s_("gate_done"), s_("acc_done"), s_("pads")
        block = ctx.enter_context(nc.Block())

        @block.sync
        def _(sp):
            with nc.allow_non_contiguous_dma(reason="1536 taps, one to a partition"):
                for k in range(TAPS):
                    sp.dma_start(w[:, k, :], conv_w[0, k:k + 1].rearrange("a (b p) -> p (a b)", p=P)).then_inc(w_loaded, 16)
            for b in range(WB):
                after(sp, acc_done, 4 * (b - 1))
                for tile, cb in ((pre, PRE), (u_, UC), (post, POST), (z, ZC)):
                    sp.dma_start(tile[b % 2][:], scr["proj"][(cb + b) * P:(cb + b + 1) * P, :]).then_inc(loaded[b % 2], 16)
                if b:
                    store = b - 1
                    sp.wait_ge(acc_done, 4 * (store + 1))
                    sp.dma_start(scr["y"][2, store * P:(store + 1) * P, :], acc[store % 2][:]).then_inc(stored[store % 2], 16)
            sp.wait_ge(acc_done, 4 * WB)
            sp.dma_start(scr["y"][2, (WB - 1) * P:WB * P, :], acc[(WB - 1) % 2][:]).then_inc(stored[(WB - 1) % 2], 16)
            for s in stored:
                sp.wait_ge(s, 16 * WB // 2)

        @block.gpsimd
        def _(pool):
            for b in range(WB):
                pool.wait_ge(loaded[b % 2], 64 * (b // 2 + 1))
                nc.gpsimd.tensor_tensor(post[b % 2][:], post[b % 2][:], z[b % 2][:], ALU.mult).then_inc(gate_done, 1)

        @block.vector
        def _(dve):
            for i in range(2):
                nc.vector.memset(prod[i][:, 0:TAPS - 1], 0.0).then_inc(pads, 1)
            dve.wait_ge(pads, 2)
            dve.wait_ge(w_loaded, 16 * TAPS)
            for b in range(WB):
                s = b % 2
                dve.wait_ge(loaded[s], 64 * (b // 2 + 1))
                nc.vector.tensor_tensor(prod[s][:, TAPS - 1:], pre[s][:], u_[s][:], ALU.mult).then_inc(prod_done, 1)
                dve.wait_ge(prod_done, b + 1)
                after(dve, stored[s], 16 * (b // 2))
                nc.vector.tensor_scalar(acc[s][:], prod[s][:, 0:T], w[:, 0, b:b + 1], None, ALU.mult).then_inc(acc_done, 1)
                for k in range(1, TAPS):
                    dve.wait_ge(acc_done, 4 * b + k)
                    nc.vector.scalar_tensor_tensor(acc[s][:], prod[s][:, k:k + T], w[:, k, b:b + 1], acc[s][:],
                                                   ALU.mult, ALU.add).then_inc(acc_done, 1)
                dve.wait_ge(acc_done, 4 * b + TAPS)
                dve.wait_ge(gate_done, b + 1)
                nc.vector.tensor_tensor(acc[s][:], acc[s][:], post[s][:], ALU.mult).then_inc(acc_done, 1)


def merge_branches(nc, sem, scr, w_branch):
    with ExitStack() as ctx:
        sb = lambda n, s, d=F32: ctx.enter_context(nc.sbuf_tensor("m_" + n, s, d))
        s_ = lambda n: sem("m_" + n)
        NB, NM = 3, D // P
        w_raw = [sb(f"w_raw{i}", [P, D]) for i in range(2)]
        w_hi = sb("w_hi", [P, NB * WB, D], F32R)
        w_lo = sb("w_lo", [P, NB * WB, D], F32R)
        y_raw = sb("y_raw", [P, WB, TC])
        y_hi = [sb(f"y_hi{b}", [P, WB, TC], F32R) for b in range(NB)]
        y_lo = [sb(f"y_lo{b}", [P, WB, TC], F32R) for b in range(NB)]
        gate = [sb(f"gate{i}", [P, TC]) for i in range(4)]
        total = sb("total", [P, NM, TC])
        acc = [ctx.enter_context(nc.psum_tensor(f"m_acc{i}", [P, TC], F32)) for i in range(4)]
        w_loaded = [s_(f"w_loaded{i}") for i in range(2)]
        w_hi_done, w_lo_done = s_("w_hi_done"), s_("w_lo_done")
        y_loaded, y_hi_done, y_lo_done = s_("y_loaded"), s_("y_hi_done"), s_("y_lo_done")
        g_loaded = [s_(f"g_loaded{i}") for i in range(4)]
        acc_done, gated, summed = s_("acc_done"), s_("gated"), s_("summed")
        stored = s_("stored")
        block = ctx.enter_context(nc.Block())
        PER = NB * NM
        SUMS = (NB - 1) * NM

        @block.sync
        def _(sp):
            sp.sem_inc(stored, 16)

            def load_y(tc, b):
                n = NB * tc + b
                reached(sp, y_lo_done, n)
                sp.dma_start(y_raw[:], scr["y"][b, :, bass.ds(tc * TC, TC)].rearrange("(k p) t -> p k t", p=P)
                             ).then_inc(y_loaded, 16)

            def load_gates(tc, b, m0, m1):
                for m in range(m0, m1):
                    last = NM * b + m - 4
                    if 0 <= last < NM:
                        reached(sp, gated, PER * tc + last + 1)
                    else:
                        reached(sp, summed, SUMS * (tc if last > 0 else tc - 1) + (last % PER) - NM + 1)
                    sp.dma_start(gate[m % 4][:], scr["proj"][(GA + NM * b + m) * P:(GA + NM * b + m + 1) * P,
                                                             bass.ds(tc * TC, TC)]).then_inc(g_loaded[m % 4], 16)

            def load_w(k):
                if k >= 2:
                    reached(sp, w_lo_done, k - 1)
                sp.dma_start(w_raw[k % 2][:], w_branch[0, k // WB, (k % WB) * P:(k % WB + 1) * P, :]
                             ).then_inc(w_loaded[k % 2], 16)

            load_y(0, 0)
            for k in range(NB * WB):
                load_w(k)
                if k == 4:
                    load_y(0, 1)
                if k == 8:
                    load_y(0, 2)

            def group(tc, more):
                for b in range(NB):
                    load_gates(tc, b, 0, NM)
                    if more:
                        load_y(tc + 1, b)
                reached(sp, summed, SUMS * (tc + 1))
                sp.dma_start(scr["m"][:, bass.ds(tc * TC, TC)].rearrange("(m p) t -> p m t", p=P), total[:]
                             ).then_inc(stored, 16)

            with sp.Fori(0, NTC - 1) as tc:
                group(tc, True)
            group(NTC - 1, False)
            arrived(sp, stored, NTC)

        @block.tensor
        def _(pe):
            pe.sem_inc(acc_done, LEAD)

            def group(tc, peeled):
                for b in range(NB):
                    for m in range(NM):
                        n = PER * tc + NM * b + m
                        if m == 0:
                            reached(pe, y_lo_done, NB * tc + b + 1)
                        reached(pe, gated, n - 3)
                        cols = slice(m * P, (m + 1) * P)
                        for k in range(WB):
                            if peeled and m == 0:
                                reached(pe, w_lo_done, WB * b + k + 1)
                            wk = WB * b + k
                            nc.tensor.matmul(acc[m % 4][:], w_hi[:, wk, cols], y_hi[b][:, k, :], start=k == 0, stop=False)
                            nc.tensor.matmul(acc[m % 4][:], w_hi[:, wk, cols], y_lo[b][:, k, :], start=False, stop=False)
                            mm = nc.tensor.matmul(acc[m % 4][:], w_lo[:, wk, cols], y_hi[b][:, k, :],
                                                  start=False, stop=k == WB - 1)
                        mm.then_inc(acc_done, 1)

            group(0, True)
            with pe.Fori(1, NTC) as tc:
                group(tc, False)

        @block.scalar
        def _(act):
            for s in (w_hi_done, y_hi_done):
                act.sem_inc(s, LEAD)

            def split_y(tc, b):
                act.wait_ge(y_loaded, (NB * tc + b + 1) * 16)
                reached(act, acc_done, PER * (tc - 1) + NM * (b + 1) if b or not isinstance(tc, int) else 0)
                nc.scalar.activation(y_hi[b][:], y_raw[:], ACT.Copy).then_inc(y_hi_done, 1)

            def split_w(k):
                act.wait_ge(w_loaded[k % 2], 16 * (k // 2 + 1))
                nc.scalar.activation(w_hi[:, k, :], w_raw[k % 2][:], ACT.Copy).then_inc(w_hi_done, 1)

            for b in range(NB):
                split_y(0, b)
                for k in range(WB * b, WB * (b + 1)):
                    split_w(k)
            with act.Fori(1, NTC) as tc:
                for b in range(NB):
                    split_y(tc, b)

        @block.gpsimd
        def _(pool):
            for s in (w_lo_done, y_lo_done):
                pool.sem_inc(s, LEAD)

            def split_y(n, b):
                reached(pool, y_hi_done, n + 1)
                nc.gpsimd.tensor_tensor(y_lo[b][:], y_raw[:], y_hi[b][:].bitcast(F32), ALU.subtract).then_inc(y_lo_done, 1)

            for b in range(NB):
                split_y(b, b)
                for k in range(WB * b, WB * (b + 1)):
                    reached(pool, w_hi_done, k + 1)
                    nc.gpsimd.tensor_tensor(w_lo[:, k, :], w_raw[k % 2][:], w_hi[:, k, :].bitcast(F32), ALU.subtract
                                            ).then_inc(w_lo_done, 1)
            with pool.Fori(1, NTC) as tc:
                for b in range(NB):
                    split_y(NB * tc + b, b)

        @block.vector
        def _(dve):
            for s in (gated, summed):
                dve.sem_inc(s, LEAD)
            with dve.Fori(0, NTC) as tc:
                for b in range(NB):
                    for m in range(NM + 1):
                        if m < NM:
                            n = PER * tc + NM * b + m
                            reached(dve, acc_done, n + 1)
                            dve.wait_ge(g_loaded[m % 4], (tc * (PER // 4) + (NM * b + m) // 4 + 1) * 16)
                            if b == 0:
                                if m == 0:
                                    arrived(dve, stored, tc)
                                nc.vector.tensor_tensor(total[:, m, :], acc[m % 4][:], gate[m % 4][:], ALU.mult
                                                        ).then_inc(gated, 1)
                            else:
                                nc.vector.tensor_tensor(gate[m % 4][:], acc[m % 4][:], gate[m % 4][:], ALU.mult
                                                        ).then_inc(gated, 1)
                        if m > 0 and b > 0:
                            n = PER * tc + NM * b + m - 1
                            reached(dve, gated, n + 1)
                            nc.vector.tensor_tensor(total[:, m - 1, :], total[:, m - 1, :], gate[(m - 1) % 4][:], ALU.add
                                                    ).then_inc(summed, 1)


def project_out(nc, sem, scr, w_out, ln_g, ln_b, x, out):
    with ExitStack() as ctx:
        sb = lambda n, s, d=F32: ctx.enter_context(nc.sbuf_tensor("o_" + n, s, d))
        s_ = lambda n: sem("o_" + n)
        TG = 256
        NG, HALF = T // TG, D // 2
        w_raw = [sb(f"w_raw{i}", [P, D]) for i in range(2)]
        w_hi = sb("w_hi", [P, KD, D], F32R)
        w_lo = sb("w_lo", [P, KD, D], F32R)
        m_raw = sb("m_raw", [P, KD, TG])
        m_hi = [sb(f"m_hi{i}", [P, KD, TG], F32R) for i in range(2)]
        m_lo = [sb(f"m_lo{i}", [P, KD, TG], F32R) for i in range(2)]
        gate, gam, bet = sb("gate", [P, D]), sb("gam", [P, D]), sb("bet", [P, D])
        xt = [sb(f"xt{i}", [P, D]) for i in range(2)]
        r = [sb(f"r{i}", [P, D]) for i in range(2)]
        o = [sb(f"o{i}", [P, D]) for i in range(2)]
        stats = sb("stats", [P, 12])
        count = sb("count", [P, 1])
        mv = sb("mv", [P, 2])
        small = sb("small", [P, 3])
        acc = [ctx.enter_context(nc.psum_tensor(f"o_acc{i}", [P, HALF], F32)) for i in range(4)]
        par_loaded = s_("par_loaded")
        w_loaded = [s_(f"w_loaded{i}") for i in range(2)]
        m_loaded = s_("m_loaded")
        x_loaded = [s_(f"x_loaded{i}") for i in range(2)]
        stored = [s_(f"stored{i}") for i in range(2)]
        w_hi_done, w_lo_done, m_hi_done, m_lo_done = s_("w_hi_done"), s_("w_lo_done"), s_("m_hi_done"), s_("m_lo_done")
        acc_done, scaled, summed, stats_done, mv_done = s_("acc_done"), s_("scaled"), s_("summed"), s_("stats_done"), s_("mv_done")
        ve_done, std_done, rstd_done, xhat_done, gam_done, bet_done = (
            s_(n) for n in ("ve_done", "std_done", "rstd_done", "xhat_done", "gam_done", "bet_done"))
        block = ctx.enter_context(nc.Block())

        @block.sync
        def _(sp):
            for s in (*stored, *x_loaded):
                sp.sem_inc(s, 16)

            def load_m(i):
                reached(sp, m_lo_done, i)
                sp.dma_start(m_raw[:], scr["m"][:, bass.ds(i * TG, TG)].rearrange("(k p) t -> p k t", p=P)
                             ).then_inc(m_loaded, 16)

            def load_x(i, u):
                reached(sp, summed, 2 * (2 * i + u - 1))
                sp.dma_start(xt[u][:], x[bass.ds((2 * i + u) * P, P), :]).then_inc(x_loaded[u], 16)

            load_m(0)
            for k in range(KD):
                if k >= 2:
                    reached(sp, w_lo_done, k - 1)
                sp.dma_start(w_raw[k % 2][:], w_out[0, k * P:(k + 1) * P, :]).then_inc(w_loaded[k % 2], 16)
            sp.dma_start(gate[:], scr["gate"][0].partition_broadcast(P)).then_inc(par_loaded, 16)
            sp.dma_start(gam[:], ln_g[0].partition_broadcast(P)).then_inc(par_loaded, 16)
            sp.dma_start(bet[:], ln_b[0].partition_broadcast(P)).then_inc(par_loaded, 16)
            load_x(0, 0)
            load_x(0, 1)

            def group(i, more):
                if more:
                    load_m(i + 1)
                for u in range(2):
                    reached(sp, bet_done, 2 * i + u + 1)
                    sp.dma_start(out[0, bass.ds((2 * i + u) * P, P), :], o[u][:]).then_inc(stored[u], 16)
                    if more:
                        load_x(i + 1, u)

            with sp.Fori(0, NG - 1) as i:
                group(i, True)
            group(NG - 1, False)
            for s in stored:
                arrived(sp, s, NG)

        @block.tensor
        def _(pe):
            pe.sem_inc(acc_done, LEAD)

            def group(i, s):
                for u in range(2):
                    for half in range(2):
                        n = 8 * i + 4 * s + 2 * u + half
                        reached(pe, scaled, n - 3)
                        bank = acc[2 * u + half]
                        cols, tok = slice(half * HALF, (half + 1) * HALF), slice(u * P, (u + 1) * P)
                        if u == 0 and half == 0:
                            reached(pe, m_lo_done, 2 * i + s + 1)
                        for k in range(KD):
                            if n is not None and isinstance(i, int) and u == 0 and half == 0:
                                reached(pe, w_lo_done, k + 1)
                            nc.tensor.matmul(bank[:], m_hi[s][:, k, tok], w_hi[:, k, cols], start=k == 0, stop=False)
                            nc.tensor.matmul(bank[:], m_hi[s][:, k, tok], w_lo[:, k, cols], start=False, stop=False)
                            mm = nc.tensor.matmul(bank[:], m_lo[s][:, k, tok], w_hi[:, k, cols],
                                                  start=False, stop=k == KD - 1)
                        mm.then_inc(acc_done, 1)

            group(0, 0)
            group(0, 1)
            with pe.Fori(1, NG // 2) as i:
                group(i, 0)
                group(i, 1)

        @block.scalar
        def _(act):
            for s in (w_hi_done, m_hi_done, std_done):
                act.sem_inc(s, LEAD)

            def split_m(i, s):
                act.wait_ge(m_loaded, (2 * i + s + 1) * 16)
                reached(act, acc_done, 4 * (2 * i + s) - 4)
                nc.scalar.activation(m_hi[s][:], m_raw[:], ACT.Copy).then_inc(m_hi_done, 1)

            def roots(i, s):
                for u in range(2):
                    n = 4 * i + 2 * s + u
                    reached(act, ve_done, n + 1)
                    nc.scalar.activation(small[:, 1:2], small[:, 0:1], ACT.Sqrt).then_inc(std_done, 1)

            split_m(0, 0)
            for k in range(KD):
                act.wait_ge(w_loaded[k % 2], 16 * (k // 2 + 1))
                nc.scalar.activation(w_hi[:, k, :], w_raw[k % 2][:], ACT.Copy).then_inc(w_hi_done, 1)
            with act.Fori(0, NG // 2 - 1) as i:
                split_m(i, 1)
                roots(i, 0)
                split_m(i + 1, 0)
                roots(i, 1)
            split_m(NG // 2 - 1, 1)
            roots(NG // 2 - 1, 0)
            roots(NG // 2 - 1, 1)

        @block.gpsimd
        def _(pool):
            for s in (w_lo_done, m_lo_done, bet_done):
                pool.sem_inc(s, LEAD)

            def split_m(i, s):
                reached(pool, m_hi_done, 2 * i + s + 1)
                nc.gpsimd.tensor_tensor(m_lo[s][:], m_raw[:], m_hi[s][:].bitcast(F32), ALU.subtract).then_inc(m_lo_done, 1)

            def shift(i, s):
                for u in range(2):
                    n = 4 * i + 2 * s + u
                    reached(pool, gam_done, n + 1)
                    pool.wait_ge(stored[u], (2 * i + s + 1) * 16)
                    nc.gpsimd.tensor_tensor(o[u][:], r[u][:], bet[:], ALU.add).then_inc(bet_done, 1)

            split_m(0, 0)
            for k in range(KD):
                reached(pool, w_hi_done, k + 1)
                nc.gpsimd.tensor_tensor(w_lo[:, k, :], w_raw[k % 2][:], w_hi[:, k, :].bitcast(F32), ALU.subtract
                                        ).then_inc(w_lo_done, 1)
            pool.wait_ge(par_loaded, 48)
            with pool.Fori(0, NG // 2 - 1) as i:
                split_m(i, 1)
                shift(i, 0)
                split_m(i + 1, 0)
                shift(i, 1)
            split_m(NG // 2 - 1, 1)
            shift(NG // 2 - 1, 0)
            shift(NG // 2 - 1, 1)

        @block.vector
        def _(dve):
            for s in (scaled, summed, stats_done, mv_done, ve_done, rstd_done, xhat_done, gam_done):
                dve.sem_inc(s, LEAD)
            dve.wait_ge(par_loaded, 48)
            with dve.Fori(0, NG) as i:
                for u in range(2):
                    n = 2 * i + u
                    reached(dve, bet_done, n - 1)
                    for half in range(2):
                        cols = slice(half * HALF, (half + 1) * HALF)
                        reached(dve, acc_done, 2 * n + half + 1)
                        nc.vector.tensor_tensor(r[u][:, cols], acc[2 * u + half][:], gate[:, cols], ALU.mult).then_inc(scaled, 1)
                    dve.wait_ge(x_loaded[u], (i + 2) * 16)
                    for half in range(2):
                        cols = slice(half * HALF, (half + 1) * HALF)
                        reached(dve, scaled, 2 * n + half + 1)
                        nc.vector.scalar_tensor_tensor(r[u][:, cols], xt[u][:, cols], ALPHA, r[u][:, cols],
                                                       ALU.mult, ALU.add).then_inc(summed, 1)
                    for half in range(2):
                        cols = slice(half * HALF, (half + 1) * HALF)
                        reached(dve, summed, 2 * n + half + 1)
                        nc.vector.bn_stats(stats[:, 6 * half:6 * half + 6], r[u][:, cols]).then_inc(stats_done, 1)
                    reached(dve, stats_done, 2 * n + 2)
                    nc.vector.tensor_copy(count[:], stats[:, 0:1])
                    nc.vector.bn_aggr(mv[:], stats[:]).then_inc(mv_done, 1)
                    reached(dve, mv_done, n + 1)
                    nc.vector.tensor_scalar(small[:, 0:1], mv[:, 1:2], LN_EPS, None, ALU.add).then_inc(ve_done, 1)
                    reached(dve, std_done, n + 1)
                    nc.vector.reciprocal(small[:, 2:3], small[:, 1:2]).then_inc(rstd_done, 1)
                    reached(dve, rstd_done, n + 1)
                    nc.vector.tensor_scalar(r[u][:], r[u][:], mv[:, 0:1], small[:, 2:3], ALU.subtract, ALU.mult
                                            ).then_inc(xhat_done, 1)
                    reached(dve, xhat_done, n + 1)
                    nc.vector.tensor_tensor(r[u][:], r[u][:], gam[:], ALU.mult).then_inc(gam_done, 1)


def build(nc, x, c, w_mod, b_mod, w_in, conv_w, hgrn_norm_w, lower_bounds, w_branch, w_out, ln_g, ln_b, out):
    dram = lambda n, s: nc.dram_tensor(n, s, F32).ap()
    proj = dram("proj", (IN_COLS + D + 3 * W, T))
    values = dram("values", (3, T, W))
    scr = {
        "gate": dram("gate_row", (1, D)),
        "proj": proj[0:IN_COLS],
        "proj_lo": dram("proj_lo", (2 * W, T)),
        "i": values[0], "v_hi": values[1], "v_lo": values[2],
        "m": proj[IN_COLS:IN_COLS + D],
        "y": proj[IN_COLS + D:].rearrange("(b w) t -> b w t", b=3),
    }

    def stage(f, *args):
        with nc.cleanup_on_exit():
            f(nc, lambda name: nc.alloc_semaphore(name=name), *args)

    with nc.sbuf_tensor("ident", [P, P], F32) as ident:
        with nc.sbuf_tensor("hT_hi", [P, KD, T], F32R) as hT_hi, nc.sbuf_tensor("hT_lo", [P, KD, T], F32R) as hT_lo:
            g = {"ident": ident, "hT_hi": hT_hi, "hT_lo": hT_lo}
            stage(modulated_input, g, x[0], c, w_mod, b_mod, scr)
            stage(token_major_values, g, w_in, scr)
            stage(project, g, w_in, scr, RUNS_1, "p1_")
            stage(project, g, w_in, scr, RUNS_2, "p2_")
        g = {"ident": ident}
        stage(attention, g, scr)
        stage(hgrn2, g, scr, lower_bounds, hgrn_norm_w)
        stage(short_conv, scr, conv_w)
        stage(merge_branches, scr, w_branch)
        stage(project_out, scr, w_out, ln_g, ln_b, x[0], out)


_INS = ["x", "c", "w_mod", "b_mod", "w_in", "conv_w", "hgrn_norm_w", "lower_bounds", "w_branch", "w_out", "ln_g", "ln_b"]


def kernel(**inputs):
    import numpy as np
    import concourse.bacc as bacc
    from concourse.bass_utils import run_bass_kernel_spmd

    nc = bacc.Bacc("TRN2", target_bir_lowering=False, num_devices=1)
    arrays, args = {}, []
    for name in _INS:
        a = np.ascontiguousarray(inputs[name])
        arrays[f"in_{name}"] = a
        args.append(nc.dram_tensor(f"in_{name}", a.shape, mybir.dt.from_np(a.dtype), kind="ExternalInput").ap())
    out = nc.dram_tensor("out_x", (1, T, D), F32, kind="ExternalOutput").ap()
    build(nc, *args, out)
    r = run_bass_kernel_spmd(nc, [arrays], core_ids=[0])
    return r.results[0]["out_x"]
```

```python
from contextlib import ExitStack

import concourse.bass as bass
from concourse import mybir

F32 = mybir.dt.float32
F32R = mybir.dt.float32r
ACT = mybir.ActivationFunctionType
ALU = mybir.AluOpType
AX = mybir.AxisListType

P = 128
T = 2048
D = 1024
KD = D // P
TC = 512
NTC = T // TC
W = 512
WB = W // P
IN_COLS = 12 * W + 3 * D
NCB = IN_COLS // P
HEADS, DH = 8, 64
ALPHA = 2.0 ** 0.25
LN_EPS = 1e-5
RMS_EPS = 1e-6
SCALE = DH ** -0.5

QA, KA, VA, ZA, QB, FB, IB, ZB, PRE, POST, UC, ZC, GA = (WB * n for n in range(13))

RUNS = [(ZA, 8, "Sigmoid", "gate"), (FB, 4, "Sigmoid", None), (ZB, 4, "Sigmoid", "gate"), (UC, 4, "Copy", None),
        (ZC, 4, "Sigmoid", "gate")]
FUNCS = {"Copy": ACT.Copy, "Sigmoid": ACT.Sigmoid}


def after(eng, sem, value):
    if isinstance(value, int) and value <= 0:
        return
    eng.wait_ge(sem, value)


def modulated_input(nc, sem, g, x, c, w_mod, b_mod, scr):
    with ExitStack() as ctx:
        sb = lambda n, s, d=F32: ctx.enter_context(nc.sbuf_tensor(n, s, d))
        MC = 256
        NM = 3 * D // MC
        c_col = sb("c_col", [P, KD])
        c_rep = sb("c_rep", [P, KD, P])
        mod = sb("mod", [P, 3 * D])
        wm = [sb(f"wm{i}", [P, KD, MC]) for i in range(2)]
        xt = [sb(f"xt{i}", [P, D]) for i in range(4)]
        hm = [sb(f"hm{i}", [P, D]) for i in range(2)]
        stats = sb("stats", [P, 4, 12])
        count = sb("count", [P, 1])
        mv = sb("mv", [P, 4, 2])
        ve = sb("ve", [P, 4])
        std = sb("std", [P, 4])
        rstd = sb("rstd", [P, 4])
        ps_mod = [ctx.enter_context(nc.psum_tensor(f"ps_mod{i}", [P, MC], F32)) for i in range(2)]
        ps_t = [ctx.enter_context(nc.psum_tensor(f"ps_t{i}", [P, 4, P], F32)) for i in range(4)]
        c_loaded, b_loaded, c_spread = sem("c_loaded"), sem("b_loaded"), sem("c_spread")
        wm_loaded = [sem(f"wm_loaded{i}") for i in range(2)]
        mod_summed, mod_ready, gate_stored = sem("mod_summed"), sem("mod_ready"), sem("gate_stored")
        x_loaded = [sem(f"x_loaded{i}") for i in range(4)]
        stats_done, mv_done, ve_done, std_done = sem("stats_done"), sem("mv_done"), sem("ve_done"), sem("std_done")
        rstd_done, xhat_done, scaled_done, hm_done = sem("rstd_done"), sem("xhat_done"), sem("scaled_done"), sem("hm_done")
        turned, hi_done, lo_done = sem("turned"), sem("hi_done"), sem("lo_done")
        ident_zero = sem("ident_zero")
        ident_ready = sem("ident_ready")
        ident, hT_hi, hT_lo = g["ident"], g["hT_hi"], g["hT_lo"]
        block = ctx.enter_context(nc.Block())

        def load_x(eng, i, u):
            after(eng, xhat_done, 4 * i + u - 3)
            eng.dma_start(xt[u][:], x[bass.ts(4 * i + u, P), :]).then_inc(x_loaded[u], 16)

        @block.sync
        def _(sp):
            with nc.allow_non_contiguous_dma(reason="1024 values of c"):
                sp.dma_start(c_col[:], c.rearrange("a (k p) -> p (a k)", p=P)).then_inc(c_loaded, 16)
            sp.dma_start(mod[:], b_mod[0].partition_broadcast(P)).then_inc(b_loaded, 16)
            for m in range(NM):
                if m >= 2:
                    sp.wait_ge(mod_summed, m - 1)
                sp.dma_start(wm[m % 2][:], w_mod[0, :, m * MC:(m + 1) * MC].rearrange("(k p) n -> p k n", p=P)
                             ).then_inc(wm_loaded[m % 2], 16)
                if m == 1:
                    for u in range(4):
                        load_x(sp, 0, u)
            with sp.Fori(1, 4) as i:
                for u in range(4):
                    load_x(sp, i, u)
            sp.wait_ge(mod_ready, NM)
            sp.dma_start(scr["gate"], mod[0:1, 2 * D:3 * D]).then_inc(gate_stored, 16)
            sp.wait_ge(gate_stored, 16)

        @block.gpsimd
        def _(pool):
            nc.gpsimd.memset(ident[:], 0.0).then_inc(ident_zero, 1)
            pool.wait_ge(ident_zero, 1)
            nc.gpsimd.affine_select(out=ident[:], in_=ident[:], compare_op=ALU.not_equal, fill=1.0, base=0,
                                    pattern=[[-1, P]], channel_multiplier=1).then_inc(ident_ready, 1)
            pool.wait_ge(mod_ready, NM)
            with pool.Fori(0, 8) as i:
                for u in range(2):
                    pool.wait_ge(scaled_done, 2 * i + u + 1)
                    nc.gpsimd.tensor_tensor(hm[u][:], hm[u][:], mod[:, 0:D], ALU.add).then_inc(hm_done, 1)

        @block.tensor
        def _(pe):
            pe.wait_ge(c_spread, 1)
            for m in range(NM):
                pe.wait_ge(wm_loaded[m % 2], 16 * (m // 2 + 1))
                if m >= 2:
                    pe.wait_ge(mod_ready, m - 1)
                for k in range(KD):
                    mm = nc.tensor.matmul(ps_mod[m % 2][:], c_rep[:, k, :], wm[m % 2][:, k, :],
                                          start=k == 0, stop=k == KD - 1)
                mm.then_inc(mod_summed, 1)
            pe.wait_ge(ident_ready, 1)
            with pe.Fori(0, 8) as i:
                for u in range(2):
                    pe.wait_ge(hm_done, 2 * i + u + 1)
                    pe.wait_ge(lo_done, 4 * i + 2 * u + 2)
                    for half in range(2):
                        for k in range(4):
                            mm = nc.tensor.transpose(ps_t[2 * u + half][:, k, :],
                                                     hm[u][:, (4 * half + k) * P:(4 * half + k + 1) * P], ident[:])
                        mm.then_inc(turned, 1)

        @block.scalar
        def _(act):
            def root(i, u):
                act.wait_ge(ve_done, 4 * i + u + 1)
                nc.scalar.activation(std[:, u:u + 1], ve[:, u:u + 1], ACT.Sqrt).then_inc(std_done, 1)

            def high(t4, u):
                for half in range(2):
                    act.wait_ge(turned, 8 * t4 + 2 * u + half + 1)
                    nc.scalar.activation(hT_hi[:, 4 * half:4 * half + 4, bass.ds((4 * t4 + u) * P, P)],
                                         ps_t[2 * (u % 2) + half][:], ACT.Copy).then_inc(hi_done, 1)

            root(0, 0)
            with act.Fori(0, 3) as i:
                for u in range(4):
                    if u < 3:
                        root(i, u + 1)
                    else:
                        root(i + 1, 0)
                    high(i, u)
            for u in range(4):
                if u < 3:
                    root(3, u + 1)
                high(3, u)

        @block.vector
        def _(dve):
            nc.vector.sem_inc(lo_done, 4)

            def statistics(i, u):
                dve.wait_ge(x_loaded[u], 16 * (i + 1))
                for half in range(2):
                    nc.vector.bn_stats(stats[:, u, 6 * half:6 * half + 6], xt[u][:, 512 * half:512 * half + 512]
                                       ).then_inc(stats_done, 1)
                dve.wait_ge(stats_done, 8 * i + 2 * u + 2)
                nc.vector.tensor_copy(count[:], stats[:, u, 0:1])
                nc.vector.bn_aggr(mv[:, u, :], stats[:, u, :]).then_inc(mv_done, 1)
                dve.wait_ge(mv_done, 4 * i + u + 1)
                nc.vector.tensor_scalar(ve[:, u:u + 1], mv[:, u, 1:2], LN_EPS, None, ALU.add).then_inc(ve_done, 1)

            def normalise(i, u):
                n = 4 * i + u
                dve.wait_ge(std_done, n + 1)
                nc.vector.reciprocal(rstd[:, u:u + 1], std[:, u:u + 1]).then_inc(rstd_done, 1)
                dve.wait_ge(rstd_done, n + 1)
                after(dve, turned, 8 * i + 2 * u - 2)
                nc.vector.tensor_scalar(hm[u % 2][:], xt[u][:], mv[:, u, 0:1], rstd[:, u:u + 1],
                                        ALU.subtract, ALU.mult).then_inc(xhat_done, 1)
                dve.wait_ge(xhat_done, n + 1)
                nc.vector.tensor_tensor(hm[u % 2][:], hm[u % 2][:], mod[:, D:2 * D], ALU.mult).then_inc(scaled_done, 1)

            def low(i, u):
                for half in range(2):
                    dve.wait_ge(hi_done, 8 * i + 2 * u + half + 1)
                    at = bass.ds((4 * i + u) * P, P)
                    nc.vector.tensor_tensor(hT_lo[:, 4 * half:4 * half + 4, at], ps_t[2 * (u % 2) + half][:],
                                            hT_hi[:, 4 * half:4 * half + 4, at].bitcast(F32),
                                            ALU.subtract).then_inc(lo_done, 1)

            dve.wait_ge(c_loaded, 16)
            nc.vector.tensor_copy(c_rep[:], c_col[:].unsqueeze(2).to_broadcast([P, KD, P])).then_inc(c_spread, 1)
            dve.wait_ge(b_loaded, 16)
            for m in range(NM):
                dve.wait_ge(mod_summed, m + 1)
                cols = mod[:, m * MC:(m + 1) * MC]
                nc.vector.scalar_tensor_tensor(cols, ps_mod[m % 2][:], 0.0 if m * MC < D else 1.0, cols,
                                               ALU.add, ALU.add).then_inc(mod_ready, 1)
                if m == 5:
                    statistics(0, 0)
            dve.wait_ge(mod_ready, NM)

            def steps(i, first=False, last=False):
                for u in range(4):
                    if u < 3:
                        statistics(i, u + 1)
                    elif not last:
                        statistics(i + 1, 0)
                    normalise(i, u)
                    if u > 0:
                        low(i, u - 1)
                    elif not first:
                        low(i - 1, 3)

            steps(0, first=True)
            with dve.Fori(1, 3) as i:
                steps(i)
            steps(3, last=True)
            low(3, 3)


def token_major_values(nc, sem, g, w_in, scr):
    with ExitStack() as ctx:
        sb = lambda n, s, d=F32: ctx.enter_context(nc.sbuf_tensor(n, s, d))
        NC_ = 256
        UNITS = [(VA * P, 0, True), (VA * P + NC_, NC_, True), (IB * P, 0, False), (IB * P + NC_, NC_, False)]
        NT = T // P
        w_raw = [sb(f"vw_raw{i}", [P, KD, NC_]) for i in range(2)]
        w_hi = [sb(f"vw_hi{i}", [P, KD, NC_], F32R) for i in range(2)]
        w_lo = [sb(f"vw_lo{i}", [P, KD, NC_], F32R) for i in range(2)]
        v_hi = [sb(f"v_hi{i}", [P, NC_], F32R) for i in range(2)]
        v_lo = [sb(f"v_lo{i}", [P, NC_], F32R) for i in range(2)]
        i_out = [sb(f"i_out{i}", [P, NC_]) for i in range(2)]
        acc = [ctx.enter_context(nc.psum_tensor(f"v_acc{i}", [P, NC_], F32)) for i in range(2)]
        w_loaded = [sem(f"vw_loaded{i}") for i in range(2)]
        w_hi_done, w_lo_done, unit_done = sem("vw_hi_done"), sem("vw_lo_done"), sem("v_unit_done")
        acc_done, hi_done, lo_done, i_done = sem("v_acc_done"), sem("v_hi_done"), sem("v_lo_done"), sem("i_done")
        hi_stored = [sem(f"v_hi_stored{i}") for i in range(2)]
        lo_stored = [sem(f"v_lo_stored{i}") for i in range(2)]
        i_stored = [sem(f"i_stored{i}") for i in range(2)]
        hT_hi, hT_lo = g["hT_hi"], g["hT_lo"]
        block = ctx.enter_context(nc.Block())

        @block.sync
        def _(sp):
            def load(n):
                after(sp, w_lo_done, 8 * (n - 1))
                c0 = UNITS[n][0]
                sp.dma_start(w_raw[n % 2][:], w_in[0, :, c0:c0 + NC_].rearrange("(k p) n -> p k n", p=P)
                             ).then_inc(w_loaded[n % 2], 16)

            load(0)
            load(1)
            for n, (_, col, split) in enumerate(UNITS):
                for t in range(NT):
                    m = NT * n + t
                    rows = slice(t * P, (t + 1) * P)
                    if split:
                        sp.wait_ge(lo_done, m + 1)
                        sp.dma_start(scr["v_hi"][rows, col:col + NC_], v_hi[m % 2][:].bitcast(F32)
                                     ).then_inc(hi_stored[m % 2], 16)
                        sp.dma_start(scr["v_lo"][rows, col:col + NC_], v_lo[m % 2][:].bitcast(F32)
                                     ).then_inc(lo_stored[m % 2], 16)
                    else:
                        sp.wait_ge(i_done, m - 2 * NT + 1)
                        sp.dma_start(scr["i"][rows, col:col + NC_], i_out[m % 2][:]).then_inc(i_stored[m % 2], 16)
                if n + 2 < len(UNITS):
                    load(n + 2)
            for u in range(2):
                sp.wait_ge(hi_stored[u], 16 * NT)
                sp.wait_ge(lo_stored[u], 16 * NT)
                sp.wait_ge(i_stored[u], 16 * NT)

        @block.tensor
        def _(pe):
            for n, (_, _, split) in enumerate(UNITS):
                for t in range(NT):
                    m = NT * n + t
                    if m - 2 < 2 * NT:
                        after(pe, lo_done, m - 1)
                    else:
                        pe.wait_ge(i_done, m - 1 - 2 * NT)
                    tok = slice(t * P, (t + 1) * P)
                    for k in range(KD):
                        if t == 0:
                            pe.wait_ge(w_lo_done, KD * n + k + 1)
                        nc.tensor.matmul(acc[m % 2][:], hT_hi[:, k, tok], w_hi[n % 2][:, k, :], start=k == 0, stop=False)
                        nc.tensor.matmul(acc[m % 2][:], hT_hi[:, k, tok], w_lo[n % 2][:, k, :], start=False, stop=False)
                        mm = nc.tensor.matmul(acc[m % 2][:], hT_lo[:, k, tok], w_hi[n % 2][:, k, :],
                                              start=False, stop=k == KD - 1)
                    mm.then_inc(acc_done, 1)

        @block.scalar
        def _(act):
            def split_weights(n):
                act.wait_ge(w_loaded[n % 2], 16 * (n // 2 + 1))
                after(act, acc_done, NT * (n - 1))
                for k in range(KD):
                    nc.scalar.activation(w_hi[n % 2][:, k, :], w_raw[n % 2][:, k, :], ACT.Copy).then_inc(w_hi_done, 1)

            split_weights(0)
            for n, (_, _, split) in enumerate(UNITS):
                for t in range(NT):
                    m = NT * n + t
                    if t == 2 and n + 1 < len(UNITS):
                        split_weights(n + 1)
                    act.wait_ge(acc_done, m + 1)
                    if split:
                        after(act, hi_stored[m % 2], 16 * (m // 2))
                        nc.scalar.activation(v_hi[m % 2][:], acc[m % 2][:], ACT.Copy).then_inc(hi_done, 1)
                    else:
                        after(act, i_stored[m % 2], 16 * ((m - 2 * NT) // 2))
                        nc.scalar.activation(i_out[m % 2][:], acc[m % 2][:], ACT.Copy).then_inc(i_done, 1)

        @block.vector
        def _(dve):
            def split_weights(n):
                for k in range(KD):
                    dve.wait_ge(w_hi_done, KD * n + k + 1)
                    nc.vector.tensor_tensor(w_lo[n % 2][:, k, :], w_raw[n % 2][:, k, :],
                                            w_hi[n % 2][:, k, :].bitcast(F32), ALU.subtract).then_inc(w_lo_done, 1)

            split_weights(0)
            for n, (_, _, split) in enumerate(UNITS):
                for t in range(NT):
                    m = NT * n + t
                    if t == 2 and n + 1 < len(UNITS):
                        split_weights(n + 1)
                    if split:
                        dve.wait_ge(hi_done, m + 1)
                        after(dve, lo_stored[m % 2], 16 * (m // 2))
                        nc.vector.tensor_tensor(v_lo[m % 2][:], acc[m % 2][:], v_hi[m % 2][:].bitcast(F32),
                                                ALU.subtract).then_inc(lo_done, 1)


def project(nc, sem, g, w_in, scr, runs, tag):
    with ExitStack() as ctx:
        sb = lambda n, s, d=F32: ctx.enter_context(nc.sbuf_tensor(tag + n, s, d))
        s_ = lambda n: sem(tag + n)
        w_raw = sb("w_raw", [P, KD, P])
        w_hi = [sb(f"w_hi{i}", [P, KD, P], F32R) for i in range(2)]
        w_lo = [sb(f"w_lo{i}", [P, KD, P], F32R) for i in range(2)]
        out = [sb(f"out{i}", [P, TC]) for i in range(2)]
        split_hi = [sb(f"split_hi{i}", [P, TC], F32R) for i in range(2)]
        split_lo = [sb(f"split_lo{i}", [P, TC], F32R) for i in range(2)]
        acc = [ctx.enter_context(nc.psum_tensor(f"{tag}acc{i}", [P, TC], F32)) for i in range(2)]
        w_loaded, w_hi_done, w_lo_done, acc_done = s_("w_loaded"), s_("w_hi_done"), s_("w_lo_done"), s_("acc_done")
        act_out, dve_in, dve_out = s_("act_out"), s_("dve_in"), s_("dve_out")
        stored = [s_(f"stored{i}") for i in range(2)]
        stored_lo = [s_(f"stored_lo{i}") for i in range(2)]
        hT_hi, hT_lo = g["hT_hi"], g["hT_lo"]
        block = ctx.enter_context(nc.Block())

        plan, n0, a0, v0 = [], 0, 0, 0
        for cb, blocks, func, then in runs:
            plan.append((cb, blocks, func, then, n0, a0, v0))
            n0 += blocks
            if then is None:
                a0 += NTC * blocks
            else:
                v0 += NTC * blocks
        TOTAL = n0

        def each_run(eng, body):
            for r, run in enumerate(plan):
                with eng.Fori(0, run[1] // 2) as i:
                    body(run, i)

        @block.sync
        def _(sp):
            def load(cb, n):
                sp.wait_ge(w_lo_done, n)
                sp.dma_start(w_raw[:], w_in[0, :, bass.ds(cb * P, P)].rearrange("(k p) n -> p k n", p=P)
                             ).then_inc(w_loaded, 16)

            load(plan[0][0], 0)
            for r, (cb, blocks, func, then, n0, a0, v0) in enumerate(plan):
                def stores(i, u):
                    for tc in range(NTC):
                        q = 2 * NTC * i + NTC * u + tc
                        s = tc % 2
                        if then is None:
                            sp.wait_ge(act_out, a0 + q + 1)
                        else:
                            sp.wait_ge(dve_out, v0 + q + 1)
                        rows = scr["proj"][bass.ds((cb + 2 * i + u) * P, P), tc * TC:(tc + 1) * TC]
                        if then == "split":
                            sp.dma_start(rows, split_hi[s][:].bitcast(F32)).then_inc(stored[s], 16)
                            sp.dma_start(scr["proj_lo"][bass.ds((cb + 2 * i + u) * P, P), tc * TC:(tc + 1) * TC],
                                         split_lo[s][:].bitcast(F32)).then_inc(stored_lo[s], 16)
                        else:
                            sp.dma_start(rows, out[s][:]).then_inc(stored[s], 16)

                def pair(i, more):
                    load(cb + 2 * i + 1, n0 + 2 * i + 1)
                    stores(i, 0)
                    if more == "same":
                        load(cb + 2 * i + 2, n0 + 2 * i + 2)
                    elif more is not None:
                        load(more, n0 + 2 * i + 2)
                    stores(i, 1)

                if blocks > 2:
                    with sp.Fori(0, blocks // 2 - 1) as i:
                        pair(i, "same")
                pair(blocks // 2 - 1, plan[r + 1][0] if r + 1 < len(plan) else None)
            n_lo = sum(b for _, b, _, then in runs if then == "split")
            for s in range(2):
                sp.wait_ge(stored[s], 16 * TOTAL * NTC // 2)
                if n_lo:
                    sp.wait_ge(stored_lo[s], 16 * n_lo * NTC // 2)

        @block.tensor
        def _(pe):
            free = {None: act_out, "gate": dve_out, "split": dve_out}
            for r, (cb, blocks, func, then, n0, a0, v0) in enumerate(plan):
                if r:
                    pe.wait_ge(free[plan[r - 1][3]], a0 if plan[r - 1][3] is None else v0)
                base = a0 if then is None else v0

                def blocks2(i, peeled=False):
                    for u in range(2):
                        pe.wait_ge(w_lo_done, n0 + 2 * i + u + 1)
                        for tc in range(NTC):
                            q = 2 * NTC * i + NTC * u + tc
                            if not (peeled and u == 0 and tc < 2):
                                pe.wait_ge(free[then], base + q - 1)
                            tok = slice(tc * TC, (tc + 1) * TC)
                            for k in range(KD):
                                nc.tensor.matmul(acc[tc % 2][:], w_hi[u][:, k, :], hT_hi[:, k, tok], start=k == 0, stop=False)
                                nc.tensor.matmul(acc[tc % 2][:], w_hi[u][:, k, :], hT_lo[:, k, tok], start=False, stop=False)
                                mm = nc.tensor.matmul(acc[tc % 2][:], w_lo[u][:, k, :], hT_hi[:, k, tok],
                                                      start=False, stop=k == KD - 1)
                            mm.then_inc(acc_done, 1)

                blocks2(0, peeled=True)
                if blocks > 2:
                    with pe.Fori(1, blocks // 2) as i:
                        blocks2(i)

        @block.gpsimd
        def _(pool):
            with pool.Fori(0, TOTAL // 2) as i:
                for u in range(2):
                    pool.wait_ge(w_hi_done, 2 * i + u + 1)
                    nc.gpsimd.tensor_tensor(w_lo[u][:], w_raw[:], w_hi[u][:].bitcast(F32), ALU.subtract
                                            ).then_inc(w_lo_done, 1)

        @block.scalar
        def _(act):
            def split_weights(n, u):
                act.wait_ge(w_loaded, 16 * (n + 1))
                after(act, acc_done, NTC * (n - 1))
                nc.scalar.activation(w_hi[u][:], w_raw[:], ACT.Copy).then_inc(w_hi_done, 1)

            split_weights(0, 0)
            split_weights(1, 1)
            for r, (cb, blocks, func, then, n0, a0, v0) in enumerate(plan):
                def pair(i, more):
                    for u in range(2):
                        for tc in range(NTC):
                            m = NTC * (n0 + 2 * i + u) + tc
                            q = 2 * NTC * i + NTC * u + tc
                            s = tc % 2
                            act.wait_ge(acc_done, m + 1)
                            after(act, stored[s], 16 * ((NTC // 2) * (n0 + 2 * i + u) + tc // 2))
                            to = split_hi if then == "split" else out
                            ins = nc.scalar.activation(to[s][:], acc[s][:], FUNCS[func])
                            ins.then_inc(act_out if then is None else dve_in, 1)
                        if more:
                            split_weights(n0 + 2 * i + u + 2, u)

                first = 0
                if n0 == 0:
                    pair(0, TOTAL > 2)
                    first = 1
                last = blocks // 2 - 1
                if last > first:
                    with act.Fori(first, last) as i:
                        pair(i, True)
                if last >= first:
                    pair(last, r + 1 < len(plan))

        @block.vector
        def _(dve):
            lo_base = 0
            for r, (cb, blocks, func, then, n0, a0, v0) in enumerate(plan):
                if then is None:
                    continue

                def pair(i):
                    for u in range(2):
                        for tc in range(NTC):
                            q = 2 * NTC * i + NTC * u + tc
                            s = tc % 2
                            dve.wait_ge(dve_in, v0 + q + 1)
                            if then == "split":
                                after(dve, stored_lo[s], 16 * ((NTC // 2) * (lo_base + 2 * i + u) + tc // 2))
                                nc.vector.tensor_tensor(split_lo[s][:], acc[s][:], split_hi[s][:].bitcast(F32),
                                                        ALU.subtract).then_inc(dve_out, 1)
                            else:
                                nc.vector.tensor_tensor(out[s][:], acc[s][:], out[s][:], ALU.mult).then_inc(dve_out, 1)

                if v0 == 0:
                    pair(0)
                    if blocks > 2:
                        with dve.Fori(1, blocks // 2) as i:
                            pair(i)
                else:
                    with dve.Fori(0, blocks // 2) as i:
                        pair(i)
                if then == "split":
                    lo_base += blocks



LEAD = 8


def reached(eng, sem, count):
    if isinstance(count, int) and count <= 0:
        return
    eng.wait_ge(sem, count + LEAD)


def arrived(eng, sem, count, each=16):
    eng.wait_ge(sem, (count + 1) * each)


class WovenColumns:
    PARTS = 4
    KP = KD // PARTS
    ALL = NTC * PARTS

    def __init__(self, nc, ctx, sem, g, w_in, scr, tag, split):
        sb = lambda n, s, d=F32: ctx.enter_context(nc.sbuf_tensor(tag + n, s, d))
        s_ = lambda n: sem(tag + n)
        self.nc, self.w_in, self.scr = nc, w_in, scr
        self.hT_hi, self.hT_lo = g["hT_hi"], g["hT_lo"]
        self.w_raw = sb("w_raw", [P, KD, P])
        self.w_hi = sb("w_hi", [P, KD, P], F32R)
        self.w_lo = sb("w_lo", [P, KD, P], F32R)
        self.out = [sb(f"out{i}", [P, TC], F32R if split else F32) for i in range(2)]
        self.acc = [ctx.enter_context(nc.psum_tensor(f"{tag}acc{i}", [P, TC], F32)) for i in range(2)]
        self.w_loaded, self.w_hi_done, self.w_lo_done = s_("w_loaded"), s_("w_hi_done"), s_("w_lo_done")
        self.part_done, self.taken = s_("part_done"), s_("taken")
        self.stored = [s_(f"stored{i}") for i in range(2)]
        if split:
            self.out_lo = [sb(f"out_lo{i}", [P, TC], F32R) for i in range(2)]
            self.low_taken = s_("low_taken")
            self.low_stored = [s_(f"low_stored{i}") for i in range(2)]

    def load(self, sp, n, col):
        reached(sp, self.w_lo_done, self.PARTS * n)
        sp.dma_start(self.w_raw[:], self.w_in[0, :, bass.ds(col, P)].rearrange("(k p) n -> p k n", p=P)
                     ).then_inc(self.w_loaded, 16)

    def split_high(self, act, n, part):
        if part == 0:
            act.wait_ge(self.w_loaded, 16 * (n + 1))
        reached(act, self.part_done, self.ALL * n - self.PARTS + part + 1 if not (isinstance(n, int) and n == 0) else 0)
        k = slice(part * self.KP, (part + 1) * self.KP)
        self.nc.scalar.activation(self.w_hi[:, k, :], self.w_raw[:, k, :], ACT.Copy).then_inc(self.w_hi_done, 1)

    def split_low(self, pool, n, part):
        reached(pool, self.w_hi_done, self.PARTS * n + part + 1)
        k = slice(part * self.KP, (part + 1) * self.KP)
        self.nc.gpsimd.tensor_tensor(self.w_lo[:, k, :], self.w_raw[:, k, :], self.w_hi[:, k, :].bitcast(F32),
                                     ALU.subtract).then_inc(self.w_lo_done, 1)

    def multiply(self, pe, n, tc, part, low=False):
        if tc == 0:
            reached(pe, self.w_lo_done, self.PARTS * n + part + 1)
        if part == 0:
            reached(pe, self.low_taken if low else self.taken, NTC * n + tc - 1)
        tok, bank = slice(tc * TC, (tc + 1) * TC), self.acc[tc % 2]
        for k in range(part * self.KP, (part + 1) * self.KP):
            self.nc.tensor.matmul(bank[:], self.w_hi[:, k, :], self.hT_hi[:, k, tok], start=k == 0, stop=False)
            self.nc.tensor.matmul(bank[:], self.w_hi[:, k, :], self.hT_lo[:, k, tok], start=False, stop=False)
            mm = self.nc.tensor.matmul(bank[:], self.w_lo[:, k, :], self.hT_hi[:, k, tok], start=False, stop=k == KD - 1)
        mm.then_inc(self.part_done, 1)

    def take(self, act, n, tc, func, rounded=False):
        reached(act, self.part_done, self.ALL * n + self.PARTS * (tc + 1))
        arrived(act, self.stored[tc % 2], 2 * n + tc // 2)
        out = self.out[tc % 2][:]
        self.nc.scalar.activation(out if rounded or out.dtype == F32 else out.bitcast(F32), self.acc[tc % 2][:], func
                                  ).then_inc(self.taken, 1)

    def take_low(self, dve, n, tc):
        s = tc % 2
        reached(dve, self.taken, NTC * n + tc + 1)
        arrived(dve, self.low_stored[s], 2 * n + tc // 2)
        self.nc.vector.tensor_tensor(self.out_lo[s][:], self.acc[s][:], self.out[s][:].bitcast(F32), ALU.subtract
                                     ).then_inc(self.low_taken, 1)

    def store(self, sp, n, tc, cb):
        reached(sp, self.taken, NTC * n + tc + 1)
        out = self.out[tc % 2][:]
        sp.dma_start(self.scr["proj"][bass.ds(cb * P, P), tc * TC:(tc + 1) * TC],
                     out if out.dtype == F32 else out.bitcast(F32)).then_inc(self.stored[tc % 2], 16)

    def store_low(self, sp, n, tc, cb):
        reached(sp, self.low_taken, NTC * n + tc + 1)
        sp.dma_start(self.scr["proj_lo"][bass.ds(cb * P, P), tc * TC:(tc + 1) * TC],
                     self.out_lo[tc % 2][:].bitcast(F32)).then_inc(self.low_stored[tc % 2], 16)


UNITS = [(g, j, b, TC if j < g else (b + 1) * P) for g in range(NTC) for j in range(g, -1, -1) for b in range(4)]
NU = len(UNITS)
STEPS = [(g, j) for g in range(NTC) for j in range(g, -1, -1)]
NS = len(STEPS)
LAG = 2
HITS = 3


def attention_and_gates(nc, sem, g_, w_in, scr):
    with ExitStack() as ctx:
        sb = lambda n, s, d=F32: ctx.enter_context(nc.sbuf_tensor("a_" + n, s, d))
        ps = lambda n, s: ctx.enter_context(nc.psum_tensor("a_" + n, s, F32))
        s_ = lambda n: sem("a_" + n)
        NB = 3 * KD // HEADS
        SLOTS = NB * WovenColumns.ALL
        k_hl = sb("k_hl", [P, T], F32R)
        v_hl = sb("v_hl", [P, T // P, P], F32R)
        q_hl = [sb(f"q_hl{i}", [P, TC], F32R) for i in range(2)]
        q_lh = [sb(f"q_lh{i}", [P, TC], F32R) for i in range(2)]
        miss = [sb(f"miss{i}", [P, TC]) for i in range(2)]
        hit = [sb(f"hit{i}", [P, TC]) for i in range(HITS)]
        left_all = sb("left", [P, 4, TC + 1])
        left = [left_all[:, i, :] for i in range(4)]
        aT_hi = sb("aT_hi", [P, 4, TC], F32R)
        aT_lo = sb("aT_lo", [P, 4, TC], F32R)
        o_hl = sb("o_hl", [P, TC])
        gate = sb("gate", [DH, TC])
        keep, skip = sb("keep", [P, P]), sb("skip", [P, P])
        fold = sb("fold", [P, DH])
        z_ps = [ps(f"z{i}", [P, TC]) for i in range(2)]
        t_ps = [ps(f"t{i}", [P, 4, P]) for i in range(2)]
        o_ps = [ps(f"o{i}", [P, TC]) for i in range(2)]
        gates = WovenColumns(nc, ctx, sem, g_, w_in, scr, "ag_", split=False)
        k_loaded = [s_(f"k_loaded{c}") for c in range(4)]
        v_loaded = [s_(f"v_loaded{c}") for c in range(4)]
        q_loaded = [s_(f"q_loaded{i}") for i in range(2)]
        gate_loaded, y_stored = s_("gate_loaded"), s_("y_stored")
        z_done, sig_done, masked, carried, scanned = s_("z_done"), s_("sig_done"), s_("masked"), s_("carried"), s_("scanned")
        a_done, turned, hi_done, lo_done = s_("a_done"), s_("turned"), s_("hi_done"), s_("lo_done")
        masks_made = s_("masks_made")
        av_done, o_copied, folded, y_done, set_up = s_("av_done"), s_("o_copied"), s_("folded"), s_("y_done"), s_("set_up")
        ident = g_["ident"]
        block = ctx.enter_context(nc.Block())

        def units_until(g):
            return 4 * sum(range(1, g + 1))

        def last_slot(g):
            return units_until(g + 1) - 1 + LAG

        @block.sync
        def _(sp):
            sp.sem_inc(y_stored, 16)
            for s in gates.stored:
                sp.sem_inc(s, 16)

            def load_k(h, c):
                reached(sp, z_done, NU * (h - 1) + 4 * (STEPS.index((NTC - 1, c)) + 1))
                cols, krow = slice(c * TC, (c + 1) * TC), bass.ds(W + h * DH, DH)
                sp.dma_start(k_hl[0:DH, cols].bitcast(F32), scr["proj"][krow, cols]).then_inc(k_loaded[c], 16)
                sp.dma_start(k_hl[DH:P, cols].bitcast(F32), scr["proj_lo"][krow, cols]).then_inc(k_loaded[c], 16)

            def load_v(h, c):
                reached(sp, av_done, NS * (h - 1) + STEPS.index((NTC - 1, c)) + 1)
                cols, rows = slice(c * TC, (c + 1) * TC), bass.ds(h * DH, DH)
                for half, v in ((slice(0, DH), "v_hi"), (slice(DH, P), "v_lo")):
                    sp.dma_start(v_hl[:, 4 * c:4 * c + 4, half].bitcast(F32),
                                 scr[v][cols, rows].rearrange("(b p) d -> p b d", p=P)).then_inc(v_loaded[c], 16)

            def load_q(h, g):
                cols, rows = slice(g * TC, (g + 1) * TC), bass.ds(h * DH, DH)
                reached(sp, z_done, NU * h + units_until(g - 1) if g >= 2 else NU * (h - 1) + units_until(g + 3))
                for tile, first, second in ((q_lh, "proj_lo", "proj"), (q_hl, "proj", "proj_lo")):
                    sp.dma_start(tile[g % 2][0:DH, :].bitcast(F32), scr[first][rows, cols]).then_inc(q_loaded[g % 2], 16)
                    sp.dma_start(tile[g % 2][DH:P, :].bitcast(F32), scr[second][rows, cols]).then_inc(q_loaded[g % 2], 16)

            def load_gate(h, g):
                arrived(sp, y_stored, NTC * h + g)
                sp.dma_start(gate[:], scr["proj"][bass.ds(ZA * P + h * DH, DH), g * TC:(g + 1) * TC]
                             ).then_inc(gate_loaded, 16)

            def store_y(h, g):
                reached(sp, y_done, NTC * h + g + 1)
                sp.dma_start(scr["y"][0, bass.ds(h * DH, DH), g * TC:(g + 1) * TC], gate[:]).then_inc(y_stored, 16)

            load_k(0, 0)
            load_q(0, 0)
            gates.load(sp, 0, GA * P)
            load_v(0, 0)
            load_q(0, 1)
            for c in range(1, 4):
                load_k(0, c)
                load_v(0, c)

            def head(h, more):
                for n in range(SLOTS + 2):
                    if n % WovenColumns.ALL == 2 and n < SLOTS and (more or n < SLOTS - WovenColumns.ALL):
                        b = NB * h + n // WovenColumns.ALL + 1
                        gates.load(sp, b, (GA + b) * P)
                    if n % 4 == 1 and n >= 5:
                        m = (n - 5) // 4
                        b = NB * h + m // NTC
                        gates.store(sp, b, m % NTC, GA + b)
                    if n == 0:
                        load_gate(h, 0)
                    for g in range(NTC):
                        if n == last_slot(g) + 5 or (n == SLOTS + 1 and last_slot(g) + 5 > n):
                            store_y(h, g)
                            if g + 1 < NTC:
                                load_gate(h, g + 1)
                    for g in (2, 3):
                        if n == units_until(g - 1) + 1:
                            load_q(h, g)
                    if more:
                        for g in (0, 1):
                            if n == units_until(g + 3) + 1:
                                load_q(h + 1, g)
                        for c in range(4):
                            step = STEPS.index((NTC - 1, c))
                            if n == 4 * (step + 1) + 1:
                                load_k(h + 1, c)
                            if n == 4 * (step + 1) + LAG + 2:
                                load_v(h + 1, c)

            with sp.Fori(0, HEADS - 1) as h:
                head(h, True)
            head(HEADS - 1, False)
            arrived(sp, y_stored, NTC * HEADS)
            for s in gates.stored:
                arrived(sp, s, 2 * NB * HEADS)

        @block.tensor
        def _(pe):
            for s in (z_done, turned, av_done, folded, gates.part_done):
                pe.sem_inc(s, LEAD)

            def scores(h, u):
                g, j, b, width = UNITS[u]
                if b == 0 and j == g:
                    pe.wait_ge(q_loaded[g % 2], (2 * h + g // 2 + 1) * 64)
                    pe.wait_ge(k_loaded[g], (h + 1) * 32)
                reached(pe, sig_done, NU * h + u - 1)
                for q, first in ((q_hl, True), (q_lh, False)):
                    mm = nc.tensor.matmul(z_ps[u % 2][:, 0:width], q[g % 2][:, b * P:(b + 1) * P],
                                          k_hl[:, j * TC:j * TC + width], start=first, stop=not first)
                mm.then_inc(z_done, 1)

            def turn(h, u):
                width = UNITS[u][3]
                reached(pe, a_done, NU * h + u + 1)
                reached(pe, lo_done, NU * h + u - 1)
                for k in range(width // P):
                    mm = nc.tensor.transpose(t_ps[u % 2][:, k, :], hit[u % HITS][:, k * P:(k + 1) * P], ident[:])
                mm.then_inc(turned, 1)

            def weighted_values(h, s):
                g, j = STEPS[s]
                reached(pe, lo_done, NU * h + 4 * (s + 1))
                if j == g:
                    pe.wait_ge(v_loaded[g], (h + 1) * 32)
                    reached(pe, y_done, NTC * h + g - 1)
                for k in range(4):
                    c0 = k * P if j == g else 0
                    for part in (aT_hi, aT_lo):
                        mm = nc.tensor.matmul(o_ps[g % 2][:, c0:TC], v_hl[:, 4 * j + k, :], part[:, k, c0:TC],
                                              start=j == g and k == 0 and part is aT_hi,
                                              stop=j == 0 and k == 3 and part is aT_lo)
                mm.then_inc(av_done, 1)

            def fold_parts(h, g):
                reached(pe, o_copied, NTC * h + g + 1)
                nc.tensor.matmul(o_ps[g % 2][0:DH, :], fold[:], o_hl[:], start=True, stop=True).then_inc(folded, 1)

            pe.wait_ge(set_up, 5)
            with pe.Fori(0, HEADS) as h:
                for n in range(SLOTS):
                    if n < NU:
                        scores(h, n)
                    gates.multiply(pe, NB * h + n // WovenColumns.ALL, n // 4 % NTC, n % 4)
                    if 0 <= n - LAG < NU:
                        turn(h, n - LAG)
                    v = n - LAG - 1
                    if 0 <= v < NU and v % 4 == 3:
                        weighted_values(h, v // 4)
                    for g in range(NTC):
                        if n == last_slot(g) + 3:
                            fold_parts(h, g)

        @block.scalar
        def _(act):
            for s in (sig_done, hi_done, o_copied, gates.w_hi_done, gates.taken):
                act.sem_inc(s, LEAD)

            def sigmoids(h, u):
                width = UNITS[u][3]
                reached(act, z_done, NU * h + u + 1)
                reached(act, scanned, NU * h + u - 1)
                nc.scalar.activation(miss[u % 2][:, 0:width], z_ps[u % 2][:, 0:width], ACT.Sigmoid, scale=-SCALE)
                reached(act, turned, NU * h + (u - HITS + 1 if u >= HITS else 0))
                nc.scalar.activation(hit[u % HITS][:, 0:width], z_ps[u % 2][:, 0:width], ACT.Sigmoid, scale=SCALE
                                     ).then_inc(sig_done, 1)

            def high(h, u):
                b, width = UNITS[u][2:]
                n = width // P
                reached(act, turned, NU * h + u + 1)
                reached(act, av_done, NS * h + u // 4)
                nc.scalar.activation(aT_hi[:, 0:n, b * P:(b + 1) * P], t_ps[u % 2][:, 0:n, :], ACT.Copy).then_inc(hi_done, 1)

            def copy_o(h, g):
                s = STEPS.index((g, 0))
                reached(act, av_done, NS * h + s + 1)
                reached(act, folded, NTC * h + g)
                nc.scalar.activation(o_hl[:], o_ps[g % 2][:], ACT.Copy).then_inc(o_copied, 1)

            def split(n, part):
                gates.split_high(act, n, part)

            for part in range(4):
                split(0, part)

            def head(h, more):
                for n in range(SLOTS + 1):
                    if n < NU:
                        sigmoids(h, n)
                    if n % 4 == 0 and n >= 4:
                        m = n // 4 - 1
                        gates.take(act, NB * h + m // NTC, m % NTC, ACT.Sigmoid)
                    r = (n - 1) % WovenColumns.ALL - 12
                    if n > 12 and r >= 0 and (more or n < SLOTS - 4):
                        split(NB * h + (n - 1) // WovenColumns.ALL + 1, r)
                    if 0 <= n - LAG < NU:
                        high(h, n - LAG)
                    for g in range(NTC):
                        if n == last_slot(g) + 2:
                            copy_o(h, g)

            with act.Fori(0, HEADS - 1) as h:
                head(h, True)
            head(HEADS - 1, False)

        @block.vector
        def _(dve):
            for s in (masked, carried, scanned, lo_done, y_done):
                dve.sem_inc(s, LEAD)
            nc.vector.tensor_tensor(fold[:], ident[:, 0:DH], ident[:, DH:P], ALU.add).then_inc(set_up, 1)
            for b in range(4):
                nc.vector.memset(left[b], 1.0).then_inc(set_up, 1)
            dve.wait_ge(set_up, 5)
            dve.wait_ge(masks_made, 4)

            diagonals = [u for u in range(NU) if UNITS[u][0] == UNITS[u][1]]
            inner = [u for u in range(NU) if u not in diagonals]

            def scan(h, u):
                g, j, b, width = UNITS[u]
                hit_u = hit[u % HITS]
                if j == g:
                    start = 1.0
                    reached(dve, sig_done, NU * h + u + 1)
                    last = slice(width - P, width)
                    nc.vector.tensor_tensor(miss[u % 2][:, last], miss[u % 2][:, last], skip[:], ALU.max).then_inc(masked, 1)
                    nc.vector.tensor_tensor(hit_u[:, last], hit_u[:, last], keep[:], ALU.mult).then_inc(masked, 1)
                    reached(dve, masked, 2 * (len(diagonals) * h + diagonals.index(u) + 1))
                    reached(dve, a_done, NU * h + u - 3)
                else:
                    start = left[b][:, TC:TC + 1]
                    reached(dve, a_done, NU * h + u - 3)
                    nc.vector.tensor_copy(left[b][:, TC:TC + 1], left[b][:, 0:1]).then_inc(carried, 1)
                    reached(dve, sig_done, NU * h + u + 1)
                    reached(dve, carried, len(inner) * h + inner.index(u) + 1)
                nc.vector.tensor_tensor_scan(left[b][:, 0:width][:, ::-1], miss[u % 2][:, 0:width][:, ::-1],
                                             miss[u % 2][:, 0:width][:, ::-1], start, ALU.mult, ALU.bypass
                                             ).then_inc(scanned, 1)

            def low(h, u):
                b, width = UNITS[u][2:]
                n = width // P
                reached(dve, hi_done, NU * h + u + 1)
                cols = slice(b * P, (b + 1) * P)
                nc.vector.tensor_tensor(aT_lo[:, 0:n, cols], t_ps[u % 2][:, 0:n, :], aT_hi[:, 0:n, cols].bitcast(F32),
                                        ALU.subtract).then_inc(lo_done, 1)

            def gated(h, g):
                reached(dve, folded, NTC * h + g + 1)
                dve.wait_ge(gate_loaded, (NTC * h + g + 1) * 16)
                nc.vector.tensor_tensor(gate[:], o_ps[g % 2][0:DH, :], gate[:], ALU.mult).then_inc(y_done, 1)

            with dve.Fori(0, HEADS) as h:
                for n in range(SLOTS):
                    if n < NU:
                        scan(h, n)
                    if 0 <= n - LAG < NU:
                        low(h, n - LAG)
                    for g in range(NTC):
                        if n == last_slot(g) + 4:
                            gated(h, g)

        @block.gpsimd
        def _(pool):
            for s in (a_done, gates.w_lo_done):
                pool.sem_inc(s, LEAD)
            nc.gpsimd.memset(keep[:], 1.0).then_inc(masks_made, 1)
            nc.gpsimd.memset(skip[:], 0.0).then_inc(masks_made, 1)
            pool.wait_ge(masks_made, 2)
            for tile, fill in ((keep, 0.0), (skip, 1.0)):
                nc.gpsimd.affine_select(out=tile[:], in_=tile[:], compare_op=ALU.is_gt, fill=fill, base=0,
                                        pattern=[[-1, P]], channel_multiplier=1).then_inc(masks_made, 1)

            def weights(h, u):
                b, width = UNITS[u][2:]
                reached(pool, scanned, NU * h + u + 1)
                nc.gpsimd.tensor_tensor(hit[u % HITS][:, 0:width], hit[u % HITS][:, 0:width], left[b][:, 1:width + 1],
                                        ALU.mult).then_inc(a_done, 1)

            for part in range(4):
                gates.split_low(pool, 0, part)

            def head(h, more):
                for n in range(SLOTS + 1):
                    if n < NU:
                        weights(h, n)
                    r = (n - 1) % WovenColumns.ALL - 12
                    if n > 12 and r >= 0 and (more or n < SLOTS - 4):
                        gates.split_low(pool, NB * h + (n - 1) // WovenColumns.ALL + 1, r)

            with pool.Fori(0, HEADS - 1) as h:
                head(h, True)
            head(HEADS - 1, False)


HH = 2
PAIRS = W // P // HH
C = P
NCH = T // C
NCU = NCH * PAIRS
LEVELS = [1 << n for n in range(7)]


def hgrn2_and_columns(nc, sem, g_, w_in, scr, lower_bounds, hgrn_norm_w):
    with ExitStack() as ctx:
        sb = lambda n, s, d=F32: ctx.enter_context(nc.sbuf_tensor("h_" + n, s, d))
        ps = lambda n, s: ctx.enter_context(nc.psum_tensor("h_" + n, s, F32))
        s_ = lambda n: sem("h_" + n)
        NL = len(LEVELS)
        NIN = 2 * NL + 3
        q = [sb(f"q{i}", [P, HH, C]) for i in range(2)]
        pre = [sb(f"pre{i}", [P, HH, C]) for i in range(2)]
        suf = [sb(f"suf{i}", [P, HH, C]) for i in range(2)]
        k = [sb(f"k{i}", [P, HH, C]) for i in range(2)]
        gate = [sb(f"gate{i}", [P, HH, C]) for i in range(2)]
        v = [sb(f"v{i}", [P, HH, C]) for i in range(2)]
        k_left = [sb(f"k_left{n}", [P, HH, C]) for n in range(NL)]
        q_right = [sb(f"q_right{n}", [P, HH * C // 2]) for n in range(NL)]
        part = [sb(f"part{i}", [P, HH, C // 2]) for i in range(2)]
        scores = [sb(f"scores{i}", [P, HH, C]) for i in range(2)]
        q_pre = [sb(f"q_pre{i}", [P, HH, C]) for i in range(2)]
        k_end = sb("k_end", [P, HH, C])
        kT = [sb(f"kT{i}", [P, HH, C]) for i in range(2)]
        state_all = sb("state", [P, PAIRS, HH, C])
        state = [state_all[:, i] for i in range(PAIRS)]
        tot = [sb(f"tot{i}", [P, HH]) for i in range(2)]
        sq = sb("sq", [P, HH, C])
        root = sb("root", [P, HH, C])
        inv = sb("inv", [P, HH, C])
        cols = WovenColumns(nc, ctx, sem, g_, w_in, scr, "hc_", split=True)
        y = [sb(f"y{i}", [P, HH, C]) for i in range(2)]
        mask = [sb(f"mask{n}", [P, C // 2]) for n in range(NL)]
        ones = sb("ones", [P, P])
        eps = sb("eps", [P, 1])
        norm_w = sb("norm_w", [P, 1])
        lb = sb("lb", [P, 6, PAIRS * HH])
        s_ps = [ps(f"s{i}", [P, HH, C]) for i in range(4)]
        kT_ps = ps("kT", [P, HH, C])
        st_ps = ms_ps = kT_ps
        o_ps = ps("o", [P, HH, C])
        par_loaded, set_up, masks_done, lb_done = s_("par_loaded"), s_("set_up"), s_("masks_done"), s_("lb_done")
        front_loaded = [s_(f"front_loaded{i}") for i in range(2)]
        tail_loaded = [s_(f"tail_loaded{i}") for i in range(2)]
        stored = [s_(f"stored{i}") for i in range(2)]
        prep, prepared, level_in, joined = s_("prep"), s_("prepared"), s_("level_in"), s_("joined")
        s_done, parted, added, kT_turned, kT_done = s_("s_done"), s_("parted"), s_("added"), s_("kT_turned"), s_("kT_done")
        st_done, o_done, state_done, sq_done = s_("st_done"), s_("o_done"), s_("state_done"), s_("sq_done")
        ms_done, root_done, inv_done, gated, y_done = s_("ms_done"), s_("root_done"), s_("inv_done"), s_("gated"), s_("y_done")
        ident = g_["ident"]
        block = ctx.enter_context(nc.Block())

        def halves(tile, H):
            return tile[:].rearrange("p h (n two x) -> p (h n) two x", two=2, x=H)

        N_SPLIT = 2 * WB

        def chunks(front, last, eng):
            front(0, 0, None, True, None)
            with eng.Fori(0, N_SPLIT) as i:
                front(i, 1, i, True, (i, 0))
                front(i + 1, 0, i, True, (i, 1))
            with eng.Fori(N_SPLIT, NCH - 1) as i:
                front(i, 1, i, False, (i, 0))
                front(i + 1, 0, i, False, (i, 1))
            front(NCH - 1, 1, NCH - 1, False, (NCH - 1, 0))
            last(NCH - 1, 1, NCH - 1)

        @block.sync
        def _(sp):
            for s in (*stored, *cols.stored, *cols.low_stored):
                sp.sem_inc(s, 16)
            with nc.allow_non_contiguous_dma(reason="640 parameters, one to a partition"):
                sp.dma_start(norm_w[:], hgrn_norm_w.rearrange("a p -> p a")).then_inc(par_loaded, 16)
                sp.dma_start(lb[:, 0, :], lower_bounds.rearrange("a (h p) -> p (a h)", p=P)).then_inc(par_loaded, 16)

            def load_front(i, u):
                at = bass.ds(i * C, C)
                reached(sp, level_in, NIN * (2 * i + u - 1))
                for tile, cb in ((q, QB), (pre, FB)):
                    rows = slice((cb + u * HH) * P, (cb + (u + 1) * HH) * P)
                    sp.dma_start(tile[u][:], scr["proj"][rows, at].rearrange("(h p) t -> p h t", p=P)
                                 ).then_inc(front_loaded[u], 16)

            def load_tail(i, u):
                at = bass.ds(i * C, C)
                reached(sp, y_done, 2 * i + u - 1)
                rows = slice((ZB + u * HH) * P, (ZB + (u + 1) * HH) * P)
                sp.dma_start(gate[u][:], scr["proj"][rows, at].rearrange("(h p) t -> p h t", p=P)
                             ).then_inc(tail_loaded[u], 16)
                sp.dma_start(v[u][:], scr["i"][at, u * HH * P:(u + 1) * HH * P].rearrange("t (h d) -> t h d", h=HH)
                             ).then_inc(tail_loaded[u], 16)

            def store(i, u):
                reached(sp, y_done, 2 * i + u + 1)
                sp.dma_start(scr["y"][1, u * HH * P:(u + 1) * HH * P, bass.ds(i * C, C)].rearrange("(h p) t -> p h t", p=P),
                             y[u][:]).then_inc(stored[u], 16)

            def store_columns(i, tc, split):
                cb = QA + i if split else PRE - N_SPLIT + i
                cols.store(sp, i, tc, cb)
                if split:
                    cols.store_low(sp, i, tc, cb)

            load_front(0, 0)
            cols.load(sp, 0, QA * P)
            load_front(0, 1)
            load_tail(0, 0)
            load_tail(0, 1)
            load_front(1, 0)
            cols.load(sp, 1, (QA + 1) * P)

            def chunk(i, split, following):
                store_columns(i, 0, split)
                if following is not False:
                    load_front(i + 1, 1)
                store(i, 0)
                if following is not False:
                    load_tail(i + 1, 0)
                store_columns(i, 1, split)
                store_columns(i, 2, split)
                if following is not None and following is not False:
                    load_front(i + 2, 0)
                store(i, 1)
                if following is not False:
                    load_tail(i + 1, 1)
                if following is not None and following is not False:
                    cols.load(sp, i + 2, following)
                store_columns(i, 3, split)

            with sp.Fori(0, N_SPLIT - 2) as i:
                chunk(i, True, i * P + (QA + 2) * P)
            with sp.Fori(N_SPLIT - 2, N_SPLIT) as i:
                chunk(i, True, i * P + (PRE - N_SPLIT + 2) * P)
            with sp.Fori(N_SPLIT, NCH - 2) as i:
                chunk(i, False, i * P + (PRE - N_SPLIT + 2) * P)
            chunk(NCH - 2, False, None)
            chunk(NCH - 1, False, False)
            for s in stored:
                arrived(sp, s, NCH)
            for s in cols.stored:
                arrived(sp, s, 2 * NCH)
            for s in cols.low_stored:
                arrived(sp, s, 2 * N_SPLIT)

        @block.gpsimd
        def _(pool):
            for s in (prep, prepared, added, cols.w_lo_done):
                pool.sem_inc(s, LEAD)
            nc.gpsimd.memset(ones[:], 1.0).then_inc(set_up, 1)
            nc.gpsimd.memset(eps[:], RMS_EPS).then_inc(set_up, 1)
            nc.gpsimd.memset(state_all[:], 0.0).then_inc(set_up, 1)
            for n, H in enumerate(LEVELS):
                nc.gpsimd.memset(k_left[n][:], 0.0).then_inc(set_up, 1)
                nc.gpsimd.memset(mask[n][:], 1.0).then_inc(masks_done, 1)
            pool.wait_ge(masks_done, NL)
            for n, H in enumerate(LEVELS):
                m = mask[n][:].rearrange("p (b x) -> p b x", x=H)
                nc.gpsimd.affine_select(out=m, in_=m, compare_op=ALU.is_ge, fill=0.0, base=0,
                                        pattern=[[-2 * H, C // (2 * H)], [0, H]], channel_multiplier=1).then_inc(masks_done, 1)
                pool.wait_ge(masks_done, NL + 2 * n + 1)
                nc.gpsimd.affine_select(out=m, in_=m, compare_op=ALU.is_ge, fill=0.0, base=H - 1,
                                        pattern=[[2 * H, C // (2 * H)], [0, H]], channel_multiplier=-1).then_inc(masks_done, 1)
            pool.wait_ge(lb_done, 6)

            def prepare_at(i, u):
                c = 2 * i + u
                pool.wait_ge(front_loaded[u], (i + 1) * 32)
                reached(pool, level_in, NIN * (c - 1))
                reached(pool, s_done, (NL + 1) * (c - 2) + 1)
                heads = slice(u * HH, (u + 1) * HH)
                nc.gpsimd.tensor_tensor(pre[u][:], pre[u][:], lb[:, 5, heads].unsqueeze(2).to_broadcast([P, HH, C]), ALU.mult
                                        ).then_inc(prep, 1)
                reached(pool, prep, 2 * c + 1)
                nc.gpsimd.tensor_tensor(pre[u][:], pre[u][:], lb[:, 4, heads].unsqueeze(2).to_broadcast([P, HH, C]), ALU.add
                                        ).then_inc(prep, 1)
                reached(pool, prep, 2 * c + 2)
                nc.gpsimd.tensor_tensor(k[u][:], ones[:].unsqueeze(1).to_broadcast([P, HH, C]), pre[u][:], ALU.subtract
                                        ).then_inc(prepared, 1)
                nc.gpsimd.memset(suf[u][:], 1.0).then_inc(prepared, 1)

            def add_parts(i, u):
                c = 2 * i + u
                for n, H in enumerate(LEVELS):
                    reached(pool, parted, (NL + 1) * c + n + 2)
                    if n:
                        reached(pool, added, NL * c + n)
                    right = halves(scores[u], H)[:, :, 1, :]
                    nc.gpsimd.tensor_tensor(right, right, part[(n + u) % 2][:].rearrange("p h (b x) -> p (h b) x", x=H),
                                            ALU.add).then_inc(added, 1)

            def split_columns(n):
                for p in range(WovenColumns.PARTS):
                    cols.split_low(pool, n, p)

            prepare_at(0, 0)
            split_columns(0)
            prepare_at(0, 1)
            add_parts(0, 0)
            prepare_at(1, 0)
            add_parts(0, 1)
            with pool.Fori(1, NCH - 1) as i:
                prepare_at(i, 1)
                add_parts(i, 0)
                split_columns(i)
                prepare_at(i + 1, 0)
                add_parts(i, 1)
            prepare_at(NCH - 1, 1)
            add_parts(NCH - 1, 0)
            split_columns(NCH - 1)
            add_parts(NCH - 1, 1)

        @block.tensor
        def _(pe):
            for s in (s_done, kT_turned, st_done, o_done, ms_done, cols.part_done):
                pe.sem_inc(s, LEAD)
            pe.wait_ge(set_up, 3 + NL)

            def multiply(half, n, b, split):
                if b is not None:
                    r = 2 * WovenColumns.PARTS * half + n
                    cols.multiply(pe, b, r // 4, r % 4, low=split)

            def chunk_state(i, u):
                c = 2 * i + u
                pe.wait_ge(tail_loaded[u], (i + 1) * 32)
                reached(pe, kT_done, c + 1)
                for h in range(HH):
                    mm = nc.tensor.matmul(st_ps[:, h, :], kT[u][:, h, :], v[u][:, h, :], start=True, stop=True)
                mm.then_inc(st_done, 1)

            def outputs(i, u):
                c = 2 * i + u
                reached(pe, added, NL * (c + 1))
                reached(pe, state_done, HH * c)
                reached(pe, gated, c)
                for h in range(HH):
                    nc.tensor.matmul(o_ps[:, h, :], v[u][:, h, :], scores[u][:, h, :], start=True, stop=False)
                    mm = nc.tensor.matmul(o_ps[:, h, :], state[u][:, h, :], q_pre[u][:, h, :], start=False, stop=True)
                mm.then_inc(o_done, 1)

            def square_sums(i, u):
                c = 2 * i + u
                reached(pe, sq_done, c + 1)
                reached(pe, state_done, HH * (c + 1))
                nc.tensor.matmul(ms_ps[:], ones[:], sq[:], start=True, stop=True).then_inc(ms_done, 1)

            def front(i, u, b, split, before):
                c = 2 * i + u
                for n in range(NL + 1):
                    if n == 0:
                        reached(pe, prepared, 2 * (c + 1))
                    else:
                        reached(pe, level_in, NIN * c + 2 * n)
                    reached(pe, parted, (NL + 1) * c + n - 3)
                    for h in range(HH):
                        if n == 0:
                            mm = nc.tensor.matmul(s_ps[n % 4][:, h, :], k[u][:, h, :], q[u][:, h, :], start=True, stop=True)
                        else:
                            mm = nc.tensor.matmul(s_ps[n % 4][:, h, 0:C // 2], k_left[n - 1][:, h, :],
                                                  q_right[n - 1][:, h * C // 2:(h + 1) * C // 2], start=True, stop=True)
                    mm.then_inc(s_done, 1)
                    if before is not None:
                        if n == 1:
                            chunk_state(*before)
                        elif n == 2:
                            outputs(*before)
                        elif n == 6:
                            square_sums(*before)
                    multiply(1 - u, n, b, split)
                reached(pe, level_in, NIN * (c + 1))
                reached(pe, root_done, c)
                for h in range(HH):
                    mm = nc.tensor.transpose(kT_ps[:, h, :], k_end[:, h, :], ident[:])
                mm.then_inc(kT_turned, 1)

            def last(i, u, b):
                for n in range(NL + 1):
                    if n == 1:
                        chunk_state(i, u)
                    elif n == 2:
                        outputs(i, u)
                    elif n == 6:
                        square_sums(i, u)
                    multiply(1, n, b, False)

            chunks(front, last, pe)

        @block.scalar
        def _(act):
            for s in (kT_done, sq_done, root_done, cols.w_hi_done, cols.taken):
                act.sem_inc(s, LEAD)
            act.wait_ge(par_loaded, 32)
            act.wait_ge(lb_done, 1)
            nc.scalar.activation(lb[:, 1, :], lb[:, 2, :], ACT.Exp).then_inc(lb_done, 1)
            act.wait_ge(set_up, 3 + NL)

            def split_columns(n):
                for p in range(WovenColumns.PARTS):
                    cols.split_high(act, n, p)

            def square(i, u):
                c = 2 * i + u
                reached(act, o_done, c + 1)
                reached(act, ms_done, c)
                nc.scalar.activation(sq[:], o_ps[:], ACT.Square).then_inc(sq_done, 1)

            def take_root(i, u):
                c = 2 * i + u
                reached(act, ms_done, c + 1)
                reached(act, inv_done, c)
                nc.scalar.activation(root[:], ms_ps[:], ACT.Sqrt, scale=1.0 / C, bias=eps[:]).then_inc(root_done, 1)

            def woven(b, half, split, before, more):
                if before is not None:
                    square(*before)
                if b is not None:
                    cols.take(act, b, 2 * half, ACT.Copy, rounded=split)
                if before is not None:
                    take_root(*before)
                if b is not None:
                    if half == 1 and more:
                        split_columns(b + 1)
                    cols.take(act, b, 2 * half + 1, ACT.Copy, rounded=split)

            def front(i, u, b, split, before):
                c = 2 * i + u
                woven(b, 1 - u, split, before, True)
                reached(act, kT_turned, c + 1)
                reached(act, st_done, c - 1)
                nc.scalar.activation(kT[u][:], kT_ps[:], ACT.Copy).then_inc(kT_done, 1)

            def last(i, u, b):
                woven(b, 1, False, (i, u), False)

            split_columns(0)
            chunks(front, last, act)

        @block.vector
        def _(dve):
            for s in (level_in, joined, parted, state_done, inv_done, gated, y_done, cols.low_taken):
                dve.sem_inc(s, LEAD)
            dve.wait_ge(par_loaded, 32)
            nc.vector.tensor_tensor(lb[:, 2, :], lb[:, 0, :], lb[:, 0, :], ALU.subtract).then_inc(lb_done, 1)
            dve.wait_ge(lb_done, 2)
            nc.vector.reciprocal(lb[:, 3, :], lb[:, 1, :]).then_inc(lb_done, 1)
            dve.wait_ge(lb_done, 3)
            nc.vector.tensor_tensor(lb[:, 1, :], lb[:, 1, :], lb[:, 3, :], ALU.mult).then_inc(lb_done, 1)
            dve.wait_ge(lb_done, 4)
            nc.vector.tensor_tensor(lb[:, 4, :], lb[:, 1, :], lb[:, 1, :], ALU.subtract).then_inc(lb_done, 1)
            dve.wait_ge(lb_done, 5)
            nc.vector.tensor_scalar(lb[:, 5, :], lb[:, 4, :], -1.0, 1.0, ALU.mult, ALU.add).then_inc(lb_done, 1)
            dve.wait_ge(set_up, 3 + NL)
            dve.wait_ge(masks_done, 3 * NL)

            def take_part(c, u, n):
                reached(dve, s_done, (NL + 1) * c + n + 1)
                bank = s_ps[n % 4][:]
                if n == 0:
                    reached(dve, o_done, c - 1)
                    nc.vector.tensor_tensor(scores[u][:], bank, ident[:].unsqueeze(1).to_broadcast([P, HH, C]),
                                            ALU.mult).then_inc(parted, 1)
                else:
                    reached(dve, added, NL * c + n - 2)
                    nc.vector.tensor_tensor(part[(n - 1 + u) % 2][:], bank[:, :, 0:C // 2],
                                            mask[n - 1][:].unsqueeze(1).to_broadcast([P, HH, C // 2]),
                                            ALU.mult).then_inc(parted, 1)

            def update_state(i, u):
                c = 2 * i + u
                reached(dve, st_done, c + 1)
                reached(dve, o_done, c + 1)
                for h in range(HH):
                    nc.vector.scalar_tensor_tensor(state[u][:, h, :], state[u][:, h, :], tot[u][:, h:h + 1],
                                                   st_ps[:, h, :], ALU.mult, ALU.add).then_inc(state_done, 1)

            def weigh(i, u):
                c = 2 * i + u
                dve.wait_ge(tail_loaded[u], (i + 1) * 32)
                reached(dve, sq_done, c + 1)
                nc.vector.scalar_tensor_tensor(gate[u][:], o_ps[:], norm_w[:, 0:1], gate[u][:], ALU.mult, ALU.mult
                                               ).then_inc(gated, 1)

            def invert(i, u):
                c = 2 * i + u
                reached(dve, root_done, c + 1)
                reached(dve, y_done, c)
                nc.vector.reciprocal(inv[:], root[:]).then_inc(inv_done, 1)

            def normalise(i, u):
                c = 2 * i + u
                reached(dve, inv_done, c + 1)
                reached(dve, gated, c + 1)
                arrived(dve, stored[u], i)
                nc.vector.tensor_tensor(y[u][:], gate[u][:], inv[:], ALU.mult).then_inc(y_done, 1)

            def front(i, u, b, split, before):
                c = 2 * i + u
                reached(dve, prepared, 2 * (c + 1))
                reached(dve, s_done, (NL + 1) * c)
                for n, H in enumerate(LEVELS):
                    if n:
                        reached(dve, joined, 2 * NL * c + 2 * n)
                    kl, kk, ss, pp, qq = (halves(x, H) for x in (k_left[n], k[u], suf[u], pre[u], q[u]))
                    nc.vector.tensor_tensor(kl[:, :, 0, :], kk[:, :, 0, :], ss[:, :, 0, :], ALU.mult).then_inc(level_in, 1)
                    nc.vector.tensor_tensor(q_right[n][:].rearrange("p (b x) -> p b x", x=H), qq[:, :, 1, :], pp[:, :, 1, :],
                                            ALU.mult).then_inc(level_in, 1)
                    nb = HH * C // (2 * H)
                    nc.vector.tensor_tensor(ss[:, :, 0, :], ss[:, :, 0, :], pp[:, :, 1, H - 1:H].to_broadcast([P, nb, H]),
                                            ALU.mult).then_inc(joined, 1)
                    if n:
                        take_part(c, u, n - 1)
                    reached(dve, joined, 2 * NL * c + 2 * n + 1)
                    nc.vector.tensor_tensor(pp[:, :, 1, :], pp[:, :, 1, :], pp[:, :, 0, H - 1:H].to_broadcast([P, nb, H]),
                                            ALU.mult).then_inc(joined, 1)
                    if before is not None:
                        if n == 4:
                            update_state(*before)
                        elif n == 5:
                            weigh(*before)
                    if b is not None and split and n == 5:
                        cols.take_low(dve, b, 2 * (1 - u))
                reached(dve, joined, 2 * NL * (c + 1))
                reached(dve, kT_turned, c)
                nc.vector.tensor_tensor(k_end[:], k[u][:], suf[u][:], ALU.mult).then_inc(level_in, 1)
                reached(dve, o_done, c - 1)
                nc.vector.tensor_tensor(q_pre[u][:], q[u][:], pre[u][:], ALU.mult).then_inc(level_in, 1)
                nc.vector.tensor_copy(tot[u][:], pre[u][:, :, C - 1]).then_inc(level_in, 1)
                take_part(c, u, NL - 1)
                if before is not None:
                    invert(*before)
                take_part(c, u, NL)
                if before is not None:
                    normalise(*before)
                if b is not None and split:
                    cols.take_low(dve, b, 2 * (1 - u) + 1)

            def last(i, u, b):
                reached(dve, level_in, NIN * NCU)
                update_state(i, u)
                weigh(i, u)
                invert(i, u)
                normalise(i, u)

            chunks(front, last, dve)


def conv_and_merge(nc, sem, scr, conv_w, w_branch):
    with ExitStack() as ctx:
        sb = lambda n, s, d=F32: ctx.enter_context(nc.sbuf_tensor("m_" + n, s, d))
        s_ = lambda n: sem("m_" + n)
        NB, NM = 3, D // P
        w_raw = [sb(f"w_raw{i}", [P, D]) for i in range(2)]
        w_hi = sb("w_hi", [P, NB * WB, D], F32R)
        w_lo = sb("w_lo", [P, NB * WB, D], F32R)
        y_raw = sb("y_raw", [P, WB, TC])
        y_conv = sb("y_conv", [P, WB, TC])
        TAPS = 3
        pre, u_, post, z = (sb(n, [P, TC]) for n in ("pre", "u", "post", "z"))
        prod = sb("prod", [P, TAPS - 1 + TC])
        halo = sb("halo", [P, WB, TAPS - 1])
        taps = sb("taps", [P, TAPS, WB])
        y_hi = [sb(f"y_hi{b}", [P, WB, TC], F32R) for b in range(NB)]
        y_lo = [sb(f"y_lo{b}", [P, WB, TC], F32R) for b in range(NB)]
        gate = [sb(f"gate{i}", [P, TC]) for i in range(4)]
        total = sb("total", [P, NM, TC])
        acc = [ctx.enter_context(nc.psum_tensor(f"m_acc{i}", [P, TC], F32)) for i in range(4)]
        w_loaded = [s_(f"w_loaded{i}") for i in range(2)]
        w_hi_done, w_lo_done = s_("w_hi_done"), s_("w_lo_done")
        y_loaded, y_hi_done, y_lo_done = s_("y_loaded"), s_("y_hi_done"), s_("y_lo_done")
        g_loaded = [s_(f"g_loaded{i}") for i in range(4)]
        acc_done, gated, summed = s_("acc_done"), s_("gated"), s_("summed")
        halo_zero = s_("halo_zero")
        taps_loaded, conv_loaded, post_done, conv_step = s_("taps_loaded"), s_("conv_loaded"), s_("post_done"), s_("conv_step")
        CONV_STEPS = 7
        stored = s_("stored")
        block = ctx.enter_context(nc.Block())
        PER = NB * NM
        SUMS = (NB - 1) * NM

        @block.sync
        def _(sp):
            sp.sem_inc(stored, 16)

            def load_y(tc, b):
                reached(sp, y_lo_done, NB * tc + 1 if b else NB * tc - 1)
                sp.dma_start(y_raw[:], scr["y"][b, :, bass.ds(tc * TC, TC)].rearrange("(k p) t -> p k t", p=P)
                             ).then_inc(y_loaded, 16)

            def load_conv(tc, k):
                reached(sp, conv_step, CONV_STEPS * (WB * tc + k))
                for tile, cb in ((pre, PRE), (u_, UC), (post, POST), (z, ZC)):
                    sp.dma_start(tile[:], scr["proj"][(cb + k) * P:(cb + k + 1) * P, bass.ds(tc * TC, TC)]
                                 ).then_inc(conv_loaded, 16)

            def load_gates(tc, b, more):
                for m in range(NM):
                    if more and NM * b + m in (12, 16, 20):
                        load_conv(tc + 1, (NM * b + m - 12) // 4)
                    last = NM * b + m - 4
                    if 0 <= last < NM:
                        reached(sp, gated, PER * tc + last + 1)
                    else:
                        reached(sp, summed, SUMS * (tc if last > 0 else tc - 1) + (last % PER) - NM + 1)
                    sp.dma_start(gate[m % 4][:], scr["proj"][(GA + NM * b + m) * P:(GA + NM * b + m + 1) * P,
                                                             bass.ds(tc * TC, TC)]).then_inc(g_loaded[m % 4], 16)

            def load_w(k):
                if k >= 2:
                    reached(sp, w_lo_done, k - 1)
                sp.dma_start(w_raw[k % 2][:], w_branch[0, k // WB, (k % WB) * P:(k % WB + 1) * P, :]
                             ).then_inc(w_loaded[k % 2], 16)

            load_y(0, 0)
            for k in range(NB * WB):
                load_w(k)
                if k == 4:
                    load_y(0, 1)
                if k >= 4 and k % 2 == 0:
                    load_conv(0, (k - 4) // 2)
                if k == 1:
                    with nc.allow_non_contiguous_dma(reason="1536 taps, one to a partition"):
                        for n in range(TAPS):
                            sp.dma_start(taps[:, n, :], conv_w[0, n:n + 1].rearrange("a (b p) -> p (a b)", p=P)
                                         ).then_inc(taps_loaded, 16)

            def group(tc, more):
                for b in range(NB):
                    load_gates(tc, b, more)
                    if more and b < 2:
                        load_y(tc + 1, b)
                if more:
                    load_conv(tc + 1, 3)
                reached(sp, summed, SUMS * (tc + 1))
                sp.dma_start(scr["m"][:, bass.ds(tc * TC, TC)].rearrange("(m p) t -> p m t", p=P), total[:]
                             ).then_inc(stored, 16)

            with sp.Fori(0, NTC - 1) as tc:
                group(tc, True)
            group(NTC - 1, False)
            arrived(sp, stored, NTC)

        @block.tensor
        def _(pe):
            pe.sem_inc(acc_done, LEAD)

            def group(tc, peeled):
                for b in range(NB):
                    for m in range(NM):
                        n = PER * tc + NM * b + m
                        if m == 0:
                            reached(pe, y_lo_done, NB * tc + b + 1)
                        reached(pe, gated, n - 3)
                        cols = slice(m * P, (m + 1) * P)
                        for k in range(WB):
                            if peeled and m == 0:
                                reached(pe, w_lo_done, WB * b + k + 1)
                            wk = WB * b + k
                            nc.tensor.matmul(acc[m % 4][:], w_hi[:, wk, cols], y_hi[b][:, k, :], start=k == 0, stop=False)
                            nc.tensor.matmul(acc[m % 4][:], w_hi[:, wk, cols], y_lo[b][:, k, :], start=False, stop=False)
                            mm = nc.tensor.matmul(acc[m % 4][:], w_lo[:, wk, cols], y_hi[b][:, k, :],
                                                  start=False, stop=k == WB - 1)
                        mm.then_inc(acc_done, 1)

            group(0, True)
            with pe.Fori(1, NTC) as tc:
                group(tc, False)

        @block.scalar
        def _(act):
            for s in (w_hi_done, y_hi_done):
                act.sem_inc(s, LEAD)

            def split_y(tc, b):
                if b < 2:
                    act.wait_ge(y_loaded, (2 * tc + b + 1) * 16)
                else:
                    reached(act, conv_step, CONV_STEPS * WB * (tc + 1))
                reached(act, acc_done, PER * (tc - 1) + NM * (b + 1) if b or not isinstance(tc, int) else 0)
                nc.scalar.activation(y_hi[b][:], (y_raw if b < 2 else y_conv)[:], ACT.Copy
                                     ).then_inc(y_hi_done, 1)

            def split_w(k):
                act.wait_ge(w_loaded[k % 2], 16 * (k // 2 + 1))
                nc.scalar.activation(w_hi[:, k, :], w_raw[k % 2][:], ACT.Copy).then_inc(w_hi_done, 1)

            for b in range(NB):
                if b < 2:
                    split_y(0, b)
                for k in range(WB * b, WB * (b + 1)):
                    split_w(k)
            split_y(0, 2)
            with act.Fori(1, NTC) as tc:
                for b in range(NB):
                    split_y(tc, b)

        @block.gpsimd
        def _(pool):
            for s in (w_lo_done, y_lo_done):
                pool.sem_inc(s, LEAD)

            def split_y(n, b):
                reached(pool, y_hi_done, n + 1)
                nc.gpsimd.tensor_tensor(y_lo[b][:], (y_raw if b < 2 else y_conv)[:], y_hi[b][:].bitcast(F32), ALU.subtract
                                        ).then_inc(y_lo_done, 1)

            def conv_gate(tc, k):
                pool.wait_ge(conv_loaded, (WB * tc + k + 1) * 64)
                nc.gpsimd.tensor_tensor(post[:], post[:], z[:], ALU.mult).then_inc(post_done, 1)

            split_y(0, 0)
            for k in range(WB, NB * WB):
                if k == WB:
                    split_y(1, 1)
                    reached(pool, w_lo_done, WB)
                reached(pool, w_hi_done, k + 1)
                nc.gpsimd.tensor_tensor(w_lo[:, k, :], w_raw[k % 2][:], w_hi[:, k, :].bitcast(F32), ALU.subtract
                                        ).then_inc(w_lo_done, 1)
                if k % 2 == 1:
                    conv_gate(0, (k - WB) // 2)

            def group(tc):
                split_y(NB * tc + 2, 2)
                for b in range(2):
                    split_y(NB * (tc + 1) + b, b)
                    for k in range(2 * b, 2 * b + 2):
                        conv_gate(tc + 1, k)

            group(0)
            with pool.Fori(1, NTC - 1) as tc:
                group(tc)
            split_y(NB * NTC - 1, 2)

        @block.vector
        def _(dve):
            for s in (gated, summed, conv_step):
                dve.sem_inc(s, LEAD)

            def convolve(tc, k):
                n = WB * tc + k
                done = CONV_STEPS * n
                dve.wait_ge(conv_loaded, (n + 1) * 64)
                reached(dve, conv_step, done)
                nc.vector.tensor_copy(prod[:, 0:TAPS - 1], halo[:, k, :]).then_inc(conv_step, 1)
                nc.vector.tensor_tensor(prod[:, TAPS - 1:], pre[:], u_[:], ALU.mult).then_inc(conv_step, 1)
                reached(dve, conv_step, done + 2)
                nc.vector.tensor_copy(halo[:, k, :], prod[:, TC:]).then_inc(conv_step, 1)
                reached(dve, y_lo_done, NB * tc)
                nc.vector.tensor_scalar(y_conv[:, k, :], prod[:, 0:TC], taps[:, 0, k:k + 1], None, ALU.mult
                                        ).then_inc(conv_step, 1)
                for t in range(1, TAPS):
                    reached(dve, conv_step, done + 3 + t)
                    nc.vector.scalar_tensor_tensor(y_conv[:, k, :], prod[:, t:t + TC], taps[:, t, k:k + 1], y_conv[:, k, :],
                                                   ALU.mult, ALU.add).then_inc(conv_step, 1)
                reached(dve, conv_step, done + 3 + TAPS)
                dve.wait_ge(post_done, n + 1)
                nc.vector.tensor_tensor(y_conv[:, k, :], y_conv[:, k, :], post[:], ALU.mult).then_inc(conv_step, 1)

            nc.vector.memset(halo[:], 0.0).then_inc(halo_zero, 1)
            for k in range(WB):
                reached(dve, w_hi_done, k + 1)
                nc.vector.tensor_tensor(w_lo[:, k, :], w_raw[k % 2][:], w_hi[:, k, :].bitcast(F32), ALU.subtract
                                        ).then_inc(w_lo_done, 1)
            dve.wait_ge(halo_zero, 1)
            dve.wait_ge(taps_loaded, 16 * TAPS)
            for k in range(WB):
                convolve(0, k)

            def group(tc, more):
                for b in range(NB):
                    for m in range(NM + 1):
                        if m < NM:
                            n = PER * tc + NM * b + m
                            reached(dve, acc_done, n + 1)
                            dve.wait_ge(g_loaded[m % 4], (tc * (PER // 4) + (NM * b + m) // 4 + 1) * 16)
                            if b == 0:
                                if m == 0:
                                    arrived(dve, stored, tc)
                                nc.vector.tensor_tensor(total[:, m, :], acc[m % 4][:], gate[m % 4][:], ALU.mult
                                                        ).then_inc(gated, 1)
                            else:
                                nc.vector.tensor_tensor(gate[m % 4][:], acc[m % 4][:], gate[m % 4][:], ALU.mult
                                                        ).then_inc(gated, 1)
                        if m > 0 and b > 0:
                            n = PER * tc + NM * b + m - 1
                            reached(dve, gated, n + 1)
                            nc.vector.tensor_tensor(total[:, m - 1, :], total[:, m - 1, :], gate[(m - 1) % 4][:], ALU.add
                                                    ).then_inc(summed, 1)
                        if more and NM * b + m in (11, 15, 19, 23) and m < NM:
                            convolve(tc + 1, (NM * b + m - 11) // 4)

            with dve.Fori(0, NTC - 1) as tc:
                group(tc, True)
            group(NTC - 1, False)


def project_out(nc, sem, scr, w_out, ln_g, ln_b, x, out):
    with ExitStack() as ctx:
        sb = lambda n, s, d=F32: ctx.enter_context(nc.sbuf_tensor("o_" + n, s, d))
        s_ = lambda n: sem("o_" + n)
        TG = 256
        NG, HALF = T // TG, D // 2
        w_raw = [sb(f"w_raw{i}", [P, D]) for i in range(2)]
        w_hi = sb("w_hi", [P, KD, D], F32R)
        w_lo = sb("w_lo", [P, KD, D], F32R)
        m_raw = sb("m_raw", [P, KD, TG])
        m_hi = [sb(f"m_hi{i}", [P, KD, TG], F32R) for i in range(2)]
        m_lo = [sb(f"m_lo{i}", [P, KD, TG], F32R) for i in range(2)]
        gate, gam, bet = sb("gate", [P, D]), sb("gam", [P, D]), sb("bet", [P, D])
        xt = [sb(f"xt{i}", [P, D]) for i in range(2)]
        r = [sb(f"r{i}", [P, D]) for i in range(2)]
        o = [sb(f"o{i}", [P, D]) for i in range(2)]
        stats = sb("stats", [P, 12])
        count = sb("count", [P, 1])
        mv = sb("mv", [P, 2])
        small = sb("small", [P, 3])
        acc = [ctx.enter_context(nc.psum_tensor(f"o_acc{i}", [P, HALF], F32)) for i in range(4)]
        par_loaded = s_("par_loaded")
        w_loaded = [s_(f"w_loaded{i}") for i in range(2)]
        m_loaded = s_("m_loaded")
        x_loaded = [s_(f"x_loaded{i}") for i in range(2)]
        stored = [s_(f"stored{i}") for i in range(2)]
        w_hi_done, w_lo_done, m_hi_done, m_lo_done = s_("w_hi_done"), s_("w_lo_done"), s_("m_hi_done"), s_("m_lo_done")
        acc_done, scaled, summed, stats_done, mv_done = s_("acc_done"), s_("scaled"), s_("summed"), s_("stats_done"), s_("mv_done")
        ve_done, std_done, rstd_done, xhat_done, gam_done, bet_done = (
            s_(n) for n in ("ve_done", "std_done", "rstd_done", "xhat_done", "gam_done", "bet_done"))
        block = ctx.enter_context(nc.Block())

        @block.sync
        def _(sp):
            for s in (*stored, *x_loaded):
                sp.sem_inc(s, 16)

            def load_m(i):
                reached(sp, m_lo_done, i)
                sp.dma_start(m_raw[:], scr["m"][:, bass.ds(i * TG, TG)].rearrange("(k p) t -> p k t", p=P)
                             ).then_inc(m_loaded, 16)

            def load_x(i, u):
                reached(sp, summed, 2 * (2 * i + u - 1))
                sp.dma_start(xt[u][:], x[bass.ds((2 * i + u) * P, P), :]).then_inc(x_loaded[u], 16)

            load_m(0)
            for k in range(KD):
                if k >= 2:
                    reached(sp, w_lo_done, k - 1)
                sp.dma_start(w_raw[k % 2][:], w_out[0, k * P:(k + 1) * P, :]).then_inc(w_loaded[k % 2], 16)
            sp.dma_start(gate[:], scr["gate"][0].partition_broadcast(P)).then_inc(par_loaded, 16)
            sp.dma_start(gam[:], ln_g[0].partition_broadcast(P)).then_inc(par_loaded, 16)
            sp.dma_start(bet[:], ln_b[0].partition_broadcast(P)).then_inc(par_loaded, 16)
            load_x(0, 0)
            load_x(0, 1)

            def group(i, more):
                if more:
                    load_m(i + 1)
                for u in range(2):
                    reached(sp, bet_done, 2 * i + u + 1)
                    sp.dma_start(out[0, bass.ds((2 * i + u) * P, P), :], o[u][:]).then_inc(stored[u], 16)
                    if more:
                        load_x(i + 1, u)

            with sp.Fori(0, NG - 1) as i:
                group(i, True)
            group(NG - 1, False)
            for s in stored:
                arrived(sp, s, NG)

        @block.tensor
        def _(pe):
            pe.sem_inc(acc_done, LEAD)

            def group(i, s):
                for u in range(2):
                    for half in range(2):
                        n = 8 * i + 4 * s + 2 * u + half
                        reached(pe, scaled, n - 3)
                        bank = acc[2 * u + half]
                        cols, tok = slice(half * HALF, (half + 1) * HALF), slice(u * P, (u + 1) * P)
                        if u == 0 and half == 0:
                            reached(pe, m_lo_done, 2 * i + s + 1)
                        for k in range(KD):
                            if n is not None and isinstance(i, int) and u == 0 and half == 0:
                                reached(pe, w_lo_done, k + 1)
                            nc.tensor.matmul(bank[:], m_hi[s][:, k, tok], w_hi[:, k, cols], start=k == 0, stop=False)
                            nc.tensor.matmul(bank[:], m_hi[s][:, k, tok], w_lo[:, k, cols], start=False, stop=False)
                            mm = nc.tensor.matmul(bank[:], m_lo[s][:, k, tok], w_hi[:, k, cols],
                                                  start=False, stop=k == KD - 1)
                        mm.then_inc(acc_done, 1)

            group(0, 0)
            group(0, 1)
            with pe.Fori(1, NG // 2) as i:
                group(i, 0)
                group(i, 1)

        @block.scalar
        def _(act):
            for s in (w_hi_done, m_hi_done, std_done):
                act.sem_inc(s, LEAD)

            def split_m(i, s):
                act.wait_ge(m_loaded, (2 * i + s + 1) * 16)
                reached(act, acc_done, 4 * (2 * i + s) - 4)
                nc.scalar.activation(m_hi[s][:], m_raw[:], ACT.Copy).then_inc(m_hi_done, 1)

            def roots(i, s):
                for u in range(2):
                    n = 4 * i + 2 * s + u
                    reached(act, ve_done, n + 1)
                    nc.scalar.activation(small[:, 1:2], small[:, 0:1], ACT.Sqrt).then_inc(std_done, 1)

            split_m(0, 0)
            for k in range(KD):
                act.wait_ge(w_loaded[k % 2], 16 * (k // 2 + 1))
                nc.scalar.activation(w_hi[:, k, :], w_raw[k % 2][:], ACT.Copy).then_inc(w_hi_done, 1)
            with act.Fori(0, NG // 2 - 1) as i:
                split_m(i, 1)
                roots(i, 0)
                split_m(i + 1, 0)
                roots(i, 1)
            split_m(NG // 2 - 1, 1)
            roots(NG // 2 - 1, 0)
            roots(NG // 2 - 1, 1)

        @block.gpsimd
        def _(pool):
            for s in (w_lo_done, m_lo_done, bet_done):
                pool.sem_inc(s, LEAD)

            def split_m(i, s):
                reached(pool, m_hi_done, 2 * i + s + 1)
                nc.gpsimd.tensor_tensor(m_lo[s][:], m_raw[:], m_hi[s][:].bitcast(F32), ALU.subtract).then_inc(m_lo_done, 1)

            def shift(i, s):
                for u in range(2):
                    n = 4 * i + 2 * s + u
                    reached(pool, gam_done, n + 1)
                    pool.wait_ge(stored[u], (2 * i + s + 1) * 16)
                    nc.gpsimd.tensor_tensor(o[u][:], r[u][:], bet[:], ALU.add).then_inc(bet_done, 1)

            split_m(0, 0)
            for k in range(KD):
                reached(pool, w_hi_done, k + 1)
                nc.gpsimd.tensor_tensor(w_lo[:, k, :], w_raw[k % 2][:], w_hi[:, k, :].bitcast(F32), ALU.subtract
                                        ).then_inc(w_lo_done, 1)
            pool.wait_ge(par_loaded, 48)
            with pool.Fori(0, NG // 2 - 1) as i:
                split_m(i, 1)
                shift(i, 0)
                split_m(i + 1, 0)
                shift(i, 1)
            split_m(NG // 2 - 1, 1)
            shift(NG // 2 - 1, 0)
            shift(NG // 2 - 1, 1)

        @block.vector
        def _(dve):
            for s in (scaled, summed, stats_done, mv_done, ve_done, rstd_done, xhat_done, gam_done):
                dve.sem_inc(s, LEAD)
            dve.wait_ge(par_loaded, 48)
            with dve.Fori(0, NG) as i:
                for u in range(2):
                    n = 2 * i + u
                    reached(dve, bet_done, n - 1)
                    for half in range(2):
                        cols = slice(half * HALF, (half + 1) * HALF)
                        reached(dve, acc_done, 2 * n + half + 1)
                        nc.vector.tensor_tensor(r[u][:, cols], acc[2 * u + half][:], gate[:, cols], ALU.mult).then_inc(scaled, 1)
                    dve.wait_ge(x_loaded[u], (i + 2) * 16)
                    for half in range(2):
                        cols = slice(half * HALF, (half + 1) * HALF)
                        reached(dve, scaled, 2 * n + half + 1)
                        nc.vector.scalar_tensor_tensor(r[u][:, cols], xt[u][:, cols], ALPHA, r[u][:, cols],
                                                       ALU.mult, ALU.add).then_inc(summed, 1)
                    for half in range(2):
                        cols = slice(half * HALF, (half + 1) * HALF)
                        reached(dve, summed, 2 * n + half + 1)
                        nc.vector.bn_stats(stats[:, 6 * half:6 * half + 6], r[u][:, cols]).then_inc(stats_done, 1)
                    reached(dve, stats_done, 2 * n + 2)
                    nc.vector.tensor_copy(count[:], stats[:, 0:1])
                    nc.vector.bn_aggr(mv[:], stats[:]).then_inc(mv_done, 1)
                    reached(dve, mv_done, n + 1)
                    nc.vector.tensor_scalar(small[:, 0:1], mv[:, 1:2], LN_EPS, None, ALU.add).then_inc(ve_done, 1)
                    reached(dve, std_done, n + 1)
                    nc.vector.reciprocal(small[:, 2:3], small[:, 1:2]).then_inc(rstd_done, 1)
                    reached(dve, rstd_done, n + 1)
                    nc.vector.tensor_scalar(r[u][:], r[u][:], mv[:, 0:1], small[:, 2:3], ALU.subtract, ALU.mult
                                            ).then_inc(xhat_done, 1)
                    reached(dve, xhat_done, n + 1)
                    nc.vector.tensor_tensor(r[u][:], r[u][:], gam[:], ALU.mult).then_inc(gam_done, 1)


def build(nc, x, c, w_mod, b_mod, w_in, conv_w, hgrn_norm_w, lower_bounds, w_branch, w_out, ln_g, ln_b, out):
    dram = lambda n, s: nc.dram_tensor(n, s, F32).ap()
    values = dram("values", (3, T, W))
    rows = [1, D, IN_COLS, 3 * W, 2 * W]
    scratch = dram("scratch", (sum(rows), T))
    gate, merged, proj, y, proj_lo = (scratch[sum(rows[:n]):sum(rows[:n + 1])] for n in range(len(rows)))
    scr = {
        "gate": gate[:, 0:D],
        "m": merged,
        "proj": proj,
        "y": y.rearrange("(b w) t -> b w t", b=3),
        "proj_lo": proj_lo,
        "i": values[0], "v_hi": values[1], "v_lo": values[2],
    }

    def stage(f, *args):
        with nc.cleanup_on_exit():
            f(nc, lambda name: nc.alloc_semaphore(name=name), *args)

    with nc.sbuf_tensor("ident", [P, P], F32) as ident:
        with nc.sbuf_tensor("hT_hi", [P, KD, T], F32R) as hT_hi, nc.sbuf_tensor("hT_lo", [P, KD, T], F32R) as hT_lo:
            g = {"ident": ident, "hT_hi": hT_hi, "hT_lo": hT_lo}
            stage(modulated_input, g, x[0], c, w_mod, b_mod, scr)
            stage(token_major_values, g, w_in, scr)
            stage(project, g, w_in, scr, RUNS, "p_")
            stage(hgrn2_and_columns, g, w_in, scr, lower_bounds, hgrn_norm_w)
            stage(attention_and_gates, g, w_in, scr)
        stage(conv_and_merge, scr, conv_w, w_branch)
        stage(project_out, scr, w_out, ln_g, ln_b, x[0], out)


_INS = ["x", "c", "w_mod", "b_mod", "w_in", "conv_w", "hgrn_norm_w", "lower_bounds", "w_branch", "w_out", "ln_g", "ln_b"]


def kernel(**inputs):
    import numpy as np
    import concourse.bacc as bacc
    from concourse.bass_utils import run_bass_kernel_spmd

    nc = bacc.Bacc("TRN2", target_bir_lowering=False, num_devices=1)
    arrays, args = {}, []
    for name in _INS:
        a = np.ascontiguousarray(inputs[name])
        arrays[f"in_{name}"] = a
        args.append(nc.dram_tensor(f"in_{name}", a.shape, mybir.dt.from_np(a.dtype), kind="ExternalInput").ap())
    out = nc.dram_tensor("out_x", (1, T, D), F32, kind="ExternalOutput").ap()
    build(nc, *args, out)
    r = run_bass_kernel_spmd(nc, [arrays], core_ids=[0])
    return r.results[0]["out_x"]
```

```python
from contextlib import ExitStack

import concourse.bass as bass
from concourse import mybir

F32 = mybir.dt.float32
F32R = mybir.dt.float32r
ACT = mybir.ActivationFunctionType
ALU = mybir.AluOpType
AX = mybir.AxisListType

P = 128
T = 2048
D = 1024
KD = D // P
TC = 512
NTC = T // TC
W = 512
WB = W // P
IN_COLS = 12 * W + 3 * D
NCB = IN_COLS // P
HEADS, DH = 8, 64
ALPHA = 2.0 ** 0.25
LN_EPS = 1e-5
RMS_EPS = 1e-6
SCALE = DH ** -0.5

QA, KA, VA, ZA, QB, FB, IB, ZB, PRE, POST, UC, ZC, GA = (WB * n for n in range(13))

RUNS = [(ZA, 8, "Sigmoid", "gate"), (FB, 4, "Sigmoid", None), (ZB, 4, "Sigmoid", "gate"), (UC, 4, "Copy", None),
        (ZC, 4, "Sigmoid", "gate")]
FUNCS = {"Copy": ACT.Copy, "Sigmoid": ACT.Sigmoid}


def after(eng, sem, value):
    if isinstance(value, int) and value <= 0:
        return
    eng.wait_ge(sem, value)


LEAD = 8


def reached(eng, sem, count):
    if isinstance(count, int) and count <= 0:
        return
    eng.wait_ge(sem, count + LEAD)


def arrived(eng, sem, count, each=16):
    eng.wait_ge(sem, (count + 1) * each)


def modulation(nc, sem, g, c, w_mod, b_mod, scr):
    with ExitStack() as ctx:
        sb = lambda n, s, d=F32: ctx.enter_context(nc.sbuf_tensor(n, s, d))
        MC = 256
        NM = 3 * D // MC
        c_col = sb("c_col", [P, KD])
        c_rep = sb("c_rep", [P, KD, P])
        gate = sb("gate", [P, D])
        wm = [sb(f"wm{i}", [P, KD, MC]) for i in range(3)]
        ps_mod = [ctx.enter_context(nc.psum_tensor(f"ps_mod{i}", [P, MC], F32)) for i in range(2)]
        c_loaded, b_loaded, c_spread = sem("c_loaded"), sem("b_loaded"), sem("c_spread")
        wm_loaded = [sem(f"wm_loaded{i}") for i in range(3)]
        mod_summed, mod_ready, gate_stored = sem("mod_summed"), sem("mod_ready"), sem("gate_stored")
        ident_zero, ident_ready = sem("ident_zero"), sem("ident_ready")
        ident, mod = g["ident"], g["mod"]
        block = ctx.enter_context(nc.Block())

        @block.sync
        def _(sp):
            with nc.allow_non_contiguous_dma(reason="1024 values of c"):
                sp.dma_start(c_col[:], c.rearrange("a (k p) -> p (a k)", p=P)).then_inc(c_loaded, 16)
            for m in range(NM):
                if m >= 3:
                    sp.wait_ge(mod_summed, m - 2)
                sp.dma_start(wm[m % 3][:], w_mod[0, :, m * MC:(m + 1) * MC].rearrange("(k p) n -> p k n", p=P)
                             ).then_inc(wm_loaded[m % 3], 16)
                if m == 1:
                    sp.dma_start(mod[:], b_mod[0, 0:2 * D].partition_broadcast(P)).then_inc(b_loaded, 16)
                    sp.dma_start(gate[:], b_mod[0, 2 * D:3 * D].partition_broadcast(P)).then_inc(b_loaded, 16)
            sp.wait_ge(mod_ready, NM)
            sp.dma_start(scr["gate"], gate[0:1, :]).then_inc(gate_stored, 16)
            sp.wait_ge(gate_stored, 16)

        @block.gpsimd
        def _(pool):
            nc.gpsimd.memset(ident[:], 0.0).then_inc(ident_zero, 1)
            pool.wait_ge(ident_zero, 1)
            nc.gpsimd.affine_select(out=ident[:], in_=ident[:], compare_op=ALU.not_equal, fill=1.0, base=0,
                                    pattern=[[-1, P]], channel_multiplier=1).then_inc(ident_ready, 1)
            pool.wait_ge(ident_ready, 1)

        @block.tensor
        def _(pe):
            pe.wait_ge(c_spread, 1)
            for m in range(NM):
                pe.wait_ge(wm_loaded[m % 3], 16 * (m // 3 + 1))
                if m >= 2:
                    pe.wait_ge(mod_ready, m - 1)
                for k in range(KD):
                    mm = nc.tensor.matmul(ps_mod[m % 2][:], c_rep[:, k, :], wm[m % 3][:, k, :],
                                          start=k == 0, stop=k == KD - 1)
                mm.then_inc(mod_summed, 1)

        @block.vector
        def _(dve):
            dve.wait_ge(c_loaded, 16)
            nc.vector.tensor_copy(c_rep[:], c_col[:].unsqueeze(2).to_broadcast([P, KD, P])).then_inc(c_spread, 1)
            dve.wait_ge(b_loaded, 32)
            for m in range(NM):
                dve.wait_ge(mod_summed, m + 1)
                at = m * MC
                cols = mod[:, at:at + MC] if at < 2 * D else gate[:, at - 2 * D:at - 2 * D + MC]
                nc.vector.scalar_tensor_tensor(cols, ps_mod[m % 2][:], 0.0 if at < D else 1.0, cols,
                                               ALU.add, ALU.add).then_inc(mod_ready, 1)
            dve.wait_ge(mod_ready, NM)


def modulated_input_and_values(nc, sem, g, x, w_in, scr):
    with ExitStack() as ctx:
        sb = lambda n, s, d=F32: ctx.enter_context(nc.sbuf_tensor(n, s, d))
        NT = T // P
        PIECE, RING = 2, 3
        NP = KD // PIECE
        xt = [sb(f"xt{i}", [P, D]) for i in range(2)]
        hm = [sb(f"hm{i}", [P, D]) for i in range(2)]
        stats = sb("stats", [P, 4, 12])
        count = sb("count", [P, 1])
        mv = sb("mv", [P, 4, 2])
        ve, std, rstd = sb("ve", [P, 4]), sb("std", [P, 4]), sb("rstd", [P, 4])
        w_raw = [sb(f"vw_raw{i}", [P, PIECE, W]) for i in range(RING)]
        w_hi = sb("vw_hi", [P, KD, W], F32R)
        w_lo = sb("vw_lo", [P, KD, W], F32R)
        v_hi = [sb(f"v_hi{i}", [P, W], F32R) for i in range(2)]
        v_lo = [sb(f"v_lo{i}", [P, W], F32R) for i in range(2)]
        ps_t = [ctx.enter_context(nc.psum_tensor(f"ps_t{i}", [P, 4, P], F32)) for i in range(4)]
        acc = [ctx.enter_context(nc.psum_tensor(f"v_acc{i}", [P, W], F32)) for i in range(2)]
        x_loaded = [sem(f"x_loaded{i}") for i in range(2)]
        w_loaded = [sem(f"vw_loaded{i}") for i in range(RING)]
        hi_stored = [sem(f"v_hi_stored{i}") for i in range(2)]
        lo_stored = [sem(f"v_lo_stored{i}") for i in range(2)]
        stats_done, mv_done, ve_done, std_done = sem("stats_done"), sem("mv_done"), sem("ve_done"), sem("std_done")
        rstd_done, xhat_done, scaled_done, hm_done = sem("rstd_done"), sem("xhat_done"), sem("scaled_done"), sem("hm_done")
        turned, hi_done, lo_done = sem("turned"), sem("hi_done"), sem("lo_done")
        w_hi_done, w_lo_done, w_used = sem("vw_hi_done"), sem("vw_lo_done"), sem("vw_used")
        acc_done, v_hi_done, v_lo_done = sem("v_acc_done"), sem("v_hi_done"), sem("v_lo_done")
        ident, mod, hT_hi, hT_lo = g["ident"], g["mod"], g["hT_hi"], g["hT_lo"]
        block = ctx.enter_context(nc.Block())

        def load_piece(eng, n):
            if n >= RING:
                reached(eng, w_lo_done, PIECE * (n - RING + 1))
            col, k = (VA if n < NP else IB) * P, n % NP * PIECE
            eng.dma_start(w_raw[n % RING][:], w_in[0, k * P:(k + PIECE) * P, col:col + W].rearrange("(k p) n -> p k n", p=P)
                          ).then_inc(w_loaded[n % RING], 16)

        @block.sync
        def _(sp):
            for s in (*hi_stored, *lo_stored):
                sp.sem_inc(s, 16)

            def load_x(i, u):
                reached(sp, xhat_done, 4 * i + u - 1)
                sp.dma_start(xt[u % 2][:], x[bass.ds((4 * i + u) * P, P), :]).then_inc(x_loaded[u % 2], 16)

            def store_v(i, u):
                reached(sp, v_lo_done, 4 * i + u + 1)
                rows = bass.ds((4 * i + u) * P, P)
                sp.dma_start(scr["v_hi"][rows, :], v_hi[u % 2][:].bitcast(F32)).then_inc(hi_stored[u % 2], 16)
                sp.dma_start(scr["v_lo"][rows, :], v_lo[u % 2][:].bitcast(F32)).then_inc(lo_stored[u % 2], 16)

            load_x(0, 0)
            load_piece(sp, 0)
            load_x(0, 1)
            for n in range(1, RING):
                load_piece(sp, n)
            load_x(0, 2)
            for n in range(RING, NP):
                load_piece(sp, n)
            load_x(0, 3)
            for n in range(NP, NP + RING):
                load_piece(sp, n)
            with sp.Fori(0, 3) as i:
                for u in range(4):
                    load_x(i + 1, u)
                    store_v(i, u)
            for u in range(3):
                store_v(3, u)
            load_piece(sp, 2 * NP - 1)
            store_v(3, 3)
            with sp.Fori(0, NT // 2) as i:
                for u in range(2):
                    reached(sp, v_hi_done, 2 * i + u + 1 + NT)
                    sp.dma_start(scr["i"][bass.ds((2 * i + u) * P, P), :], v_hi[u][:].bitcast(F32)).then_inc(hi_stored[u], 16)
            for u in range(2):
                arrived(sp, hi_stored[u], NT)
                arrived(sp, lo_stored[u], NT // 2)

        @block.gpsimd
        def _(pool):
            for s in (hm_done, w_lo_done):
                pool.sem_inc(s, LEAD)

            def shift(i, u):
                reached(pool, scaled_done, 4 * i + u + 1)
                nc.gpsimd.tensor_tensor(hm[u % 2][:], hm[u % 2][:], mod[:, 0:D], ALU.add).then_inc(hm_done, 1)

            for k in range(KD):
                reached(pool, w_hi_done, k + 1)
                nc.gpsimd.tensor_tensor(w_lo[:, k, :], w_raw[k // PIECE % RING][:, k % PIECE, :], w_hi[:, k, :].bitcast(F32),
                                        ALU.subtract).then_inc(w_lo_done, 1)
                if k in (1, 5):
                    shift(0, k // 4)
            for u in range(2, 4):
                shift(0, u)
            with pool.Fori(1, 4) as i:
                for u in range(4):
                    shift(i, u)

        @block.tensor
        def _(pe):
            for s in (turned, acc_done, w_used):
                pe.sem_inc(s, LEAD)

            def turn(i, u):
                reached(pe, hm_done, 4 * i + u + 1)
                reached(pe, lo_done, 2 * (4 * i + u) - 2)
                for half in range(2):
                    for k in range(4):
                        mm = nc.tensor.transpose(ps_t[2 * (u % 2) + half][:, k, :],
                                                 hm[u % 2][:, (4 * half + k) * P:(4 * half + k + 1) * P], ident[:])
                    mm.then_inc(turned, 1)

            def product(n):
                unit, t = divmod(n, NT)
                reached(pe, v_lo_done if n < NT + 2 else v_hi_done, n - 1)
                tok = slice(t * P, (t + 1) * P)
                for k in range(KD):
                    if t == 0:
                        reached(pe, w_lo_done, KD * unit + k + 1)
                    nc.tensor.matmul(acc[n % 2][:], hT_hi[:, k, tok], w_hi[:, k, :], start=k == 0, stop=False)
                    nc.tensor.matmul(acc[n % 2][:], hT_hi[:, k, tok], w_lo[:, k, :], start=False, stop=False)
                    mm = nc.tensor.matmul(acc[n % 2][:], hT_lo[:, k, tok], w_hi[:, k, :], start=False, stop=k == KD - 1)
                    if n == NT - 1 and k < KD - 1:
                        mm.then_inc(w_used, 1)
                mm.then_inc(acc_done, 1)

            turn(0, 0)
            for t in range(NT):
                if t + 1 < NT:
                    turn((t + 1) // 4, (t + 1) % 4)
                reached(pe, lo_done, 2 * (t + 1))
                product(t)
            for t in range(NT):
                product(NT + t)

        @block.scalar
        def _(act):
            for s in (std_done, hi_done, w_hi_done, v_hi_done):
                act.sem_inc(s, LEAD)

            def split_weights(unit, k):
                n = NP * unit + k // PIECE
                if k % PIECE == 0:
                    act.wait_ge(w_loaded[n % RING], 16 * (n // RING + 1))
                if unit:
                    if k < KD - 1:
                        reached(act, w_used, k + 1)
                    else:
                        reached(act, acc_done, NT)
                nc.scalar.activation(w_hi[:, k, :], w_raw[n % RING][:, k % PIECE, :], ACT.Copy).then_inc(w_hi_done, 1)

            def root(i, u):
                reached(act, ve_done, 4 * i + u + 1)
                nc.scalar.activation(std[:, u:u + 1], ve[:, u:u + 1], ACT.Sqrt).then_inc(std_done, 1)

            def high(i, u):
                for half in range(2):
                    reached(act, turned, 2 * (4 * i + u) + half + 1)
                    nc.scalar.activation(hT_hi[:, 4 * half:4 * half + 4, bass.ds((4 * i + u) * P, P)],
                                         ps_t[2 * (u % 2) + half][:], ACT.Copy).then_inc(hi_done, 1)

            def take(i, u):
                reached(act, acc_done, 4 * i + u + 1)
                arrived(act, hi_stored[u % 2], 2 * i + u // 2)
                nc.scalar.activation(v_hi[u % 2][:], acc[u % 2][:], ACT.Copy).then_inc(v_hi_done, 1)

            root(0, 0)
            for k in range(KD):
                split_weights(0, k)
                if k == 1:
                    root(0, 1)

            def steps(i, first=False, last=False):
                for u in range(4):
                    if not (first and u == 0):
                        if u < 3:
                            root(i, u + 1)
                        elif not last:
                            root(i + 1, 0)
                    high(i, u)
                    if u > 0:
                        take(i, u - 1)
                    elif not first:
                        take(i - 1, 3)

            steps(0, first=True)
            with act.Fori(1, 3) as i:
                steps(i)
            steps(3, last=True)
            for k in range(KD):
                split_weights(1, k)
            take(3, 3)
            with act.Fori(0, NT // 2) as i:
                for u in range(2):
                    reached(act, acc_done, 2 * i + u + 1 + NT)
                    arrived(act, hi_stored[u], NT // 2 + i)
                    nc.scalar.activation(v_hi[u][:].bitcast(F32), acc[u][:], ACT.Copy).then_inc(v_hi_done, 1)

        @block.vector
        def _(dve):
            for s in (stats_done, mv_done, ve_done, rstd_done, xhat_done, scaled_done, lo_done, v_lo_done):
                dve.sem_inc(s, LEAD)

            def statistics(i, u):
                dve.wait_ge(x_loaded[u % 2], 16 * (2 * i + u // 2 + 1))
                for half in range(2):
                    nc.vector.bn_stats(stats[:, u, 6 * half:6 * half + 6], xt[u % 2][:, 512 * half:512 * half + 512]
                                       ).then_inc(stats_done, 1)
                reached(dve, stats_done, 2 * (4 * i + u) + 2)
                nc.vector.tensor_copy(count[:], stats[:, u, 0:1])
                nc.vector.bn_aggr(mv[:, u, :], stats[:, u, :]).then_inc(mv_done, 1)
                reached(dve, mv_done, 4 * i + u + 1)
                nc.vector.tensor_scalar(ve[:, u:u + 1], mv[:, u, 1:2], LN_EPS, None, ALU.add).then_inc(ve_done, 1)

            def normalise(i, u):
                n = 4 * i + u
                reached(dve, std_done, n + 1)
                nc.vector.reciprocal(rstd[:, u:u + 1], std[:, u:u + 1]).then_inc(rstd_done, 1)
                reached(dve, rstd_done, n + 1)
                reached(dve, turned, 2 * n - 2)
                nc.vector.tensor_scalar(hm[u % 2][:], xt[u % 2][:], mv[:, u, 0:1], rstd[:, u:u + 1],
                                        ALU.subtract, ALU.mult).then_inc(xhat_done, 1)
                reached(dve, xhat_done, n + 1)
                nc.vector.tensor_tensor(hm[u % 2][:], hm[u % 2][:], mod[:, D:2 * D], ALU.mult).then_inc(scaled_done, 1)

            def low(i, u):
                for half in range(2):
                    reached(dve, hi_done, 2 * (4 * i + u) + half + 1)
                    at = bass.ds((4 * i + u) * P, P)
                    nc.vector.tensor_tensor(hT_lo[:, 4 * half:4 * half + 4, at], ps_t[2 * (u % 2) + half][:],
                                            hT_hi[:, 4 * half:4 * half + 4, at].bitcast(F32),
                                            ALU.subtract).then_inc(lo_done, 1)

            def take_low(i, u):
                reached(dve, v_hi_done, 4 * i + u + 1)
                arrived(dve, lo_stored[u % 2], 2 * i + u // 2)
                nc.vector.tensor_tensor(v_lo[u % 2][:], acc[u % 2][:], v_hi[u % 2][:].bitcast(F32), ALU.subtract
                                        ).then_inc(v_lo_done, 1)

            def steps(i, first=False, last=False):
                for u in range(4):
                    if u < 3:
                        statistics(i, u + 1)
                    elif not last:
                        statistics(i + 1, 0)
                    normalise(i, u)
                    if u > 0:
                        low(i, u - 1)
                    elif not first:
                        low(i - 1, 3)
                    if u > 1:
                        take_low(i, u - 2)
                    elif not first:
                        take_low(i - 1, u + 2)

            statistics(0, 0)
            steps(0, first=True)
            with dve.Fori(1, 3) as i:
                steps(i)
            steps(3, last=True)
            low(3, 3)
            take_low(3, 2)
            for k in range(KD):
                reached(dve, w_hi_done, KD + k + 1)
                nc.vector.tensor_tensor(w_lo[:, k, :], w_raw[(NP + k // PIECE) % RING][:, k % PIECE, :],
                                        w_hi[:, k, :].bitcast(F32), ALU.subtract).then_inc(w_lo_done, 1)
            take_low(3, 3)


def project(nc, sem, g, w_in, scr, runs, tag):
    with ExitStack() as ctx:
        sb = lambda n, s, d=F32: ctx.enter_context(nc.sbuf_tensor(tag + n, s, d))
        s_ = lambda n: sem(tag + n)
        w_raw = sb("w_raw", [P, KD, P])
        w_hi = [sb(f"w_hi{i}", [P, KD, P], F32R) for i in range(2)]
        w_lo = [sb(f"w_lo{i}", [P, KD, P], F32R) for i in range(2)]
        out = [sb(f"out{i}", [P, TC]) for i in range(2)]
        split_hi = [sb(f"split_hi{i}", [P, TC], F32R) for i in range(2)]
        split_lo = [sb(f"split_lo{i}", [P, TC], F32R) for i in range(2)]
        acc = [ctx.enter_context(nc.psum_tensor(f"{tag}acc{i}", [P, TC], F32)) for i in range(2)]
        w_loaded, w_hi_done, w_lo_done, acc_done = s_("w_loaded"), s_("w_hi_done"), s_("w_lo_done"), s_("acc_done")
        act_out, dve_in, dve_out = s_("act_out"), s_("dve_in"), s_("dve_out")
        stored = [s_(f"stored{i}") for i in range(2)]
        stored_lo = [s_(f"stored_lo{i}") for i in range(2)]
        hT_hi, hT_lo = g["hT_hi"], g["hT_lo"]
        block = ctx.enter_context(nc.Block())

        plan, n0, a0, v0 = [], 0, 0, 0
        for cb, blocks, func, then in runs:
            plan.append((cb, blocks, func, then, n0, a0, v0))
            n0 += blocks
            if then is None:
                a0 += NTC * blocks
            else:
                v0 += NTC * blocks
        TOTAL = n0

        def each_run(eng, body):
            for r, run in enumerate(plan):
                with eng.Fori(0, run[1] // 2) as i:
                    body(run, i)

        @block.sync
        def _(sp):
            def load(cb, n):
                sp.wait_ge(w_lo_done, n)
                sp.dma_start(w_raw[:], w_in[0, :, bass.ds(cb * P, P)].rearrange("(k p) n -> p k n", p=P)
                             ).then_inc(w_loaded, 16)

            load(plan[0][0], 0)
            for r, (cb, blocks, func, then, n0, a0, v0) in enumerate(plan):
                def stores(i, u):
                    for tc in range(NTC):
                        q = 2 * NTC * i + NTC * u + tc
                        s = tc % 2
                        if then is None:
                            sp.wait_ge(act_out, a0 + q + 1)
                        else:
                            sp.wait_ge(dve_out, v0 + q + 1)
                        rows = scr["proj"][bass.ds((cb + 2 * i + u) * P, P), tc * TC:(tc + 1) * TC]
                        if then == "split":
                            sp.dma_start(rows, split_hi[s][:].bitcast(F32)).then_inc(stored[s], 16)
                            sp.dma_start(scr["proj_lo"][bass.ds((cb + 2 * i + u) * P, P), tc * TC:(tc + 1) * TC],
                                         split_lo[s][:].bitcast(F32)).then_inc(stored_lo[s], 16)
                        else:
                            sp.dma_start(rows, out[s][:]).then_inc(stored[s], 16)

                def pair(i, more):
                    load(cb + 2 * i + 1, n0 + 2 * i + 1)
                    stores(i, 0)
                    if more == "same":
                        load(cb + 2 * i + 2, n0 + 2 * i + 2)
                    elif more is not None:
                        load(more, n0 + 2 * i + 2)
                    stores(i, 1)

                if blocks > 2:
                    with sp.Fori(0, blocks // 2 - 1) as i:
                        pair(i, "same")
                pair(blocks // 2 - 1, plan[r + 1][0] if r + 1 < len(plan) else None)
            n_lo = sum(b for _, b, _, then in runs if then == "split")
            for s in range(2):
                sp.wait_ge(stored[s], 16 * TOTAL * NTC // 2)
                if n_lo:
                    sp.wait_ge(stored_lo[s], 16 * n_lo * NTC // 2)

        @block.tensor
        def _(pe):
            free = {None: act_out, "gate": dve_out, "split": dve_out}
            for r, (cb, blocks, func, then, n0, a0, v0) in enumerate(plan):
                if r:
                    pe.wait_ge(free[plan[r - 1][3]], a0 if plan[r - 1][3] is None else v0)
                base = a0 if then is None else v0

                def blocks2(i, peeled=False):
                    for u in range(2):
                        pe.wait_ge(w_lo_done, n0 + 2 * i + u + 1)
                        for tc in range(NTC):
                            q = 2 * NTC * i + NTC * u + tc
                            if not (peeled and u == 0 and tc < 2):
                                pe.wait_ge(free[then], base + q - 1)
                            tok = slice(tc * TC, (tc + 1) * TC)
                            for k in range(KD):
                                nc.tensor.matmul(acc[tc % 2][:], w_hi[u][:, k, :], hT_hi[:, k, tok], start=k == 0, stop=False)
                                nc.tensor.matmul(acc[tc % 2][:], w_hi[u][:, k, :], hT_lo[:, k, tok], start=False, stop=False)
                                mm = nc.tensor.matmul(acc[tc % 2][:], w_lo[u][:, k, :], hT_hi[:, k, tok],
                                                      start=False, stop=k == KD - 1)
                            mm.then_inc(acc_done, 1)

                blocks2(0, peeled=True)
                if blocks > 2:
                    with pe.Fori(1, blocks // 2) as i:
                        blocks2(i)

        @block.gpsimd
        def _(pool):
            with pool.Fori(0, TOTAL // 2) as i:
                for u in range(2):
                    pool.wait_ge(w_hi_done, 2 * i + u + 1)
                    nc.gpsimd.tensor_tensor(w_lo[u][:], w_raw[:], w_hi[u][:].bitcast(F32), ALU.subtract
                                            ).then_inc(w_lo_done, 1)

        @block.scalar
        def _(act):
            def split_weights(n, u):
                act.wait_ge(w_loaded, 16 * (n + 1))
                after(act, acc_done, NTC * (n - 1))
                nc.scalar.activation(w_hi[u][:], w_raw[:], ACT.Copy).then_inc(w_hi_done, 1)

            split_weights(0, 0)
            split_weights(1, 1)
            for r, (cb, blocks, func, then, n0, a0, v0) in enumerate(plan):
                def pair(i, more):
                    for u in range(2):
                        for tc in range(NTC):
                            m = NTC * (n0 + 2 * i + u) + tc
                            q = 2 * NTC * i + NTC * u + tc
                            s = tc % 2
                            act.wait_ge(acc_done, m + 1)
                            after(act, stored[s], 16 * ((NTC // 2) * (n0 + 2 * i + u) + tc // 2))
                            to = split_hi if then == "split" else out
                            ins = nc.scalar.activation(to[s][:], acc[s][:], FUNCS[func])
                            ins.then_inc(act_out if then is None else dve_in, 1)
                        if more:
                            split_weights(n0 + 2 * i + u + 2, u)

                first = 0
                if n0 == 0:
                    pair(0, TOTAL > 2)
                    first = 1
                last = blocks // 2 - 1
                if last > first:
                    with act.Fori(first, last) as i:
                        pair(i, True)
                if last >= first:
                    pair(last, r + 1 < len(plan))

        @block.vector
        def _(dve):
            lo_base = 0
            for r, (cb, blocks, func, then, n0, a0, v0) in enumerate(plan):
                if then is None:
                    continue

                def pair(i):
                    for u in range(2):
                        for tc in range(NTC):
                            q = 2 * NTC * i + NTC * u + tc
                            s = tc % 2
                            dve.wait_ge(dve_in, v0 + q + 1)
                            if then == "split":
                                after(dve, stored_lo[s], 16 * ((NTC // 2) * (lo_base + 2 * i + u) + tc // 2))
                                nc.vector.tensor_tensor(split_lo[s][:], acc[s][:], split_hi[s][:].bitcast(F32),
                                                        ALU.subtract).then_inc(dve_out, 1)
                            else:
                                nc.vector.tensor_tensor(out[s][:], acc[s][:], out[s][:], ALU.mult).then_inc(dve_out, 1)

                if v0 == 0:
                    pair(0)
                    if blocks > 2:
                        with dve.Fori(1, blocks // 2) as i:
                            pair(i)
                else:
                    with dve.Fori(0, blocks // 2) as i:
                        pair(i)
                if then == "split":
                    lo_base += blocks


class WovenColumns:
    PARTS = 4
    KP = KD // PARTS
    ALL = NTC * PARTS

    def __init__(self, nc, ctx, sem, g, w_in, scr, tag, split):
        sb = lambda n, s, d=F32: ctx.enter_context(nc.sbuf_tensor(tag + n, s, d))
        s_ = lambda n: sem(tag + n)
        self.nc, self.w_in, self.scr = nc, w_in, scr
        self.hT_hi, self.hT_lo = g["hT_hi"], g["hT_lo"]
        self.w_raw = sb("w_raw", [P, KD, P])
        self.w_hi = sb("w_hi", [P, KD, P], F32R)
        self.w_lo = sb("w_lo", [P, KD, P], F32R)
        self.out = [sb(f"out{i}", [P, TC], F32R if split else F32) for i in range(2)]
        self.acc = [ctx.enter_context(nc.psum_tensor(f"{tag}acc{i}", [P, TC], F32)) for i in range(2)]
        self.w_loaded, self.w_hi_done, self.w_lo_done = s_("w_loaded"), s_("w_hi_done"), s_("w_lo_done")
        self.part_done, self.taken = s_("part_done"), s_("taken")
        self.stored = [s_(f"stored{i}") for i in range(2)]
        if split:
            self.out_lo = [sb(f"out_lo{i}", [P, TC], F32R) for i in range(2)]
            self.low_taken = s_("low_taken")
            self.low_stored = [s_(f"low_stored{i}") for i in range(2)]

    def load(self, sp, n, col):
        reached(sp, self.w_lo_done, self.PARTS * n)
        sp.dma_start(self.w_raw[:], self.w_in[0, :, bass.ds(col, P)].rearrange("(k p) n -> p k n", p=P)
                     ).then_inc(self.w_loaded, 16)

    def split_high(self, act, n, part):
        if part == 0:
            act.wait_ge(self.w_loaded, 16 * (n + 1))
        reached(act, self.part_done, self.ALL * n - self.PARTS + part + 1)
        k = slice(part * self.KP, (part + 1) * self.KP)
        self.nc.scalar.activation(self.w_hi[:, k, :], self.w_raw[:, k, :], ACT.Copy).then_inc(self.w_hi_done, 1)

    def split_low(self, pool, n, part):
        reached(pool, self.w_hi_done, self.PARTS * n + part + 1)
        k = slice(part * self.KP, (part + 1) * self.KP)
        self.nc.gpsimd.tensor_tensor(self.w_lo[:, k, :], self.w_raw[:, k, :], self.w_hi[:, k, :].bitcast(F32),
                                     ALU.subtract).then_inc(self.w_lo_done, 1)

    def multiply(self, pe, n, tc, part, low=False):
        if tc == 0:
            reached(pe, self.w_lo_done, self.PARTS * n + part + 1)
        if part == 0:
            reached(pe, self.low_taken if low else self.taken, NTC * n + tc - 1)
        tok, bank = slice(tc * TC, (tc + 1) * TC), self.acc[tc % 2]
        for k in range(part * self.KP, (part + 1) * self.KP):
            self.nc.tensor.matmul(bank[:], self.w_hi[:, k, :], self.hT_hi[:, k, tok], start=k == 0, stop=False)
            self.nc.tensor.matmul(bank[:], self.w_hi[:, k, :], self.hT_lo[:, k, tok], start=False, stop=False)
            mm = self.nc.tensor.matmul(bank[:], self.w_lo[:, k, :], self.hT_hi[:, k, tok], start=False, stop=k == KD - 1)
        mm.then_inc(self.part_done, 1)

    def take(self, act, n, tc, func, rounded=False):
        reached(act, self.part_done, self.ALL * n + self.PARTS * (tc + 1))
        arrived(act, self.stored[tc % 2], 2 * n + tc // 2)
        out = self.out[tc % 2][:]
        self.nc.scalar.activation(out if rounded or out.dtype == F32 else out.bitcast(F32), self.acc[tc % 2][:], func
                                  ).then_inc(self.taken, 1)

    def take_low(self, dve, n, tc):
        s = tc % 2
        reached(dve, self.taken, NTC * n + tc + 1)
        arrived(dve, self.low_stored[s], 2 * n + tc // 2)
        self.nc.vector.tensor_tensor(self.out_lo[s][:], self.acc[s][:], self.out[s][:].bitcast(F32), ALU.subtract
                                     ).then_inc(self.low_taken, 1)

    def store(self, sp, n, tc, cb):
        reached(sp, self.taken, NTC * n + tc + 1)
        out = self.out[tc % 2][:]
        sp.dma_start(self.scr["proj"][bass.ds(cb * P, P), tc * TC:(tc + 1) * TC],
                     out if out.dtype == F32 else out.bitcast(F32)).then_inc(self.stored[tc % 2], 16)

    def store_low(self, sp, n, tc, cb):
        reached(sp, self.low_taken, NTC * n + tc + 1)
        sp.dma_start(self.scr["proj_lo"][bass.ds(cb * P, P), tc * TC:(tc + 1) * TC],
                     self.out_lo[tc % 2][:].bitcast(F32)).then_inc(self.low_stored[tc % 2], 16)


UNITS = [(g, j, b, TC if j < g else (b + 1) * P) for g in range(NTC) for j in range(g, -1, -1) for b in range(4)]
NU = len(UNITS)
STEPS = [(g, j) for g in range(NTC) for j in range(g, -1, -1)]
NS = len(STEPS)
LAG = 2
HITS = 3


def attention_and_gates(nc, sem, g_, w_in, scr):
    with ExitStack() as ctx:
        sb = lambda n, s, d=F32: ctx.enter_context(nc.sbuf_tensor("a_" + n, s, d))
        ps = lambda n, s: ctx.enter_context(nc.psum_tensor("a_" + n, s, F32))
        s_ = lambda n: sem("a_" + n)
        NB = 3 * KD // HEADS
        SLOTS = NB * WovenColumns.ALL
        k_hl = sb("k_hl", [P, T], F32R)
        v_hl = sb("v_hl", [P, T // P, P], F32R)
        q_hl = [sb(f"q_hl{i}", [P, TC], F32R) for i in range(2)]
        q_lh = [sb(f"q_lh{i}", [P, TC], F32R) for i in range(2)]
        miss = [sb(f"miss{i}", [P, TC]) for i in range(2)]
        hit = [sb(f"hit{i}", [P, TC]) for i in range(HITS)]
        left_all = sb("left", [P, 4, TC + 1])
        left = [left_all[:, i, :] for i in range(4)]
        aT_hi = sb("aT_hi", [P, 4, TC], F32R)
        aT_lo = sb("aT_lo", [P, 4, TC], F32R)
        o_hl = sb("o_hl", [P, TC])
        gate = sb("gate", [DH, TC])
        keep, skip = sb("keep", [P, P]), sb("skip", [P, P])
        fold = sb("fold", [P, DH])
        z_ps = [ps(f"z{i}", [P, TC]) for i in range(2)]
        t_ps = [ps(f"t{i}", [P, 4, P]) for i in range(2)]
        o_ps = [ps(f"o{i}", [P, TC]) for i in range(2)]
        gates = WovenColumns(nc, ctx, sem, g_, w_in, scr, "ag_", split=False)
        k_loaded = [s_(f"k_loaded{c}") for c in range(4)]
        v_loaded = [s_(f"v_loaded{c}") for c in range(4)]
        q_loaded = [s_(f"q_loaded{i}") for i in range(2)]
        gate_loaded, y_stored = s_("gate_loaded"), s_("y_stored")
        z_done, sig_done, masked, carried, scanned = s_("z_done"), s_("sig_done"), s_("masked"), s_("carried"), s_("scanned")
        a_done, turned, hi_done, lo_done = s_("a_done"), s_("turned"), s_("hi_done"), s_("lo_done")
        masks_made = s_("masks_made")
        av_done, o_copied, folded, y_done, set_up = s_("av_done"), s_("o_copied"), s_("folded"), s_("y_done"), s_("set_up")
        ident = g_["ident"]
        block = ctx.enter_context(nc.Block())

        def units_until(g):
            return 4 * sum(range(1, g + 1))

        def last_slot(g):
            return units_until(g + 1) - 1 + LAG

        @block.sync
        def _(sp):
            sp.sem_inc(y_stored, 16)
            for s in gates.stored:
                sp.sem_inc(s, 16)

            def load_k(h, c):
                reached(sp, z_done, NU * (h - 1) + 4 * (STEPS.index((NTC - 1, c)) + 1))
                cols, krow = slice(c * TC, (c + 1) * TC), bass.ds(W + h * DH, DH)
                sp.dma_start(k_hl[0:DH, cols].bitcast(F32), scr["proj"][krow, cols]).then_inc(k_loaded[c], 16)
                sp.dma_start(k_hl[DH:P, cols].bitcast(F32), scr["proj_lo"][krow, cols]).then_inc(k_loaded[c], 16)

            def load_v(h, c):
                reached(sp, av_done, NS * (h - 1) + STEPS.index((NTC - 1, c)) + 1)
                cols, rows = slice(c * TC, (c + 1) * TC), bass.ds(h * DH, DH)
                for half, v in ((slice(0, DH), "v_hi"), (slice(DH, P), "v_lo")):
                    sp.dma_start(v_hl[:, 4 * c:4 * c + 4, half].bitcast(F32),
                                 scr[v][cols, rows].rearrange("(b p) d -> p b d", p=P)).then_inc(v_loaded[c], 16)

            def load_q(h, g):
                cols, rows = slice(g * TC, (g + 1) * TC), bass.ds(h * DH, DH)
                reached(sp, z_done, NU * h + units_until(g - 1) if g >= 2 else NU * (h - 1) + units_until(g + 3))
                for tile, first, second in ((q_lh, "proj_lo", "proj"), (q_hl, "proj", "proj_lo")):
                    sp.dma_start(tile[g % 2][0:DH, :].bitcast(F32), scr[first][rows, cols]).then_inc(q_loaded[g % 2], 16)
                    sp.dma_start(tile[g % 2][DH:P, :].bitcast(F32), scr[second][rows, cols]).then_inc(q_loaded[g % 2], 16)

            def load_gate(h, g):
                arrived(sp, y_stored, NTC * h + g)
                sp.dma_start(gate[:], scr["proj"][bass.ds(ZA * P + h * DH, DH), g * TC:(g + 1) * TC]
                             ).then_inc(gate_loaded, 16)

            def store_y(h, g):
                reached(sp, y_done, NTC * h + g + 1)
                sp.dma_start(scr["y"][0, bass.ds(h * DH, DH), g * TC:(g + 1) * TC], gate[:]).then_inc(y_stored, 16)

            load_k(0, 0)
            load_q(0, 0)
            gates.load(sp, 0, GA * P)
            load_v(0, 0)
            load_q(0, 1)
            for c in range(1, 4):
                load_k(0, c)
                load_v(0, c)

            def head(h, more):
                for n in range(SLOTS + 2):
                    if n % WovenColumns.ALL == 2 and n < SLOTS and (more or n < SLOTS - WovenColumns.ALL):
                        b = NB * h + n // WovenColumns.ALL + 1
                        gates.load(sp, b, (GA + b) * P)
                    if n % 4 == 1 and n >= 5:
                        m = (n - 5) // 4
                        b = NB * h + m // NTC
                        gates.store(sp, b, m % NTC, GA + b)
                    if n == 0:
                        load_gate(h, 0)
                    for g in range(NTC):
                        if n == last_slot(g) + 5 or (n == SLOTS + 1 and last_slot(g) + 5 > n):
                            store_y(h, g)
                            if g + 1 < NTC:
                                load_gate(h, g + 1)
                    for g in (2, 3):
                        if n == units_until(g - 1) + 1:
                            load_q(h, g)
                    if more:
                        for g in (0, 1):
                            if n == units_until(g + 3) + 1:
                                load_q(h + 1, g)
                        for c in range(4):
                            step = STEPS.index((NTC - 1, c))
                            if n == 4 * (step + 1) + 1:
                                load_k(h + 1, c)
                            if n == 4 * (step + 1) + LAG + 2:
                                load_v(h + 1, c)

            with sp.Fori(0, HEADS - 1) as h:
                head(h, True)
            head(HEADS - 1, False)
            arrived(sp, y_stored, NTC * HEADS)
            for s in gates.stored:
                arrived(sp, s, 2 * NB * HEADS)

        @block.tensor
        def _(pe):
            for s in (z_done, turned, av_done, folded, gates.part_done):
                pe.sem_inc(s, LEAD)

            def scores(h, u):
                g, j, b, width = UNITS[u]
                if b == 0 and j == g:
                    pe.wait_ge(q_loaded[g % 2], (2 * h + g // 2 + 1) * 64)
                    pe.wait_ge(k_loaded[g], (h + 1) * 32)
                reached(pe, sig_done, NU * h + u - 1)
                for q, first in ((q_hl, True), (q_lh, False)):
                    mm = nc.tensor.matmul(z_ps[u % 2][:, 0:width], q[g % 2][:, b * P:(b + 1) * P],
                                          k_hl[:, j * TC:j * TC + width], start=first, stop=not first)
                mm.then_inc(z_done, 1)

            def turn(h, u):
                width = UNITS[u][3]
                reached(pe, a_done, NU * h + u + 1)
                reached(pe, lo_done, NU * h + u - 1)
                for k in range(width // P):
                    mm = nc.tensor.transpose(t_ps[u % 2][:, k, :], hit[u % HITS][:, k * P:(k + 1) * P], ident[:])
                mm.then_inc(turned, 1)

            def weighted_values(h, s):
                g, j = STEPS[s]
                reached(pe, lo_done, NU * h + 4 * (s + 1))
                if j == g:
                    pe.wait_ge(v_loaded[g], (h + 1) * 32)
                    reached(pe, y_done, NTC * h + g - 1)
                for k in range(4):
                    c0 = k * P if j == g else 0
                    for part in (aT_hi, aT_lo):
                        mm = nc.tensor.matmul(o_ps[g % 2][:, c0:TC], v_hl[:, 4 * j + k, :], part[:, k, c0:TC],
                                              start=j == g and k == 0 and part is aT_hi,
                                              stop=j == 0 and k == 3 and part is aT_lo)
                mm.then_inc(av_done, 1)

            def fold_parts(h, g):
                reached(pe, o_copied, NTC * h + g + 1)
                nc.tensor.matmul(o_ps[g % 2][0:DH, :], fold[:], o_hl[:], start=True, stop=True).then_inc(folded, 1)

            pe.wait_ge(set_up, 5)
            with pe.Fori(0, HEADS) as h:
                for n in range(SLOTS):
                    if n < NU:
                        scores(h, n)
                    gates.multiply(pe, NB * h + n // WovenColumns.ALL, n // 4 % NTC, n % 4)
                    if 0 <= n - LAG < NU:
                        turn(h, n - LAG)
                    v = n - LAG - 1
                    if 0 <= v < NU and v % 4 == 3:
                        weighted_values(h, v // 4)
                    for g in range(NTC):
                        if n == last_slot(g) + 3:
                            fold_parts(h, g)

        @block.scalar
        def _(act):
            for s in (sig_done, hi_done, o_copied, gates.w_hi_done, gates.taken):
                act.sem_inc(s, LEAD)

            def sigmoids(h, u):
                width = UNITS[u][3]
                reached(act, z_done, NU * h + u + 1)
                reached(act, scanned, NU * h + u - 1)
                nc.scalar.activation(miss[u % 2][:, 0:width], z_ps[u % 2][:, 0:width], ACT.Sigmoid, scale=-SCALE)
                reached(act, turned, NU * h + (u - HITS + 1 if u >= HITS else 0))
                nc.scalar.activation(hit[u % HITS][:, 0:width], z_ps[u % 2][:, 0:width], ACT.Sigmoid, scale=SCALE
                                     ).then_inc(sig_done, 1)

            def high(h, u):
                b, width = UNITS[u][2:]
                n = width // P
                reached(act, turned, NU * h + u + 1)
                reached(act, av_done, NS * h + u // 4)
                nc.scalar.activation(aT_hi[:, 0:n, b * P:(b + 1) * P], t_ps[u % 2][:, 0:n, :], ACT.Copy).then_inc(hi_done, 1)

            def copy_o(h, g):
                s = STEPS.index((g, 0))
                reached(act, av_done, NS * h + s + 1)
                reached(act, folded, NTC * h + g)
                nc.scalar.activation(o_hl[:], o_ps[g % 2][:], ACT.Copy).then_inc(o_copied, 1)

            def split(n, part):
                gates.split_high(act, n, part)

            for part in range(4):
                split(0, part)

            def head(h, more):
                for n in range(SLOTS + 1):
                    if n < NU:
                        sigmoids(h, n)
                    if n % 4 == 0 and n >= 4:
                        m = n // 4 - 1
                        gates.take(act, NB * h + m // NTC, m % NTC, ACT.Sigmoid)
                    r = (n - 1) % WovenColumns.ALL - 12
                    if n > 12 and r >= 0 and (more or n < SLOTS - 4):
                        split(NB * h + (n - 1) // WovenColumns.ALL + 1, r)
                    if 0 <= n - LAG < NU:
                        high(h, n - LAG)
                    for g in range(NTC):
                        if n == last_slot(g) + 2:
                            copy_o(h, g)

            with act.Fori(0, HEADS - 1) as h:
                head(h, True)
            head(HEADS - 1, False)

        @block.vector
        def _(dve):
            for s in (masked, carried, scanned, lo_done, y_done):
                dve.sem_inc(s, LEAD)
            nc.vector.tensor_tensor(fold[:], ident[:, 0:DH], ident[:, DH:P], ALU.add).then_inc(set_up, 1)
            for b in range(4):
                nc.vector.memset(left[b], 1.0).then_inc(set_up, 1)
            dve.wait_ge(set_up, 5)
            dve.wait_ge(masks_made, 4)

            diagonals = [u for u in range(NU) if UNITS[u][0] == UNITS[u][1]]
            inner = [u for u in range(NU) if u not in diagonals]

            def scan(h, u):
                g, j, b, width = UNITS[u]
                hit_u = hit[u % HITS]
                if j == g:
                    start = 1.0
                    reached(dve, sig_done, NU * h + u + 1)
                    last = slice(width - P, width)
                    nc.vector.tensor_tensor(miss[u % 2][:, last], miss[u % 2][:, last], skip[:], ALU.max).then_inc(masked, 1)
                    nc.vector.tensor_tensor(hit_u[:, last], hit_u[:, last], keep[:], ALU.mult).then_inc(masked, 1)
                    reached(dve, masked, 2 * (len(diagonals) * h + diagonals.index(u) + 1))
                    reached(dve, a_done, NU * h + u - 3)
                else:
                    start = left[b][:, TC:TC + 1]
                    reached(dve, a_done, NU * h + u - 3)
                    nc.vector.tensor_copy(left[b][:, TC:TC + 1], left[b][:, 0:1]).then_inc(carried, 1)
                    reached(dve, sig_done, NU * h + u + 1)
                    reached(dve, carried, len(inner) * h + inner.index(u) + 1)
                nc.vector.tensor_tensor_scan(left[b][:, 0:width][:, ::-1], miss[u % 2][:, 0:width][:, ::-1],
                                             miss[u % 2][:, 0:width][:, ::-1], start, ALU.mult, ALU.bypass
                                             ).then_inc(scanned, 1)

            def low(h, u):
                b, width = UNITS[u][2:]
                n = width // P
                reached(dve, hi_done, NU * h + u + 1)
                cols = slice(b * P, (b + 1) * P)
                nc.vector.tensor_tensor(aT_lo[:, 0:n, cols], t_ps[u % 2][:, 0:n, :], aT_hi[:, 0:n, cols].bitcast(F32),
                                        ALU.subtract).then_inc(lo_done, 1)

            def gated(h, g):
                reached(dve, folded, NTC * h + g + 1)
                dve.wait_ge(gate_loaded, (NTC * h + g + 1) * 16)
                nc.vector.tensor_tensor(gate[:], o_ps[g % 2][0:DH, :], gate[:], ALU.mult).then_inc(y_done, 1)

            with dve.Fori(0, HEADS) as h:
                for n in range(SLOTS):
                    if n < NU:
                        scan(h, n)
                    if 0 <= n - LAG < NU:
                        low(h, n - LAG)
                    for g in range(NTC):
                        if n == last_slot(g) + 4:
                            gated(h, g)

        @block.gpsimd
        def _(pool):
            for s in (a_done, gates.w_lo_done):
                pool.sem_inc(s, LEAD)
            nc.gpsimd.memset(keep[:], 1.0).then_inc(masks_made, 1)
            nc.gpsimd.memset(skip[:], 0.0).then_inc(masks_made, 1)
            pool.wait_ge(masks_made, 2)
            for tile, fill in ((keep, 0.0), (skip, 1.0)):
                nc.gpsimd.affine_select(out=tile[:], in_=tile[:], compare_op=ALU.is_gt, fill=fill, base=0,
                                        pattern=[[-1, P]], channel_multiplier=1).then_inc(masks_made, 1)

            def weights(h, u):
                b, width = UNITS[u][2:]
                reached(pool, scanned, NU * h + u + 1)
                nc.gpsimd.tensor_tensor(hit[u % HITS][:, 0:width], hit[u % HITS][:, 0:width], left[b][:, 1:width + 1],
                                        ALU.mult).then_inc(a_done, 1)

            for part in range(4):
                gates.split_low(pool, 0, part)

            def head(h, more):
                for n in range(SLOTS + 1):
                    if n < NU:
                        weights(h, n)
                    r = (n - 1) % WovenColumns.ALL - 12
                    if n > 12 and r >= 0 and (more or n < SLOTS - 4):
                        gates.split_low(pool, NB * h + (n - 1) // WovenColumns.ALL + 1, r)

            with pool.Fori(0, HEADS - 1) as h:
                head(h, True)
            head(HEADS - 1, False)


HH = 2
PAIRS = W // P // HH
C = P
NCH = T // C
NCU = NCH * PAIRS
LEVELS = [1 << n for n in range(7)]


def hgrn2_and_columns(nc, sem, g_, w_in, scr, lower_bounds, hgrn_norm_w):
    with ExitStack() as ctx:
        sb = lambda n, s, d=F32: ctx.enter_context(nc.sbuf_tensor("h_" + n, s, d))
        ps = lambda n, s: ctx.enter_context(nc.psum_tensor("h_" + n, s, F32))
        s_ = lambda n: sem("h_" + n)
        NL = len(LEVELS)
        NIN = 2 * NL + 3
        q = [sb(f"q{i}", [P, HH, C]) for i in range(2)]
        pre = [sb(f"pre{i}", [P, HH, C]) for i in range(2)]
        suf = [sb(f"suf{i}", [P, HH, C]) for i in range(2)]
        k = [sb(f"k{i}", [P, HH, C]) for i in range(2)]
        gate = [sb(f"gate{i}", [P, HH, C]) for i in range(2)]
        v = [sb(f"v{i}", [P, HH, C]) for i in range(2)]
        k_left = [sb(f"k_left{n}", [P, HH, C]) for n in range(NL)]
        q_right = [sb(f"q_right{n}", [P, HH * C // 2]) for n in range(NL)]
        part = [sb(f"part{i}", [P, HH, C // 2]) for i in range(2)]
        scores = [sb(f"scores{i}", [P, HH, C]) for i in range(2)]
        q_pre = [sb(f"q_pre{i}", [P, HH, C]) for i in range(2)]
        k_end = sb("k_end", [P, HH, C])
        kT = [sb(f"kT{i}", [P, HH, C]) for i in range(2)]
        state_all = sb("state", [P, PAIRS, HH, C])
        state = [state_all[:, i] for i in range(PAIRS)]
        tot = [sb(f"tot{i}", [P, HH]) for i in range(2)]
        sq = sb("sq", [P, HH, C])
        root = sb("root", [P, HH, C])
        inv = sb("inv", [P, HH, C])
        cols = WovenColumns(nc, ctx, sem, g_, w_in, scr, "hc_", split=True)
        y = [sb(f"y{i}", [P, HH, C]) for i in range(2)]
        mask = [sb(f"mask{n}", [P, C // 2]) for n in range(NL)]
        ones = sb("ones", [P, P])
        eps = sb("eps", [P, 1])
        norm_w = sb("norm_w", [P, 1])
        lb = sb("lb", [P, 6, PAIRS * HH])
        s_ps = [ps(f"s{i}", [P, HH, C]) for i in range(4)]
        kT_ps = ps("kT", [P, HH, C])
        st_ps = ms_ps = kT_ps
        o_ps = ps("o", [P, HH, C])
        par_loaded, set_up, masks_done, lb_done = s_("par_loaded"), s_("set_up"), s_("masks_done"), s_("lb_done")
        front_loaded = [s_(f"front_loaded{i}") for i in range(2)]
        tail_loaded = [s_(f"tail_loaded{i}") for i in range(2)]
        stored = [s_(f"stored{i}") for i in range(2)]
        prep, prepared, level_in, joined = s_("prep"), s_("prepared"), s_("level_in"), s_("joined")
        s_done, parted, added, kT_turned, kT_done = s_("s_done"), s_("parted"), s_("added"), s_("kT_turned"), s_("kT_done")
        st_done, o_done, state_done, sq_done = s_("st_done"), s_("o_done"), s_("state_done"), s_("sq_done")
        ms_done, root_done, inv_done, gated, y_done = s_("ms_done"), s_("root_done"), s_("inv_done"), s_("gated"), s_("y_done")
        ident = g_["ident"]
        block = ctx.enter_context(nc.Block())

        def halves(tile, H):
            return tile[:].rearrange("p h (n two x) -> p (h n) two x", two=2, x=H)

        N_SPLIT = 2 * WB

        def chunks(front, last, eng):
            front(0, 0, None, True, None, None)
            front(0, 1, 0, True, (0, 0), None)
            front(1, 0, 0, True, (0, 1), (0, 0))
            with eng.Fori(1, N_SPLIT) as i:
                front(i, 1, i, True, (i, 0), (i - 1, 1))
                front(i + 1, 0, i, True, (i, 1), (i, 0))
            front(N_SPLIT, 1, N_SPLIT, False, (N_SPLIT, 0), (N_SPLIT - 1, 1))
            front(N_SPLIT + 1, 0, N_SPLIT, False, (N_SPLIT, 1), (N_SPLIT, 0))
            with eng.Fori(N_SPLIT + 1, NCH - 1) as i:
                front(i, 1, i, False, (i, 0), (i - 1, 1))
                front(i + 1, 0, i, False, (i, 1), (i, 0))
            front(NCH - 1, 1, NCH - 1, False, (NCH - 1, 0), (NCH - 2, 1))
            last(NCH - 1)

        @block.sync
        def _(sp):
            for s in (*stored, *cols.stored, *cols.low_stored):
                sp.sem_inc(s, 16)
            with nc.allow_non_contiguous_dma(reason="640 parameters, one to a partition"):
                sp.dma_start(norm_w[:], hgrn_norm_w.rearrange("a p -> p a")).then_inc(par_loaded, 16)
                sp.dma_start(lb[:, 0, :], lower_bounds.rearrange("a (h p) -> p (a h)", p=P)).then_inc(par_loaded, 16)

            def load_front(i, u):
                at = bass.ds(i * C, C)
                reached(sp, level_in, NIN * (2 * i + u - 1))
                for tile, cb in ((q, QB), (pre, FB)):
                    rows = slice((cb + u * HH) * P, (cb + (u + 1) * HH) * P)
                    sp.dma_start(tile[u][:], scr["proj"][rows, at].rearrange("(h p) t -> p h t", p=P)
                                 ).then_inc(front_loaded[u], 16)

            def load_tail(i, u):
                at = bass.ds(i * C, C)
                reached(sp, y_done, 2 * i + u - 1)
                rows = slice((ZB + u * HH) * P, (ZB + (u + 1) * HH) * P)
                sp.dma_start(gate[u][:], scr["proj"][rows, at].rearrange("(h p) t -> p h t", p=P)
                             ).then_inc(tail_loaded[u], 16)
                sp.dma_start(v[u][:], scr["i"][at, u * HH * P:(u + 1) * HH * P].rearrange("t (h d) -> t h d", h=HH)
                             ).then_inc(tail_loaded[u], 16)

            def store(i, u):
                reached(sp, y_done, 2 * i + u + 1)
                sp.dma_start(scr["y"][1, u * HH * P:(u + 1) * HH * P, bass.ds(i * C, C)].rearrange("(h p) t -> p h t", p=P),
                             y[u][:]).then_inc(stored[u], 16)

            def store_columns(i, tc, split):
                cb = QA + i if split else PRE - N_SPLIT + i
                cols.store(sp, i, tc, cb)
                if split:
                    cols.store_low(sp, i, tc, cb)

            load_front(0, 0)
            cols.load(sp, 0, QA * P)
            load_front(0, 1)
            load_tail(0, 0)
            load_tail(0, 1)
            load_front(1, 0)
            cols.load(sp, 1, (QA + 1) * P)

            def chunk(i, split, following, first=False):
                if not first:
                    store(i - 1, 1)
                    load_tail(i, 1)
                store_columns(i, 0, split)
                if following is not False:
                    load_front(i + 1, 1)
                store_columns(i, 1, split)
                store(i, 0)
                if following is not False:
                    load_tail(i + 1, 0)
                store_columns(i, 2, split)
                if following is not None and following is not False:
                    load_front(i + 2, 0)
                if following is not None and following is not False:
                    cols.load(sp, i + 2, following)
                store_columns(i, 3, split)

            chunk(0, True, (QA + 2) * P, first=True)
            with sp.Fori(1, N_SPLIT - 2) as i:
                chunk(i, True, i * P + (QA + 2) * P)
            with sp.Fori(N_SPLIT - 2, N_SPLIT) as i:
                chunk(i, True, i * P + (PRE - N_SPLIT + 2) * P)
            with sp.Fori(N_SPLIT, NCH - 2) as i:
                chunk(i, False, i * P + (PRE - N_SPLIT + 2) * P)
            chunk(NCH - 2, False, None)
            chunk(NCH - 1, False, False)
            store(NCH - 1, 1)
            for s in stored:
                arrived(sp, s, NCH)
            for s in cols.stored:
                arrived(sp, s, 2 * NCH)
            for s in cols.low_stored:
                arrived(sp, s, 2 * N_SPLIT)

        @block.gpsimd
        def _(pool):
            for s in (prep, prepared, added, cols.w_lo_done):
                pool.sem_inc(s, LEAD)
            nc.gpsimd.memset(ones[:], 1.0).then_inc(set_up, 1)
            nc.gpsimd.memset(eps[:], RMS_EPS).then_inc(set_up, 1)
            nc.gpsimd.memset(state_all[:], 0.0).then_inc(set_up, 1)
            for n, H in enumerate(LEVELS):
                nc.gpsimd.memset(k_left[n][:], 0.0).then_inc(set_up, 1)
                nc.gpsimd.memset(mask[n][:], 1.0).then_inc(masks_done, 1)
            pool.wait_ge(masks_done, NL)
            for n, H in enumerate(LEVELS):
                m = mask[n][:].rearrange("p (b x) -> p b x", x=H)
                nc.gpsimd.affine_select(out=m, in_=m, compare_op=ALU.is_ge, fill=0.0, base=0,
                                        pattern=[[-2 * H, C // (2 * H)], [0, H]], channel_multiplier=1).then_inc(masks_done, 1)
                pool.wait_ge(masks_done, NL + 2 * n + 1)
                nc.gpsimd.affine_select(out=m, in_=m, compare_op=ALU.is_ge, fill=0.0, base=H - 1,
                                        pattern=[[2 * H, C // (2 * H)], [0, H]], channel_multiplier=-1).then_inc(masks_done, 1)
            pool.wait_ge(lb_done, 6)

            def prepare_at(i, u):
                c = 2 * i + u
                pool.wait_ge(front_loaded[u], (i + 1) * 32)
                reached(pool, level_in, NIN * (c - 1))
                reached(pool, s_done, (NL + 1) * (c - 2) + 1)
                heads = slice(u * HH, (u + 1) * HH)
                nc.gpsimd.tensor_tensor(pre[u][:], pre[u][:], lb[:, 5, heads].unsqueeze(2).to_broadcast([P, HH, C]), ALU.mult
                                        ).then_inc(prep, 1)
                reached(pool, prep, 2 * c + 1)
                nc.gpsimd.tensor_tensor(pre[u][:], pre[u][:], lb[:, 4, heads].unsqueeze(2).to_broadcast([P, HH, C]), ALU.add
                                        ).then_inc(prep, 1)
                reached(pool, prep, 2 * c + 2)
                nc.gpsimd.tensor_tensor(k[u][:], ones[:].unsqueeze(1).to_broadcast([P, HH, C]), pre[u][:], ALU.subtract
                                        ).then_inc(prepared, 1)
                nc.gpsimd.memset(suf[u][:], 1.0).then_inc(prepared, 1)

            def add_parts(i, u):
                c = 2 * i + u
                for n, H in enumerate(LEVELS):
                    reached(pool, parted, (NL + 1) * c + n + 2)
                    if n:
                        reached(pool, added, NL * c + n)
                    right = halves(scores[u], H)[:, :, 1, :]
                    nc.gpsimd.tensor_tensor(right, right, part[(n + u) % 2][:].rearrange("p h (b x) -> p (h b) x", x=H),
                                            ALU.add).then_inc(added, 1)
                    if n == 4 and u == 0 and not (isinstance(i, int) and i == 0):
                        split_columns(i)

            def split_columns(n):
                for p in range(WovenColumns.PARTS):
                    cols.split_low(pool, n, p)

            prepare_at(0, 0)
            split_columns(0)
            prepare_at(0, 1)
            add_parts(0, 0)
            prepare_at(1, 0)
            add_parts(0, 1)
            with pool.Fori(1, NCH - 1) as i:
                prepare_at(i, 1)
                add_parts(i, 0)
                prepare_at(i + 1, 0)
                add_parts(i, 1)
            prepare_at(NCH - 1, 1)
            add_parts(NCH - 1, 0)
            add_parts(NCH - 1, 1)

        @block.tensor
        def _(pe):
            for s in (s_done, kT_turned, st_done, o_done, ms_done, cols.part_done):
                pe.sem_inc(s, LEAD)
            pe.wait_ge(set_up, 3 + NL)

            def multiply(half, n, b, split):
                if b is not None:
                    r = 2 * WovenColumns.PARTS * half + n
                    low = split or (isinstance(b, int) and b == N_SPLIT and r // 4 < 2)
                    cols.multiply(pe, b, r // 4, r % 4, low=low)

            def chunk_state(i, u):
                c = 2 * i + u
                pe.wait_ge(tail_loaded[u], (i + 1) * 32)
                reached(pe, kT_done, c + 1)
                for h in range(HH):
                    mm = nc.tensor.matmul(st_ps[:, h, :], kT[u][:, h, :], v[u][:, h, :], start=True, stop=True)
                mm.then_inc(st_done, 1)

            def outputs(i, u):
                c = 2 * i + u
                reached(pe, added, NL * (c + 1))
                reached(pe, state_done, HH * c)
                reached(pe, gated, c)
                for h in range(HH):
                    nc.tensor.matmul(o_ps[:, h, :], v[u][:, h, :], scores[u][:, h, :], start=True, stop=False)
                    mm = nc.tensor.matmul(o_ps[:, h, :], state[u][:, h, :], q_pre[u][:, h, :], start=False, stop=True)
                mm.then_inc(o_done, 1)

            def square_sums(i, u):
                c = 2 * i + u
                reached(pe, sq_done, c + 1)
                reached(pe, state_done, HH * (c + 1))
                nc.tensor.matmul(ms_ps[:], ones[:], sq[:], start=True, stop=True).then_inc(ms_done, 1)

            def front(i, u, b, split, before, before2):
                c = 2 * i + u
                for n in range(NL + 1):
                    if n == 0:
                        reached(pe, prepared, 2 * (c + 1))
                    else:
                        reached(pe, level_in, NIN * c + 2 * n)
                    reached(pe, parted, (NL + 1) * c + n - 3)
                    for h in range(HH):
                        if n == 0:
                            mm = nc.tensor.matmul(s_ps[n % 4][:, h, :], k[u][:, h, :], q[u][:, h, :], start=True, stop=True)
                        else:
                            mm = nc.tensor.matmul(s_ps[n % 4][:, h, 0:C // 2], k_left[n - 1][:, h, :],
                                                  q_right[n - 1][:, h * C // 2:(h + 1) * C // 2], start=True, stop=True)
                    mm.then_inc(s_done, 1)
                    if before is not None:
                        if n == 1:
                            chunk_state(*before)
                        elif n == 4:
                            outputs(*before)
                        elif n == NL:
                            square_sums(*before)
                    multiply(1 - u, n, b, split)
                reached(pe, level_in, NIN * (c + 1))
                reached(pe, root_done, c)
                for h in range(HH):
                    mm = nc.tensor.transpose(kT_ps[:, h, :], k_end[:, h, :], ident[:])
                mm.then_inc(kT_turned, 1)

            def last(i):
                for n in range(NL + 1):
                    if n == 1:
                        chunk_state(i, 1)
                    elif n == 4:
                        outputs(i, 1)
                    elif n == NL:
                        square_sums(i, 1)
                    multiply(1, n, i, False)

            chunks(front, last, pe)

        @block.scalar
        def _(act):
            for s in (kT_done, sq_done, root_done, cols.w_hi_done, cols.taken):
                act.sem_inc(s, LEAD)
            act.wait_ge(par_loaded, 32)
            act.wait_ge(lb_done, 1)
            nc.scalar.activation(lb[:, 1, :], lb[:, 2, :], ACT.Exp).then_inc(lb_done, 1)
            act.wait_ge(set_up, 3 + NL)

            def split_columns(n):
                for p in range(WovenColumns.PARTS):
                    cols.split_high(act, n, p)

            def square(i, u):
                c = 2 * i + u
                reached(act, o_done, c + 1)
                reached(act, ms_done, c)
                nc.scalar.activation(sq[:], o_ps[:], ACT.Square).then_inc(sq_done, 1)

            def take_root(i, u):
                c = 2 * i + u
                reached(act, ms_done, c + 1)
                reached(act, inv_done, c)
                nc.scalar.activation(root[:], ms_ps[:], ACT.Sqrt, scale=1.0 / C, bias=eps[:]).then_inc(root_done, 1)

            def woven(b, half, split, before, more):
                if b is not None:
                    cols.take(act, b, 2 * half, ACT.Copy, rounded=split)
                if before is not None:
                    square(*before)
                if half == 1 and more and b is not None:
                    for p in range(3):
                        cols.split_high(act, b + 1, p)
                if before is not None:
                    take_root(*before)
                if half == 1 and more and b is not None:
                    cols.split_high(act, b + 1, 3)
                if b is not None:
                    cols.take(act, b, 2 * half + 1, ACT.Copy, rounded=split)

            def front(i, u, b, split, before, before2):
                c = 2 * i + u
                woven(b, 1 - u, split, before, True)
                reached(act, kT_turned, c + 1)
                reached(act, st_done, c - 1)
                nc.scalar.activation(kT[u][:], kT_ps[:], ACT.Copy).then_inc(kT_done, 1)

            def last(i):
                woven(i, 1, False, (i, 1), False)

            split_columns(0)
            chunks(front, last, act)

        @block.vector
        def _(dve):
            for s in (level_in, joined, parted, state_done, inv_done, gated, y_done, cols.low_taken):
                dve.sem_inc(s, LEAD)
            dve.wait_ge(par_loaded, 32)
            nc.vector.tensor_tensor(lb[:, 2, :], lb[:, 0, :], lb[:, 0, :], ALU.subtract).then_inc(lb_done, 1)
            dve.wait_ge(lb_done, 2)
            nc.vector.reciprocal(lb[:, 3, :], lb[:, 1, :]).then_inc(lb_done, 1)
            dve.wait_ge(lb_done, 3)
            nc.vector.tensor_tensor(lb[:, 1, :], lb[:, 1, :], lb[:, 3, :], ALU.mult).then_inc(lb_done, 1)
            dve.wait_ge(lb_done, 4)
            nc.vector.tensor_tensor(lb[:, 4, :], lb[:, 1, :], lb[:, 1, :], ALU.subtract).then_inc(lb_done, 1)
            dve.wait_ge(lb_done, 5)
            nc.vector.tensor_scalar(lb[:, 5, :], lb[:, 4, :], -1.0, 1.0, ALU.mult, ALU.add).then_inc(lb_done, 1)
            dve.wait_ge(set_up, 3 + NL)
            dve.wait_ge(masks_done, 3 * NL)

            def take_part(c, u, n):
                reached(dve, s_done, (NL + 1) * c + n + 1)
                bank = s_ps[n % 4][:]
                if n == 0:
                    reached(dve, o_done, c - 1)
                    nc.vector.tensor_tensor(scores[u][:], bank, ident[:].unsqueeze(1).to_broadcast([P, HH, C]),
                                            ALU.mult).then_inc(parted, 1)
                else:
                    reached(dve, added, NL * c + n - 2)
                    nc.vector.tensor_tensor(part[(n - 1 + u) % 2][:], bank[:, :, 0:C // 2],
                                            mask[n - 1][:].unsqueeze(1).to_broadcast([P, HH, C // 2]),
                                            ALU.mult).then_inc(parted, 1)

            def update_state(i, u):
                c = 2 * i + u
                reached(dve, st_done, c + 1)
                reached(dve, o_done, c + 1)
                for h in range(HH):
                    nc.vector.scalar_tensor_tensor(state[u][:, h, :], state[u][:, h, :], tot[u][:, h:h + 1],
                                                   st_ps[:, h, :], ALU.mult, ALU.add).then_inc(state_done, 1)

            def weigh(i, u):
                c = 2 * i + u
                dve.wait_ge(tail_loaded[u], (i + 1) * 32)
                reached(dve, sq_done, c + 1)
                nc.vector.scalar_tensor_tensor(gate[u][:], o_ps[:], norm_w[:, 0:1], gate[u][:], ALU.mult, ALU.mult
                                               ).then_inc(gated, 1)

            def invert(i, u):
                c = 2 * i + u
                reached(dve, root_done, c + 1)
                reached(dve, y_done, c)
                nc.vector.reciprocal(inv[:], root[:]).then_inc(inv_done, 1)

            def normalise(i, u):
                c = 2 * i + u
                reached(dve, inv_done, c + 1)
                reached(dve, gated, c + 1)
                arrived(dve, stored[u], i)
                nc.vector.tensor_tensor(y[u][:], gate[u][:], inv[:], ALU.mult).then_inc(y_done, 1)

            def front(i, u, b, split, before, before2):
                c = 2 * i + u
                reached(dve, prepared, 2 * (c + 1))
                for n, H in enumerate(LEVELS):
                    reached(dve, s_done, (NL + 1) * (c - 1) + n + 2)
                    if n:
                        reached(dve, joined, 2 * NL * c + 2 * n - 1)
                    kl, kk, ss, pp, qq = (halves(x, H) for x in (k_left[n], k[u], suf[u], pre[u], q[u]))
                    nc.vector.tensor_tensor(kl[:, :, 0, :], kk[:, :, 0, :], ss[:, :, 0, :], ALU.mult).then_inc(level_in, 1)
                    if n:
                        reached(dve, joined, 2 * NL * c + 2 * n)
                    nc.vector.tensor_tensor(q_right[n][:].rearrange("p (b x) -> p b x", x=H), qq[:, :, 1, :], pp[:, :, 1, :],
                                            ALU.mult).then_inc(level_in, 1)
                    nb = HH * C // (2 * H)
                    nc.vector.tensor_tensor(ss[:, :, 0, :], ss[:, :, 0, :], pp[:, :, 1, H - 1:H].to_broadcast([P, nb, H]),
                                            ALU.mult).then_inc(joined, 1)
                    if n >= 2:
                        take_part(c, u, n - 2)
                    elif before is not None:
                        take_part(c - 1, 1 - u, NL - 1 + n)
                    reached(dve, joined, 2 * NL * c + 2 * n + 1)
                    nc.vector.tensor_tensor(pp[:, :, 1, :], pp[:, :, 1, :], pp[:, :, 0, H - 1:H].to_broadcast([P, nb, H]),
                                            ALU.mult).then_inc(joined, 1)
                    if before is not None:
                        if n == 5:
                            update_state(*before)
                        elif n == 6:
                            weigh(*before)
                    if before2 is not None:
                        if n == 1:
                            invert(*before2)
                        elif n == 2:
                            normalise(*before2)
                    if n == 2 and before2 is not None:
                        if u == 0 and split:
                            cols.take_low(dve, b, 1)
                        elif u == 1 and (split or (isinstance(b, int) and b == N_SPLIT)):
                            cols.take_low(dve, b - 1, 3)
                    if b is not None and split and n == 5:
                        cols.take_low(dve, b, 2 * (1 - u))
                reached(dve, joined, 2 * NL * (c + 1))
                reached(dve, kT_turned, c)
                nc.vector.tensor_tensor(k_end[:], k[u][:], suf[u][:], ALU.mult).then_inc(level_in, 1)
                reached(dve, o_done, c - 1)
                nc.vector.tensor_tensor(q_pre[u][:], q[u][:], pre[u][:], ALU.mult).then_inc(level_in, 1)
                nc.vector.tensor_copy(tot[u][:], pre[u][:, :, C - 1]).then_inc(level_in, 1)
                take_part(c, u, NL - 2)

            def last(i):
                reached(dve, level_in, NIN * NCU)
                take_part(NCU - 1, 1, NL - 1)
                invert(i, 0)
                normalise(i, 0)
                take_part(NCU - 1, 1, NL)
                update_state(i, 1)
                weigh(i, 1)
                invert(i, 1)
                normalise(i, 1)

            chunks(front, last, dve)


def conv_and_merge(nc, sem, scr, conv_w, w_branch):
    with ExitStack() as ctx:
        sb = lambda n, s, d=F32: ctx.enter_context(nc.sbuf_tensor("m_" + n, s, d))
        s_ = lambda n: sem("m_" + n)
        NB, NM = 3, D // P
        RAW = 3
        BY_DVE = WB + 1
        w_raw = [sb(f"w_raw{i}", [P, D]) for i in range(RAW)]
        w_hi = sb("w_hi", [P, NB * WB, D], F32R)
        w_lo = sb("w_lo", [P, NB * WB, D], F32R)
        y_raw = sb("y_raw", [P, WB, TC])
        y_conv = sb("y_conv", [P, WB, TC])
        TAPS = 3
        pre, u_, post, z = (sb(n, [P, TC]) for n in ("pre", "u", "post", "z"))
        prod = sb("prod", [P, TAPS - 1 + TC])
        halo = sb("halo", [P, WB, TAPS - 1])
        taps = sb("taps", [P, TAPS, WB])
        y_hi = [sb(f"y_hi{b}", [P, WB, TC], F32R) for b in range(NB)]
        y_lo = [sb(f"y_lo{b}", [P, WB, TC], F32R) for b in range(NB)]
        gate = [sb(f"gate{i}", [P, TC]) for i in range(4)]
        total = sb("total", [P, NM, TC])
        acc = [ctx.enter_context(nc.psum_tensor(f"m_acc{i}", [P, TC], F32)) for i in range(4)]
        w_loaded = [s_(f"w_loaded{i}") for i in range(RAW)]
        w_hi_done, w_lo_done = s_("w_hi_done"), s_("w_lo_done")
        y_loaded, y_hi_done, y_lo_done = s_("y_loaded"), s_("y_hi_done"), s_("y_lo_done")
        g_loaded = [s_(f"g_loaded{i}") for i in range(4)]
        acc_done, gated, summed = s_("acc_done"), s_("gated"), s_("summed")
        halo_zero = s_("halo_zero")
        y0_hi_done, y0_lo_done = s_("y0_hi_done"), s_("y0_lo_done")
        taps_loaded, conv_loaded, post_done, conv_step = s_("taps_loaded"), s_("conv_loaded"), s_("post_done"), s_("conv_step")
        CONV_STEPS = 7
        stored = [s_(f"stored{i}") for i in range(2)]
        HALF = NM // 2
        block = ctx.enter_context(nc.Block())
        PER = NB * NM
        SUMS = (NB - 1) * NM

        @block.sync
        def _(sp):
            for s in stored:
                sp.sem_inc(s, 16)

            def load_y(tc, b):
                reached(sp, y_lo_done, NB * tc + 1 if b else NB * tc - 1)
                sp.dma_start(y_raw[:], scr["y"][b, :, bass.ds(tc * TC, TC)].rearrange("(k p) t -> p k t", p=P)
                             ).then_inc(y_loaded, 16)

            def load_conv(tc, k):
                reached(sp, conv_step, CONV_STEPS * (WB * tc + k))
                for tile, cb in ((pre, PRE), (u_, UC), (post, POST), (z, ZC)):
                    sp.dma_start(tile[:], scr["proj"][(cb + k) * P:(cb + k + 1) * P, bass.ds(tc * TC, TC)]
                                 ).then_inc(conv_loaded, 16)

            def load_gate(tc, b, m):
                last = NM * b + m - 4
                if 0 <= last < NM:
                    reached(sp, gated, PER * tc + last + 1)
                else:
                    reached(sp, summed, SUMS * (tc if last > 0 else tc - 1) + (last % PER) - NM + 1)
                sp.dma_start(gate[m % 4][:], scr["proj"][(GA + NM * b + m) * P:(GA + NM * b + m + 1) * P,
                                                         bass.ds(tc * TC, TC)]).then_inc(g_loaded[m % 4], 16)

            def store_half(tc, half):
                reached(sp, summed, SUMS * tc + NM + HALF * (half + 1))
                rows = slice(half * HALF * P, (half + 1) * HALF * P)
                sp.dma_start(scr["m"][rows, bass.ds(tc * TC, TC)].rearrange("(m p) t -> p m t", p=P),
                             total[:, half * HALF:(half + 1) * HALF, :]).then_inc(stored[half], 16)

            def group(tc, first, more):
                for b in range(NB):
                    for m in range(NM):
                        p = NM * b + m
                        if p == 4 and not first:
                            store_half(tc - 1, 1)
                        if more and p in (12, 16, 20):
                            load_conv(tc + 1, (p - 12) // 4)
                        if first and p in (5, 7, 9):
                            load_conv(tc, (p - 3) // 2)
                        load_gate(tc, b, m)
                    if more and b < 2:
                        load_y(tc + 1, b)
                store_half(tc, 0)
                if more:
                    load_conv(tc + 1, 3)

            load_y(0, 0)
            with nc.allow_non_contiguous_dma(reason="1536 taps, one to a partition"):
                for n in range(TAPS):
                    sp.dma_start(taps[:, n, :], conv_w[0, n:n + 1].rearrange("a (b p) -> p (a b)", p=P)
                                 ).then_inc(taps_loaded, 16)
            load_conv(0, 0)
            load_y(0, 1)
            group(0, True, True)
            with sp.Fori(1, NTC - 1) as tc:
                group(tc, False, True)
            group(NTC - 1, False, False)
            store_half(NTC - 1, 1)
            for s in stored:
                arrived(sp, s, NTC)

        @block.tensor
        def _(pe):
            pe.sem_inc(acc_done, LEAD)

            def product(b, m, k):
                wk, cols = WB * b + k, slice(m * P, (m + 1) * P)
                nc.tensor.matmul(acc[m % 4][:], w_hi[:, wk, cols], y_hi[b][:, k, :], start=k == 0, stop=False)
                nc.tensor.matmul(acc[m % 4][:], w_hi[:, wk, cols], y_lo[b][:, k, :], start=False, stop=False)
                mm = nc.tensor.matmul(acc[m % 4][:], w_lo[:, wk, cols], y_hi[b][:, k, :], start=False, stop=k == WB - 1)
                if k == WB - 1:
                    mm.then_inc(acc_done, 1)

            def group(tc, first):
                for b in range(NB):
                    if not (first and b == 0):
                        reached(pe, y_lo_done, NB * tc + b + 1)
                    else:
                        for k in range(WB):
                            if k < WB - 1:
                                pe.wait_ge(y0_lo_done, k + 1)
                            else:
                                reached(pe, y_lo_done, 1)
                            reached(pe, w_lo_done, k + 1)
                            for m in range(4):
                                product(b, m, k)
                    for m in range(4 if first and b == 0 else 0, NM):
                        reached(pe, gated, PER * tc + NM * b + m - 3)
                        for k in range(WB):
                            if first and m == 0 and b:
                                reached(pe, w_lo_done, WB * b + k + 1)
                            product(b, m, k)

            group(0, True)
            with pe.Fori(1, NTC) as tc:
                group(tc, False)

        @block.scalar
        def _(act):
            for s in (w_hi_done, y_hi_done):
                act.sem_inc(s, LEAD)

            def split_y(tc, b):
                if b < 2:
                    act.wait_ge(y_loaded, (2 * tc + b + 1) * 16)
                else:
                    reached(act, conv_step, CONV_STEPS * WB * (tc + 1))
                reached(act, acc_done, PER * (tc - 1) + NM * (b + 1))
                nc.scalar.activation(y_hi[b][:], (y_raw if b < 2 else y_conv)[:], ACT.Copy
                                     ).then_inc(y_hi_done, 1)

            def split_w(k):
                act.wait_ge(w_loaded[k % RAW], 16 * (k // RAW + 1))
                nc.scalar.activation(w_hi[:, k, :], w_raw[k % RAW][:], ACT.Copy).then_inc(w_hi_done, 1)

            def load_w(k):
                reached(act, w_lo_done, k - RAW + 1)
                nc.scalar.dma_start(w_raw[k % RAW][:], w_branch[0, k // WB, (k % WB) * P:(k % WB + 1) * P, :]
                                    ).then_inc(w_loaded[k % RAW], 16)

            for k in range(RAW):
                load_w(k)
            act.wait_ge(y_loaded, 16)
            for k in range(WB):
                nc.scalar.activation(y_hi[0][:, k, :], y_raw[:, k, :], ACT.Copy
                                     ).then_inc(y0_hi_done if k < WB - 1 else y_hi_done, 1)
                split_w(k)
                load_w(k + RAW)
            for k in range(WB, NB * WB):
                split_w(k)
                if k + RAW < NB * WB:
                    load_w(k + RAW)
                if k == BY_DVE:
                    split_y(0, 1)
            split_y(0, 2)
            with act.Fori(1, NTC) as tc:
                for b in range(NB):
                    split_y(tc, b)

        @block.gpsimd
        def _(pool):
            for s in (w_lo_done, y_lo_done):
                pool.sem_inc(s, LEAD)

            def split_y(n, b):
                reached(pool, y_hi_done, n + 1)
                nc.gpsimd.tensor_tensor(y_lo[b][:], (y_raw if b < 2 else y_conv)[:], y_hi[b][:].bitcast(F32), ALU.subtract
                                        ).then_inc(y_lo_done, 1)

            def conv_gate(tc, k):
                pool.wait_ge(conv_loaded, (WB * tc + k + 1) * 64)
                nc.gpsimd.tensor_tensor(post[:], post[:], z[:], ALU.mult).then_inc(post_done, 1)

            reached(pool, w_lo_done, BY_DVE)
            for k in range(BY_DVE, NB * WB):
                reached(pool, w_hi_done, k + 1)
                nc.gpsimd.tensor_tensor(w_lo[:, k, :], w_raw[k % RAW][:], w_hi[:, k, :].bitcast(F32), ALU.subtract
                                        ).then_inc(w_lo_done, 1)
                if k < BY_DVE + WB:
                    conv_gate(0, k - BY_DVE)
                if k == BY_DVE:
                    split_y(1, 1)

            def group(tc):
                if isinstance(tc, int) and tc == 0:
                    reached(pool, y_lo_done, NB)
                else:
                    split_y(NB * tc + 2, 2)
                for b in range(2):
                    split_y(NB * (tc + 1) + b, b)
                    for k in range(2 * b, 2 * b + 2):
                        conv_gate(tc + 1, k)

            group(0)
            with pool.Fori(1, NTC - 1) as tc:
                group(tc)
            split_y(NB * NTC - 1, 2)

        @block.vector
        def _(dve):
            for s in (gated, summed, conv_step):
                dve.sem_inc(s, LEAD)

            def convolve(tc, k):
                n = WB * tc + k
                done = CONV_STEPS * n
                dve.wait_ge(conv_loaded, (n + 1) * 64)
                reached(dve, conv_step, done)
                nc.vector.tensor_copy(prod[:, 0:TAPS - 1], halo[:, k, :]).then_inc(conv_step, 1)
                nc.vector.tensor_tensor(prod[:, TAPS - 1:], pre[:], u_[:], ALU.mult).then_inc(conv_step, 1)
                reached(dve, conv_step, done + 2)
                nc.vector.tensor_copy(halo[:, k, :], prod[:, TC:]).then_inc(conv_step, 1)
                reached(dve, y_lo_done, NB * tc)
                nc.vector.tensor_scalar(y_conv[:, k, :], prod[:, 0:TC], taps[:, 0, k:k + 1], None, ALU.mult
                                        ).then_inc(conv_step, 1)
                for t in range(1, TAPS):
                    reached(dve, conv_step, done + 3 + t)
                    nc.vector.scalar_tensor_tensor(y_conv[:, k, :], prod[:, t:t + TC], taps[:, t, k:k + 1], y_conv[:, k, :],
                                                   ALU.mult, ALU.add).then_inc(conv_step, 1)
                reached(dve, conv_step, done + 3 + TAPS)
                dve.wait_ge(post_done, n + 1)
                nc.vector.tensor_tensor(y_conv[:, k, :], y_conv[:, k, :], post[:], ALU.mult).then_inc(conv_step, 1)

            def split_w(k):
                reached(dve, w_hi_done, k + 1)
                nc.vector.tensor_tensor(w_lo[:, k, :], w_raw[k % RAW][:], w_hi[:, k, :].bitcast(F32), ALU.subtract
                                        ).then_inc(w_lo_done, 1)

            nc.vector.memset(halo[:], 0.0).then_inc(halo_zero, 1)
            for k in range(WB):
                if k < WB - 1:
                    dve.wait_ge(y0_hi_done, k + 1)
                else:
                    reached(dve, y_hi_done, 1)
                nc.vector.tensor_tensor(y_lo[0][:, k, :], y_raw[:, k, :], y_hi[0][:, k, :].bitcast(F32), ALU.subtract
                                        ).then_inc(y0_lo_done if k < WB - 1 else y_lo_done, 1)
                split_w(k)
            for k in range(WB, BY_DVE):
                split_w(k)
            dve.wait_ge(halo_zero, 1)
            dve.wait_ge(taps_loaded, 16 * TAPS)

            def group(tc, first, more):
                for b in range(NB):
                    for m in range(NM + 1):
                        if m < NM:
                            n = PER * tc + NM * b + m
                            reached(dve, acc_done, n + 1)
                            dve.wait_ge(g_loaded[m % 4], (tc * (PER // 4) + (NM * b + m) // 4 + 1) * 16)
                            if b == 0:
                                if m % HALF == 0:
                                    arrived(dve, stored[m // HALF], tc)
                                nc.vector.tensor_tensor(total[:, m, :], acc[m % 4][:], gate[m % 4][:], ALU.mult
                                                        ).then_inc(gated, 1)
                            else:
                                nc.vector.tensor_tensor(gate[m % 4][:], acc[m % 4][:], gate[m % 4][:], ALU.mult
                                                        ).then_inc(gated, 1)
                        if m > 0 and b > 0:
                            n = PER * tc + NM * b + m - 1
                            reached(dve, gated, n + 1)
                            nc.vector.tensor_tensor(total[:, m - 1, :], total[:, m - 1, :], gate[(m - 1) % 4][:], ALU.add
                                                    ).then_inc(summed, 1)
                        if more and NM * b + m in (11, 15, 19, 23) and m < NM:
                            convolve(tc + 1, (NM * b + m - 11) // 4)
                        if first and NM * b + m in (3, 5, 7, 9) and m < NM:
                            convolve(tc, (NM * b + m - 3) // 2)
                        if first and b == 1 and m == 2:
                            reached(dve, y_hi_done, NB)
                            nc.vector.tensor_tensor(y_lo[2][:], y_conv[:], y_hi[2][:].bitcast(F32), ALU.subtract
                                                    ).then_inc(y_lo_done, 1)

            group(0, True, True)
            with dve.Fori(1, NTC - 1) as tc:
                group(tc, False, True)
            group(NTC - 1, False, False)


def project_out(nc, sem, scr, w_out, ln_g, ln_b, x, out):
    with ExitStack() as ctx:
        sb = lambda n, s, d=F32: ctx.enter_context(nc.sbuf_tensor("o_" + n, s, d))
        s_ = lambda n: sem("o_" + n)
        TG = 256
        NG, HALF = T // TG, D // 2
        w_raw = [sb(f"w_raw{i}", [P, D]) for i in range(2)]
        w_hi = sb("w_hi", [P, KD, D], F32R)
        w_lo = sb("w_lo", [P, KD, D], F32R)
        m_raw = sb("m_raw", [P, KD, TG])
        m_hi = [sb(f"m_hi{i}", [P, KD, TG], F32R) for i in range(2)]
        m_lo = [sb(f"m_lo{i}", [P, KD, TG], F32R) for i in range(2)]
        gate, gam, bet = sb("gate", [P, D]), sb("gam", [P, D]), sb("bet", [P, D])
        xt = [sb(f"xt{i}", [P, D]) for i in range(2)]
        r = [sb(f"r{i}", [P, D]) for i in range(2)]
        o = [sb(f"o{i}", [P, D]) for i in range(2)]
        stats = sb("stats", [P, 12])
        count = sb("count", [P, 1])
        mv = sb("mv", [P, 2])
        small = sb("small", [P, 3])
        acc = [ctx.enter_context(nc.psum_tensor(f"o_acc{i}", [P, HALF], F32)) for i in range(4)]
        par_loaded = s_("par_loaded")
        w_loaded = [s_(f"w_loaded{i}") for i in range(2)]
        m_loaded = s_("m_loaded")
        x_loaded = [s_(f"x_loaded{i}") for i in range(2)]
        stored = [s_(f"stored{i}") for i in range(2)]
        w_hi_done, m_hi_done, m_lo_done = s_("w_hi_done"), s_("m_hi_done"), s_("m_lo_done")
        w_lo_done = [s_("w_lo_even"), s_("w_lo_odd")]
        m0_hi_done, m0_lo_done = s_("m0_hi_done"), s_("m0_lo_done")
        acc_done, scaled, summed, stats_done, mv_done = s_("acc_done"), s_("scaled"), s_("summed"), s_("stats_done"), s_("mv_done")
        ve_done, std_done, rstd_done, xhat_done, gam_done, bet_done = (
            s_(n) for n in ("ve_done", "std_done", "rstd_done", "xhat_done", "gam_done", "bet_done"))
        block = ctx.enter_context(nc.Block())

        @block.sync
        def _(sp):
            for s in (*stored, *x_loaded):
                sp.sem_inc(s, 16)

            def load_m(i):
                reached(sp, m_lo_done, i)
                sp.dma_start(m_raw[:], scr["m"][:, bass.ds(i * TG, TG)].rearrange("(k p) t -> p k t", p=P)
                             ).then_inc(m_loaded, 16)

            def load_x(i, u):
                reached(sp, summed, 2 * (2 * i + u - 1))
                sp.dma_start(xt[u][:], x[bass.ds((2 * i + u) * P, P), :]).then_inc(x_loaded[u], 16)

            load_m(0)
            load_m(1)
            sp.dma_start(gate[:], scr["gate"][0].partition_broadcast(P)).then_inc(par_loaded, 16)
            sp.dma_start(gam[:], ln_g[0].partition_broadcast(P)).then_inc(par_loaded, 16)
            sp.dma_start(bet[:], ln_b[0].partition_broadcast(P)).then_inc(par_loaded, 16)
            load_x(0, 0)
            load_x(0, 1)

            def group(i, more, x_more):
                if more:
                    load_m(i + 2)
                for u in range(2):
                    reached(sp, bet_done, 2 * i + u + 1)
                    sp.dma_start(out[0, bass.ds((2 * i + u) * P, P), :], o[u][:]).then_inc(stored[u], 16)
                    if x_more:
                        load_x(i + 1, u)

            with sp.Fori(0, NG - 2) as i:
                group(i, True, True)
            group(NG - 2, False, True)
            group(NG - 1, False, False)
            for s in stored:
                arrived(sp, s, NG)

        @block.tensor
        def _(pe):
            pe.sem_inc(acc_done, LEAD)

            def group(i, s):
                for u in range(2):
                    for half in range(2):
                        n = 8 * i + 4 * s + 2 * u + half
                        reached(pe, scaled, n - 3)
                        bank = acc[2 * u + half]
                        cols, tok = slice(half * HALF, (half + 1) * HALF), slice(u * P, (u + 1) * P)
                        if u == 0 and half == 0:
                            reached(pe, m_lo_done, 2 * i + s + 1)
                        for k in range(KD):
                            nc.tensor.matmul(bank[:], m_hi[s][:, k, tok], w_hi[:, k, cols], start=k == 0, stop=False)
                            nc.tensor.matmul(bank[:], m_hi[s][:, k, tok], w_lo[:, k, cols], start=False, stop=False)
                            mm = nc.tensor.matmul(bank[:], m_lo[s][:, k, tok], w_hi[:, k, cols],
                                                  start=False, stop=k == KD - 1)
                        mm.then_inc(acc_done, 1)

            for k in range(KD):
                if k % 2 == 0:
                    if k < KD - 2:
                        pe.wait_ge(m0_lo_done, k // 2 + 1)
                    else:
                        reached(pe, m_lo_done, 1)
                pe.wait_ge(w_lo_done[k % 2], k // 2 + 1)
                for u in range(2):
                    for half in range(2):
                        bank, cols, tok = acc[2 * u + half], slice(half * HALF, (half + 1) * HALF), slice(u * P, (u + 1) * P)
                        nc.tensor.matmul(bank[:], m_hi[0][:, k, tok], w_hi[:, k, cols], start=k == 0, stop=False)
                        nc.tensor.matmul(bank[:], m_hi[0][:, k, tok], w_lo[:, k, cols], start=False, stop=False)
                        mm = nc.tensor.matmul(bank[:], m_lo[0][:, k, tok], w_hi[:, k, cols], start=False, stop=k == KD - 1)
                        if k == KD - 1:
                            mm.then_inc(acc_done, 1)
            group(0, 1)
            with pe.Fori(1, NG // 2) as i:
                group(i, 0)
                group(i, 1)

        @block.scalar
        def _(act):
            for s in (w_hi_done, m_hi_done, std_done):
                act.sem_inc(s, LEAD)

            def split_m(i, s):
                act.wait_ge(m_loaded, (2 * i + s + 1) * 16)
                reached(act, acc_done, 4 * (2 * i + s) - 4)
                nc.scalar.activation(m_hi[s][:], m_raw[:], ACT.Copy).then_inc(m_hi_done, 1)

            def roots(i, s):
                for u in range(2):
                    n = 4 * i + 2 * s + u
                    reached(act, ve_done, n + 1)
                    nc.scalar.activation(small[:, 1:2], small[:, 0:1], ACT.Sqrt).then_inc(std_done, 1)

            def load_w(k):
                if k >= 2:
                    act.wait_ge(w_lo_done[k % 2], k // 2)
                nc.scalar.dma_start(w_raw[k % 2][:], w_out[0, k * P:(k + 1) * P, :]).then_inc(w_loaded[k % 2], 16)

            load_w(0)
            load_w(1)
            act.wait_ge(m_loaded, 16)
            for k in range(KD):
                if k % 2 == 0:
                    nc.scalar.activation(m_hi[0][:, k:k + 2, :], m_raw[:, k:k + 2, :], ACT.Copy
                                         ).then_inc(m0_hi_done if k < KD - 2 else m_hi_done, 1)
                act.wait_ge(w_loaded[k % 2], 16 * (k // 2 + 1))
                nc.scalar.activation(w_hi[:, k, :], w_raw[k % 2][:], ACT.Copy).then_inc(w_hi_done, 1)
                if k + 2 < KD:
                    load_w(k + 2)
            with act.Fori(0, NG // 2 - 1) as i:
                split_m(i, 1)
                roots(i, 0)
                split_m(i + 1, 0)
                roots(i, 1)
            split_m(NG // 2 - 1, 1)
            roots(NG // 2 - 1, 0)
            roots(NG // 2 - 1, 1)

        @block.gpsimd
        def _(pool):
            for s in (m_lo_done, bet_done):
                pool.sem_inc(s, LEAD)

            def split_m(i, s):
                reached(pool, m_hi_done, 2 * i + s + 1)
                nc.gpsimd.tensor_tensor(m_lo[s][:], m_raw[:], m_hi[s][:].bitcast(F32), ALU.subtract).then_inc(m_lo_done, 1)

            def shift(i, s):
                for u in range(2):
                    n = 4 * i + 2 * s + u
                    reached(pool, gam_done, n + 1)
                    pool.wait_ge(stored[u], (2 * i + s + 1) * 16)
                    nc.gpsimd.tensor_tensor(o[u][:], r[u][:], bet[:], ALU.add).then_inc(bet_done, 1)

            for k in range(1, KD, 2):
                reached(pool, w_hi_done, k + 1)
                nc.gpsimd.tensor_tensor(w_lo[:, k, :], w_raw[k % 2][:], w_hi[:, k, :].bitcast(F32), ALU.subtract
                                        ).then_inc(w_lo_done[1], 1)
            pool.wait_ge(par_loaded, 48)
            reached(pool, m_lo_done, 2)
            shift(0, 0)
            split_m(1, 0)
            shift(0, 1)
            with pool.Fori(1, NG // 2 - 1) as i:
                split_m(i, 1)
                shift(i, 0)
                split_m(i + 1, 0)
                shift(i, 1)
            split_m(NG // 2 - 1, 1)
            shift(NG // 2 - 1, 0)
            shift(NG // 2 - 1, 1)

        @block.vector
        def _(dve):
            for s in (scaled, summed, stats_done, mv_done, ve_done, rstd_done, xhat_done, gam_done):
                dve.sem_inc(s, LEAD)
            for k in range(0, KD, 2):
                if k < KD - 2:
                    dve.wait_ge(m0_hi_done, k // 2 + 1)
                else:
                    reached(dve, m_hi_done, 1)
                nc.vector.tensor_tensor(m_lo[0][:, k:k + 2, :], m_raw[:, k:k + 2, :], m_hi[0][:, k:k + 2, :].bitcast(F32),
                                        ALU.subtract).then_inc(m0_lo_done if k < KD - 2 else m_lo_done, 1)
                reached(dve, w_hi_done, k + 1)
                nc.vector.tensor_tensor(w_lo[:, k, :], w_raw[k % 2][:], w_hi[:, k, :].bitcast(F32), ALU.subtract
                                        ).then_inc(w_lo_done[0], 1)
            reached(dve, m_hi_done, 2)
            nc.vector.tensor_tensor(m_lo[1][:], m_raw[:], m_hi[1][:].bitcast(F32), ALU.subtract).then_inc(m_lo_done, 1)
            dve.wait_ge(par_loaded, 48)
            with dve.Fori(0, NG) as i:
                for u in range(2):
                    n = 2 * i + u
                    reached(dve, bet_done, n - 1)
                    for half in range(2):
                        cols = slice(half * HALF, (half + 1) * HALF)
                        reached(dve, acc_done, 2 * n + half + 1)
                        nc.vector.tensor_tensor(r[u][:, cols], acc[2 * u + half][:], gate[:, cols], ALU.mult).then_inc(scaled, 1)
                    dve.wait_ge(x_loaded[u], (i + 2) * 16)
                    for half in range(2):
                        cols = slice(half * HALF, (half + 1) * HALF)
                        reached(dve, scaled, 2 * n + half + 1)
                        nc.vector.scalar_tensor_tensor(r[u][:, cols], xt[u][:, cols], ALPHA, r[u][:, cols],
                                                       ALU.mult, ALU.add).then_inc(summed, 1)
                    for half in range(2):
                        cols = slice(half * HALF, (half + 1) * HALF)
                        reached(dve, summed, 2 * n + half + 1)
                        nc.vector.bn_stats(stats[:, 6 * half:6 * half + 6], r[u][:, cols]).then_inc(stats_done, 1)
                    reached(dve, stats_done, 2 * n + 2)
                    nc.vector.tensor_copy(count[:], stats[:, 0:1])
                    nc.vector.bn_aggr(mv[:], stats[:]).then_inc(mv_done, 1)
                    reached(dve, mv_done, n + 1)
                    nc.vector.tensor_scalar(small[:, 0:1], mv[:, 1:2], LN_EPS, None, ALU.add).then_inc(ve_done, 1)
                    reached(dve, std_done, n + 1)
                    nc.vector.reciprocal(small[:, 2:3], small[:, 1:2]).then_inc(rstd_done, 1)
                    reached(dve, rstd_done, n + 1)
                    nc.vector.tensor_scalar(r[u][:], r[u][:], mv[:, 0:1], small[:, 2:3], ALU.subtract, ALU.mult
                                            ).then_inc(xhat_done, 1)
                    reached(dve, xhat_done, n + 1)
                    nc.vector.tensor_tensor(r[u][:], r[u][:], gam[:], ALU.mult).then_inc(gam_done, 1)


def build(nc, x, c, w_mod, b_mod, w_in, conv_w, hgrn_norm_w, lower_bounds, w_branch, w_out, ln_g, ln_b, out):
    dram = lambda n, s: nc.dram_tensor(n, s, F32).ap()
    values = dram("values", (3, T, W))
    rows = [1, D, IN_COLS, 3 * W, 2 * W]
    scratch = dram("scratch", (sum(rows), T))
    gate, merged, proj, y, proj_lo = (scratch[sum(rows[:n]):sum(rows[:n + 1])] for n in range(len(rows)))
    scr = {
        "gate": gate[:, 0:D],
        "m": merged,
        "proj": proj,
        "y": y.rearrange("(b w) t -> b w t", b=3),
        "proj_lo": proj_lo,
        "i": values[0], "v_hi": values[1], "v_lo": values[2],
    }

    def stage(f, *args):
        with nc.cleanup_on_exit():
            f(nc, lambda name: nc.alloc_semaphore(name=name), *args)

    with nc.sbuf_tensor("ident", [P, P], F32) as ident:
        with nc.sbuf_tensor("hT_hi", [P, KD, T], F32R) as hT_hi, nc.sbuf_tensor("hT_lo", [P, KD, T], F32R) as hT_lo:
            g = {"ident": ident, "hT_hi": hT_hi, "hT_lo": hT_lo}
            with nc.sbuf_tensor("mod", [P, 2 * D], F32) as g["mod"]:
                stage(modulation, g, c, w_mod, b_mod, scr)
                stage(modulated_input_and_values, g, x[0], w_in, scr)
            stage(project, g, w_in, scr, RUNS, "p_")
            stage(hgrn2_and_columns, g, w_in, scr, lower_bounds, hgrn_norm_w)
            stage(attention_and_gates, g, w_in, scr)
        stage(conv_and_merge, scr, conv_w, w_branch)
        stage(project_out, scr, w_out, ln_g, ln_b, x[0], out)


_INS = ["x", "c", "w_mod", "b_mod", "w_in", "conv_w", "hgrn_norm_w", "lower_bounds", "w_branch", "w_out", "ln_g", "ln_b"]


def kernel(**inputs):
    import numpy as np
    import concourse.bacc as bacc
    from concourse.bass_utils import run_bass_kernel_spmd

    nc = bacc.Bacc("TRN2", target_bir_lowering=False, num_devices=1)
    arrays, args = {}, []
    for name in _INS:
        a = np.ascontiguousarray(inputs[name])
        arrays[f"in_{name}"] = a
        args.append(nc.dram_tensor(f"in_{name}", a.shape, mybir.dt.from_np(a.dtype), kind="ExternalInput").ap())
    out = nc.dram_tensor("out_x", (1, T, D), F32, kind="ExternalOutput").ap()
    build(nc, *args, out)
    r = run_bass_kernel_spmd(nc, [arrays], core_ids=[0])
    return r.results[0]["out_x"]
```
